# Optimizing a Trainium2 kernel written in Bass

```python
import math
import jax, jax.numpy as jnp
from jax import lax
import numpy as np

D_MODEL = 1024
BATCH = 1
SEQ = 256
DEPTH = 2

HEAD_DIM = 64
ROPE_THETA = 10000.0
A_Q_HEADS = 8
A_KV_HEADS = 2
A_WINDOW = 128
A_BLOCK = 128
B_Q_HEADS = 8
B_Q_RANK = 256
B_IDX_HEADS = 8
B_IDX_DIM = HEAD_DIM
B_TOPK_MAX = 256
B_QBLOCK = 128
C_HEADS = 16
C_BLOCK = 256
C_TOPK = 3
C_QCHUNK = 16
D_FF = 4 * D_MODEL
N_EVEN = (DEPTH + 1) // 2
N_ODD = DEPTH // 2
DN_ALPHA = (2 * DEPTH) ** 0.25
DN_BETA = (8 * DEPTH) ** -0.25
LN_EPS = 1e-5
RMS_EPS = 1e-6

AB_WIDTHS = (A_Q_HEADS * HEAD_DIM, A_KV_HEADS * HEAD_DIM, A_KV_HEADS * HEAD_DIM,
             B_Q_RANK, HEAD_DIM, HEAD_DIM, B_IDX_DIM, B_IDX_HEADS)
AB_IN_WIDTH = sum(AB_WIDTHS)
AB_MIX_WIDTH = (A_Q_HEADS + B_Q_HEADS) * HEAD_DIM
C_WIDTH = C_HEADS * HEAD_DIM


def _split_widths(t, widths):
    return jnp.split(t, np.cumsum(widths)[:-1].tolist(), axis=-1)

def layer_norm(x, g, b):
    xf = x.astype(jnp.float32)
    mu = jnp.mean(xf, axis=-1, keepdims=True)
    var = jnp.mean(jnp.square(xf - mu), axis=-1, keepdims=True)
    return ((xf - mu) * lax.rsqrt(var + LN_EPS) * g.astype(jnp.float32) + b.astype(jnp.float32)).astype(x.dtype)

def rms_norm(x, g):
    xf = x.astype(jnp.float32)
    ms = jnp.mean(jnp.square(xf), axis=-1, keepdims=True)
    return (xf * lax.rsqrt(ms + RMS_EPS) * g.astype(jnp.float32)).astype(x.dtype)

def rope_tables(positions):
    inv = ROPE_THETA ** (-jnp.arange(0, HEAD_DIM, 2, dtype=jnp.float32) / HEAD_DIM)
    ang = positions.astype(jnp.float32)[..., None] * inv
    ang = jnp.concatenate([ang, ang], axis=-1)
    return jnp.cos(ang)[:, :, None, :], jnp.sin(ang)[:, :, None, :]

def apply_rope(t, cos, sin):
    t1, t2 = jnp.split(t, 2, axis=-1)
    rot = jnp.concatenate([-t2, t1], axis=-1)
    return (t * cos + rot * sin).astype(t.dtype)

def ada_modulation(c, w, b):
    m = jax.nn.silu(c) @ w + b
    shift, scale, gate = jnp.split(m[:, None, :], 3, axis=-1)
    return shift, scale, 1.0 + gate

def swa_sink_attention(q, k, v, sinks):
    Bn, S, HQ, hd = q.shape
    HKV = k.shape[2]
    G = HQ // HKV
    nb = S // A_BLOCK
    qb = q.reshape(Bn, nb, A_BLOCK, HKV, G, hd)

    def band(t):
        tb = t.reshape(Bn, nb, A_BLOCK, HKV, hd)
        prev = jnp.pad(tb[:, :-1], ((0, 0), (1, 0), (0, 0), (0, 0), (0, 0)))
        return jnp.concatenate([prev, tb], axis=2)

    kb, vb = band(k), band(v)
    s = jnp.einsum('bnqkgd,bnskd->bnkgqs', qb, kb, preferred_element_type=jnp.float32) * (hd ** -0.5)
    qpos = jnp.arange(nb)[:, None, None] * A_BLOCK + jnp.arange(A_BLOCK)[None, :, None]
    kpos = jnp.arange(nb)[:, None, None] * A_BLOCK - A_BLOCK + jnp.arange(2 * A_BLOCK)[None, None, :]
    diff = qpos - kpos
    mask = (diff >= 0) & (diff < A_WINDOW) & (kpos >= 0)
    s = jnp.where(mask[None, :, None, None], s, -jnp.inf)
    sink = jnp.broadcast_to(sinks.astype(jnp.float32).reshape(HKV, G)[None, None, :, :, None, None],
                            s.shape[:-1] + (1,))
    p = jax.nn.softmax(jnp.concatenate([s, sink], axis=-1), axis=-1)[..., :-1]
    o = jnp.einsum('bnkgqs,bnskd->bnqkgd', p.astype(vb.dtype), vb)
    return o.reshape(Bn, S, HQ * hd)

def dsa_attention(q, k, v, iq, ik, iw):
    Bn, S, H, hd = q.shape
    n_top = min(B_TOPK_MAX, S // 4)
    nqb = S // B_QBLOCK

    def to_blocks(t):
        return jnp.moveaxis(t.reshape((Bn, nqb, B_QBLOCK) + t.shape[2:]), 1, 0)

    kpos = jnp.arange(S)
    bidx = jnp.arange(Bn)[:, None, None]
    scale = hd ** -0.5

    def one_block(args):
        i, qb, iqb, iwb = args
        tpos = i * B_QBLOCK + jnp.arange(B_QBLOCK)
        raw = jnp.einsum('bqhd,bsd->bhqs', iqb, ik, preferred_element_type=jnp.float32)
        score = jnp.einsum('bhqs,bqh->bqs', jax.nn.relu(raw), iwb.astype(jnp.float32))
        causal = kpos[None, :] <= tpos[:, None]
        score = jnp.where(causal[None], score, -jnp.inf)
        _, idx = lax.top_k(score, n_top)
        valid = idx <= tpos[None, :, None]
        kg = k[bidx, idx]
        vg = v[bidx, idx]
        s = jnp.einsum('bqhd,bqkd->bhqk', qb, kg, preferred_element_type=jnp.float32) * scale
        s = jnp.where(valid[:, None], s, -jnp.inf)
        p = jax.nn.softmax(s, axis=-1)
        o = jnp.einsum('bhqk,bqkd->bqhd', p.astype(vg.dtype), vg)
        return o.reshape(Bn, B_QBLOCK, H * hd)

    out = lax.map(one_block, (jnp.arange(nqb), to_blocks(q), to_blocks(iq), to_blocks(iw)))
    return jnp.moveaxis(out, 0, 1).reshape(Bn, S, H * hd)

def moba_attention(q, k, v):
    Bn, S, H, hd = q.shape
    nb = -(-S // C_BLOCK)
    Sp = nb * C_BLOCK
    pad = ((0, 0), (0, Sp - S), (0, 0), (0, 0))
    kb = jnp.pad(k, pad).reshape(Bn, nb, C_BLOCK, H, hd).transpose(0, 3, 1, 2, 4)
    vb = jnp.pad(v, pad).reshape(Bn, nb, C_BLOCK, H, hd).transpose(0, 3, 1, 2, 4)
    kmean = jnp.mean(kb.astype(jnp.float32), axis=3)
    n_sel = min(C_TOPK, nb - 1)
    nqc = S // C_QCHUNK
    qc = q.reshape(Bn, nqc, C_QCHUNK, H, hd).transpose(1, 0, 3, 2, 4)
    bi = jnp.arange(Bn)[:, None, None, None]
    hi = jnp.arange(H)[None, :, None, None]
    scale = hd ** -0.5

    def one_chunk(args):
        i, qblk = args
        tpos = i * C_QCHUNK + jnp.arange(C_QCHUNK)
        own = tpos // C_BLOCK
        own_idx = jnp.broadcast_to(own[None, None, :, None], (Bn, H, C_QCHUNK, 1))
        own_ok = jnp.ones((Bn, H, C_QCHUNK, 1), dtype=bool)
        if n_sel > 0:
            gate = jnp.einsum('bhqd,bhnd->bhqn', qblk, kmean, preferred_element_type=jnp.float32)
            past = jnp.arange(nb)[None, :] < own[:, None]
            gate = jnp.where(past[None, None], gate, -jnp.inf)
            _, sel = lax.top_k(gate, n_sel)
            sel_ok = sel < own[None, None, :, None]
            blk = jnp.concatenate([sel, own_idx], axis=-1)
            blk_ok = jnp.concatenate([sel_ok, own_ok], axis=-1)
        else:
            blk, blk_ok = own_idx, own_ok
        kg = kb[bi, hi, blk]
        vg = vb[bi, hi, blk]
        s = jnp.einsum('bhqd,bhqnjd->bhqnj', qblk, kg, preferred_element_type=jnp.float32) * scale
        kpos = blk[..., None] * C_BLOCK + jnp.arange(C_BLOCK)
        ok = blk_ok[..., None] & (kpos <= tpos[None, None, :, None, None])
        s = jnp.where(ok, s, -jnp.inf)
        p = jax.nn.softmax(s.reshape(s.shape[:3] + (-1,)), axis=-1).reshape(s.shape)
        o = jnp.einsum('bhqnj,bhqnjd->bqhd', p.astype(vg.dtype), vg)
        return o.reshape(Bn, C_QCHUNK, H * hd)

    out = lax.map(one_chunk, (jnp.arange(nqc), qc))
    return jnp.moveaxis(out, 0, 1).reshape(Bn, S, H * hd)

def mixer_ab(h, cos, sin, w_in, q_norm, w_uq, w_uiq, sinks, w_out):
    Bn, S, _ = h.shape
    aq, ak, av, cq, bk, bv, bik, biw = _split_widths(h @ w_in, AB_WIDTHS)
    aq = apply_rope(aq.reshape(Bn, S, A_Q_HEADS, HEAD_DIM), cos, sin)
    ak = apply_rope(ak.reshape(Bn, S, A_KV_HEADS, HEAD_DIM), cos, sin)
    av = av.reshape(Bn, S, A_KV_HEADS, HEAD_DIM)
    ya = swa_sink_attention(aq, ak, av, sinks)
    cq = rms_norm(cq, q_norm)
    bq = apply_rope((cq @ w_uq).reshape(Bn, S, B_Q_HEADS, HEAD_DIM), cos, sin)
    biq = apply_rope((cq @ w_uiq).reshape(Bn, S, B_IDX_HEADS, B_IDX_DIM), cos, sin)
    bk = apply_rope(bk[:, :, None, :], cos, sin)[:, :, 0]
    bik = apply_rope(bik[:, :, None, :], cos, sin)[:, :, 0]
    iw = biw * (B_IDX_HEADS ** -0.5 * B_IDX_DIM ** -0.5)
    yb = dsa_attention(bq, bk, bv, biq, bik, iw)
    return jnp.concatenate([ya, yb], axis=-1) @ w_out

def mixer_c(h, cos, sin, w_in, w_out):
    Bn, S, _ = h.shape
    q, k, v = jnp.split(h @ w_in, 3, axis=-1)
    q = apply_rope(q.reshape(Bn, S, C_HEADS, HEAD_DIM), cos, sin)
    k = apply_rope(k.reshape(Bn, S, C_HEADS, HEAD_DIM), cos, sin)
    v = v.reshape(Bn, S, C_HEADS, HEAD_DIM)
    return moba_attention(q, k, v) @ w_out

def squared_relu_mlp(h, w1, w2):
    return jnp.square(jax.nn.relu(h @ w1)) @ w2

def first_inputs(seed: int = 0) -> dict:
    key = jax.random.key(seed)
    ks = jax.random.split(key, 20)
    f32 = jnp.float32
    n = lambda k, shp, s: jax.random.normal(k, shp, f32) * s
    D = D_MODEL
    return {
        "x": n(ks[0], (BATCH, SEQ, D), 1.0),
        "c": n(ks[1], (BATCH, D), 1.0),
        "positions": jnp.broadcast_to(jnp.arange(SEQ, dtype=jnp.int32)[None, :], (BATCH, SEQ)),
        "ab_w_in": n(ks[2], (N_EVEN, D, AB_IN_WIDTH), D ** -0.5),
        "ab_q_norm": 1.0 + n(ks[3], (N_EVEN, B_Q_RANK), 0.02),
        "ab_w_uq": n(ks[4], (N_EVEN, B_Q_RANK, B_Q_HEADS * HEAD_DIM), B_Q_RANK ** -0.5),
        "ab_w_uiq": n(ks[5], (N_EVEN, B_Q_RANK, B_IDX_HEADS * B_IDX_DIM), B_Q_RANK ** -0.5),
        "ab_sinks": n(ks[6], (N_EVEN, A_Q_HEADS), 1.0),
        "ab_w_out": n(ks[7], (N_EVEN, AB_MIX_WIDTH, D), AB_MIX_WIDTH ** -0.5 * DN_BETA),
        "c_w_in": n(ks[8], (N_ODD, D, 3 * C_WIDTH), D ** -0.5),
        "c_w_out": n(ks[9], (N_ODD, C_WIDTH, D), C_WIDTH ** -0.5 * DN_BETA),
        "ada_w": n(ks[10], (DEPTH, 2, D, 3 * D), 0.1 * D ** -0.5),
        "ada_b": n(ks[11], (DEPTH, 2, 3 * D), 0.02),
        "ln_g": 1.0 + n(ks[12], (DEPTH, 2, D), 0.02),
        "ln_b": n(ks[13], (DEPTH, 2, D), 0.02),
        "mlp_w1": n(ks[14], (DEPTH, D, D_FF), D ** -0.5),
        "mlp_w2": n(ks[15], (DEPTH, D_FF, D), D_FF ** -0.5 * DN_BETA),
    }

def first_block(x, c, positions, ab_w_in, ab_q_norm, ab_w_uq, ab_w_uiq, ab_sinks, ab_w_out,
              c_w_in, c_w_out, ada_w, ada_b, ln_g, ln_b, mlp_w1, mlp_w2):
    cos, sin = rope_tables(positions)
    for layer in range(DEPTH):
        shift, scale, gate = ada_modulation(c, ada_w[layer, 0], ada_b[layer, 0])
        h = x * (1.0 + scale) + shift
        if layer % 2 == 0:
            e = layer // 2
            y = mixer_ab(h, cos, sin, ab_w_in[e], ab_q_norm[e], ab_w_uq[e], ab_w_uiq[e],
                         ab_sinks[e], ab_w_out[e])
        else:
            o = layer // 2
            y = mixer_c(h, cos, sin, c_w_in[o], c_w_out[o])
        x = layer_norm(DN_ALPHA * x + gate * y, ln_g[layer, 0], ln_b[layer, 0])
        shift, scale, gate = ada_modulation(c, ada_w[layer, 1], ada_b[layer, 1])
        h = x * (1.0 + scale) + shift
        y = squared_relu_mlp(h, mlp_w1[layer], mlp_w2[layer])
        x = layer_norm(DN_ALPHA * x + gate * y, ln_g[layer, 1], ln_b[layer, 1])
    return x


N_A_LAYERS = DEPTH // 2
N_B_LAYERS = DEPTH - N_A_LAYERS
HGRN_EXPAND = 128
HGRN_HEADS = D_MODEL // HGRN_EXPAND
HGRN_DK = HGRN_EXPAND
HGRN_DV = D_MODEL // HGRN_HEADS
HGRN_CHUNK = 64
MLA_HEADS = 16
MLA_NOPE = 128
MLA_ROPE = 64
MLA_V = 128
MLA_Q_LORA = 256
MLA_KV_LORA = 256
QBLOCK = 128
D_FF_2 = 4 * D_MODEL
EPS = 1e-6


def rmsnorm(x, gain):
    xf = x.astype(jnp.float32)
    y = xf * lax.rsqrt(jnp.mean(xf * xf, axis=-1, keepdims=True) + EPS)
    return (y * gain.astype(jnp.float32)).astype(x.dtype)

def rope_tables_2(seq):
    half = MLA_ROPE // 2
    inv_freq = ROPE_THETA ** (-jnp.arange(half, dtype=jnp.float32) / half)
    ang = jnp.arange(seq, dtype=jnp.float32)[:, None] * inv_freq[None, :]
    return jnp.cos(ang), jnp.sin(ang)

def apply_rope_2(x, cos, sin):
    half = MLA_ROPE // 2
    xf = x.astype(jnp.float32)
    x1, x2 = xf[..., :half], xf[..., half:]
    return jnp.concatenate([x1 * cos - x2 * sin, x2 * cos + x1 * sin], axis=-1).astype(x.dtype)

def hgrn_lower_bounds(lb_logits):
    return jnp.cumsum(jax.nn.softmax(lb_logits.astype(jnp.float32), axis=0), axis=0)

def hgrn2_mixer(xn, w_q, w_f, w_i, w_g, g_norm, w_o, lb):
    bsz, seq, _ = xn.shape
    nc = seq // HGRN_CHUNK
    f32 = jnp.float32
    q = jax.nn.silu((xn @ w_q).astype(f32))
    forget = lb + (1.0 - lb) * jax.nn.sigmoid((xn @ w_f).astype(f32))
    log_f = jnp.log(forget)
    k = 1.0 - forget
    v = (xn @ w_i).astype(f32)

    def chunks(t, d):
        return t.reshape(bsz, nc, HGRN_CHUNK, HGRN_HEADS, d).transpose(1, 0, 3, 2, 4)

    causal = jnp.tril(jnp.ones((HGRN_CHUNK, HGRN_CHUNK), dtype=bool))

    def step(state, inp):
        qc, kc, vc, gc = inp
        b = jnp.cumsum(gc, axis=2)
        o_inter = jnp.einsum('bhtd,bhdv->bhtv', qc * jnp.exp(b), state)
        diff = b[:, :, :, None, :] - b[:, :, None, :, :]
        decay = jnp.exp(jnp.where(causal[:, :, None], diff, -jnp.inf))
        scores = jnp.einsum('bhtd,bhsd,bhtsd->bhts', qc, kc, decay)
        o_intra = jnp.einsum('bhts,bhsv->bhtv', scores, vc)
        b_last = b[:, :, -1:, :]
        new_state = jnp.exp(b_last[:, :, 0, :])[..., None] * state + jnp.einsum(
            'bhsd,bhsv->bhdv', kc * jnp.exp(b_last - b), vc)
        return new_state, o_inter + o_intra

    state0 = jnp.zeros((bsz, HGRN_HEADS, HGRN_DK, HGRN_DV), f32)
    _, o = lax.scan(step, state0, (chunks(q, HGRN_DK), chunks(k, HGRN_DK),
                                   chunks(v, HGRN_DV), chunks(log_f, HGRN_DK)))
    o = o.transpose(1, 0, 3, 2, 4).reshape(bsz, seq, HGRN_HEADS, HGRN_DV)
    o = rmsnorm(o, g_norm)
    gate = jax.nn.silu((xn @ w_g).astype(f32)).reshape(bsz, seq, HGRN_HEADS, HGRN_DV)
    o = (o * gate).reshape(bsz, seq, D_MODEL).astype(xn.dtype)
    return o @ w_o

def shared_mla_kv(h, in_norm, w_dkv, kv_norm, w_uk, w_uv, cos, sin):
    bsz, seq, _ = h.shape
    hn = rmsnorm(h, in_norm)
    ckr = hn @ w_dkv
    c_kv = rmsnorm(ckr[..., :MLA_KV_LORA], kv_norm)
    k_rope = apply_rope_2(ckr[..., MLA_KV_LORA:], cos, sin)
    k_nope = (c_kv @ w_uk).reshape(bsz, seq, MLA_HEADS, MLA_NOPE)
    v = (c_kv @ w_uv).reshape(bsz, seq, MLA_HEADS, MLA_V)
    return k_nope, k_rope, v

def mla_mixer(xn, w_dq, q_norm, w_uq, w_o, k_nope, k_rope, v, cos, sin):
    bsz, seq, _ = xn.shape
    nb = seq // QBLOCK
    c_q = rmsnorm(xn @ w_dq, q_norm)
    q = (c_q @ w_uq).reshape(bsz, seq, MLA_HEADS, MLA_NOPE + MLA_ROPE)
    q_nope = q[..., :MLA_NOPE]
    q_rope = apply_rope_2(q[..., MLA_NOPE:], cos[:, None, :], sin[:, None, :])
    qn_b = q_nope.reshape(bsz, nb, QBLOCK, MLA_HEADS, MLA_NOPE).transpose(1, 0, 2, 3, 4)
    qr_b = q_rope.reshape(bsz, nb, QBLOCK, MLA_HEADS, MLA_ROPE).transpose(1, 0, 2, 3, 4)
    starts = jnp.arange(nb, dtype=jnp.int32) * QBLOCK
    key_pos = jnp.arange(seq, dtype=jnp.int32)
    scale = (MLA_NOPE + MLA_ROPE) ** -0.5

    def block(args):
        qn, qr, start = args
        s = jnp.einsum('bqhd,bkhd->bhqk', qn, k_nope) + jnp.einsum('bqhr,bkr->bhqk', qr, k_rope)
        s = s.astype(jnp.float32) * scale
        q_pos = start + jnp.arange(QBLOCK, dtype=jnp.int32)
        s = jnp.where(key_pos[None, :] <= q_pos[:, None], s, -jnp.inf)
        p = jax.nn.softmax(s, axis=-1).astype(v.dtype)
        return jnp.einsum('bhqk,bkhv->bqhv', p, v)

    o = lax.map(block, (qn_b, qr_b, starts))
    o = o.transpose(1, 0, 2, 3, 4).reshape(bsz, seq, MLA_HEADS * MLA_V)
    return o @ w_o

def sq_relu_mlp(xn, w_up, w_down):
    return jnp.square(jax.nn.relu(xn @ w_up)) @ w_down

def second_inputs(seed: int = 0) -> dict:
    key = jax.random.key(seed)
    ks = jax.random.split(key, 24)
    f32 = jnp.float32

    def w(k, shape, fan_in):
        return jax.random.normal(k, shape, f32) * (fan_in ** -0.5)

    def gain(k, shape):
        return 1.0 + 0.02 * jax.random.normal(k, shape, f32)

    D = D_MODEL
    return {
        'x': jax.random.normal(ks[0], (BATCH, SEQ, D), f32),
        'hgrn_norm': gain(ks[1], (N_A_LAYERS, D)),
        'hgrn_w_q': w(ks[2], (N_A_LAYERS, D, D), D),
        'hgrn_w_f': w(ks[3], (N_A_LAYERS, D, D), D),
        'hgrn_w_i': w(ks[4], (N_A_LAYERS, D, D), D),
        'hgrn_w_g': w(ks[5], (N_A_LAYERS, D, D), D),
        'hgrn_g_norm': gain(ks[6], (N_A_LAYERS, HGRN_DV)),
        'hgrn_w_o': w(ks[7], (N_A_LAYERS, D, D), D),
        'hgrn_lb_logits': 0.5 * jax.random.normal(ks[8], (N_A_LAYERS + 1, D), f32),
        'mla_norm': gain(ks[9], (N_B_LAYERS, D)),
        'mla_w_dq': w(ks[10], (N_B_LAYERS, D, MLA_Q_LORA), D),
        'mla_q_norm': gain(ks[11], (N_B_LAYERS, MLA_Q_LORA)),
        'mla_w_uq': w(ks[12], (N_B_LAYERS, MLA_Q_LORA, MLA_HEADS * (MLA_NOPE + MLA_ROPE)), MLA_Q_LORA),
        'mla_w_o': w(ks[13], (N_B_LAYERS, MLA_HEADS * MLA_V, D), MLA_HEADS * MLA_V),
        'kv_in_norm': gain(ks[14], (D,)),
        'kv_w_dkv': w(ks[15], (D, MLA_KV_LORA + MLA_ROPE), D),
        'kv_norm': gain(ks[16], (MLA_KV_LORA,)),
        'kv_w_uk': w(ks[17], (MLA_KV_LORA, MLA_HEADS * MLA_NOPE), MLA_KV_LORA),
        'kv_w_uv': w(ks[18], (MLA_KV_LORA, MLA_HEADS * MLA_V), MLA_KV_LORA),
        'mlp_norm': gain(ks[19], (DEPTH, D)),
        'mlp_w_up': w(ks[20], (DEPTH, D, D_FF_2), D),
        'mlp_w_down': w(ks[21], (DEPTH, D_FF_2, D), D_FF_2),
        'final_norm': gain(ks[22], (D,)),
    }

def second_block(x, hgrn_norm, hgrn_w_q, hgrn_w_f, hgrn_w_i, hgrn_w_g, hgrn_g_norm, hgrn_w_o,
              hgrn_lb_logits, mla_norm, mla_w_dq, mla_q_norm, mla_w_uq, mla_w_o,
              kv_in_norm, kv_w_dkv, kv_norm, kv_w_uk, kv_w_uv,
              mlp_norm, mlp_w_up, mlp_w_down, final_norm):
    seq = x.shape[1]
    cos, sin = rope_tables_2(seq)
    lower_bounds = hgrn_lower_bounds(hgrn_lb_logits)
    h = x
    k_nope = k_rope = v = None
    for l in range(DEPTH):
        if l < N_A_LAYERS:
            h = h + hgrn2_mixer(rmsnorm(h, hgrn_norm[l]), hgrn_w_q[l], hgrn_w_f[l], hgrn_w_i[l],
                                hgrn_w_g[l], hgrn_g_norm[l], hgrn_w_o[l], lower_bounds[l])
        else:
            j = l - N_A_LAYERS
            h = h + mla_mixer(rmsnorm(h, mla_norm[j]), mla_w_dq[j], mla_q_norm[j], mla_w_uq[j],
                              mla_w_o[j], k_nope, k_rope, v, cos, sin)
        h = h + sq_relu_mlp(rmsnorm(h, mlp_norm[l]), mlp_w_up[l], mlp_w_down[l])
        if l == N_A_LAYERS - 1:
            k_nope, k_rope, v = shared_mla_kv(h, kv_in_norm, kv_w_dkv, kv_norm, kv_w_uk, kv_w_uv, cos, sin)
    return rmsnorm(h, final_norm)


def setup_inputs(seed=0):
    out = dict(first_inputs(seed))
    for name, value in second_inputs(seed + 1).items():
        if name != "x":
            out[name + "_2"] = value
    return out


def reference(
    x, c, positions, ab_w_in, ab_q_norm, ab_w_uq, ab_w_uiq, ab_sinks, ab_w_out, c_w_in, c_w_out,
    ada_w, ada_b, ln_g, ln_b, mlp_w1, mlp_w2, hgrn_norm_2, hgrn_w_q_2, hgrn_w_f_2, hgrn_w_i_2,
    hgrn_w_g_2, hgrn_g_norm_2, hgrn_w_o_2, hgrn_lb_logits_2, mla_norm_2, mla_w_dq_2,
    mla_q_norm_2, mla_w_uq_2, mla_w_o_2, kv_in_norm_2, kv_w_dkv_2, kv_norm_2, kv_w_uk_2,
    kv_w_uv_2, mlp_norm_2, mlp_w_up_2, mlp_w_down_2, final_norm_2,
):
    x = first_block(
        x, c, positions, ab_w_in, ab_q_norm, ab_w_uq, ab_w_uiq, ab_sinks, ab_w_out, c_w_in,
        c_w_out, ada_w, ada_b, ln_g, ln_b, mlp_w1, mlp_w2,
    )
    return second_block(
        x, hgrn_norm_2, hgrn_w_q_2, hgrn_w_f_2, hgrn_w_i_2, hgrn_w_g_2, hgrn_g_norm_2,
        hgrn_w_o_2, hgrn_lb_logits_2, mla_norm_2, mla_w_dq_2, mla_q_norm_2, mla_w_uq_2,
        mla_w_o_2, kv_in_norm_2, kv_w_dkv_2, kv_norm_2, kv_w_uk_2, kv_w_uv_2, mlp_norm_2,
        mlp_w_up_2, mlp_w_down_2, final_norm_2,
    )


_drawn_inputs = setup_inputs


def setup_inputs(seed=0):
    import zlib

    import numpy as np

    out = dict(_drawn_inputs(seed))
    spreads = {}
    factors = {'ab_q_norm': 8.0,
     'ab_sinks': 6.295,
     'hgrn_norm_2': 3.351,
     'hgrn_g_norm_2': 4.693,
     'mla_norm_2': 8.0,
     'mla_q_norm_2': 8.0,
     'kv_in_norm_2': 8.0,
     'kv_norm_2': 8.0,
     'final_norm_2': 8.807,
     'mlp_norm_2': 4.258}
    for name, (base, spread) in spreads.items():
        noise = np.random.default_rng([zlib.crc32(name.encode()), seed]).standard_normal(out[name].shape)
        drawn = base * np.exp(spread * noise) if base else spread * noise
        out[name] = __import__('jax').numpy.asarray(drawn.astype(out[name].dtype))
    for name, factor in factors.items():
        out[name] = (out[name] * factor).astype(out[name].dtype)
    return out
```

```python
import concourse.bass as bass
from concourse import mybir
from contextlib import ExitStack

D = 1024
SEQ = 256
P = 128
TT = SEQ // P
KT = D // P
HD = 64
D_FF = 4 * D
HEADS_A, KV_A, HEADS_B, HEADS_C = 8, 2, 8, 16
TOPK = min(256, SEQ // 4)
IDX_HEADS = 8
HG_HEADS = 8
MLA_HEADS, NOPE, ROPE = 16, 128, 64
RANK = 256
ALPHA = (2 * 2) ** 0.25
LN_EPS, RMS_EPS = 1e-5, 1e-6
NEG = -1.0e30
TAKEN = -3.0e38

UNIT = 2048
SLOTS = 4
AB = 0
M0 = AB + 11
CU = M0 + 32
M1 = CU + 16
HG = M1 + 32
M2 = HG + 20
ML = M2 + 32
M3 = ML + 18
UNITS = M3 + 32
PAIRS = D_FF // 256

COL = {}
_at = 0
for _name, _n in (("c", 8), ("ln_g", 32), ("ln_b", 32), ("ab_q", 2), ("hgrn", 8), ("mla", 8), ("mla_q", 2),
                  ("kv_in", 8), ("kv", 2), ("mlp", 16), ("lb", 16)):
    COL[_name] = _at
    _at += _n
NCOLS = _at

LEVELS = 8
N_CONST = 5 + LEVELS
TWO_PI = 6.283185307179586
PI_BELOW = 3.1415925
ROUNDER = 1.5 * 2.0 ** 23


def _parts(x, bits, n):
    import math
    out = []
    for _ in range(n - 1):
        step = 2.0 ** (math.floor(math.log2(abs(x))) - bits + 1)
        out.append(math.floor(x / step) * step)
        x -= out[-1]
    return out + [x]


TWO_PI_PARTS = _parts(TWO_PI, 8, 4)

HTF = 0
ADAW = HTF + 2048
ADAC = ADAW + 3 * D
GATE = ADAC + 3 * D
SCR = GATE + D
ARENA = SCR + 7424


def START_BUF(A, k):
    at = (ADAW, SCR, SCR + 3 * D)[k % 3]
    return A[:, at:at + 3 * D]


def two_block_kernel(nc, stream, ada_w, ada_b, x, x_t, pos, cols, ln_g, ln_b, sinks, g_norm, final_norm,
                     consts, rope_cols, rope_2, out):
    f32, f32r, bf16 = mybir.dt.float32, mybir.dt.float32r, mybir.dt.bfloat16
    ALU = mybir.AluOpType
    ACT = mybir.ActivationFunctionType
    AX = mybir.AxisListType
    ctx = ExitStack()
    with ctx:
        def sb(name, shape, dt=f32):
            return ctx.enter_context(nc.sbuf_tensor(name, shape, dt))

        def sem(name):
            return ctx.enter_context(nc.semaphore(name))

        raw = sb("raw", [P, SLOTS, UNIT])
        w_hi = sb("w_hi", [P, SLOTS, UNIT], f32r)
        w_lo = sb("w_lo", [P, SLOTS, UNIT], f32r)
        X = sb("X", [P, TT, D])
        hT_hi = sb("hT_hi", [P, KT, SEQ], f32r)
        hT_lo = sb("hT_lo", [P, KT, SEQ], f32r)
        R = sb("R", [P, 2, KT, SEQ], f32r)
        A = sb("A", [P, ARENA])
        ident = sb("ident", [P, P])
        perm = sb("perm", [P, P])
        ones = sb("ones", [P, P])
        ident_b = sb("ident_b", [P, P], bf16)
        causal_b = sb("causal_b", [P, P], bf16)
        band_b = sb("band_b", [P, P], bf16)
        level_m = sb("level_m", [P, LEVELS, P], mybir.dt.uint8)
        cosT = sb("cosT", [P, SEQ])
        sinT = sb("sinT", [P, SEQ])
        vec = sb("vec", [P, NCOLS])
        silu_c = sb("silu_c", [P, KT])
        zero8 = sb("zero8", [P, KT])
        sc_c = sb("sc_c", [P, KT])
        bi_c = sb("bi_c", [P, KT])
        tmp_c = sb("tmp_c", [P, 4, KT])
        rc = sb("rc", [P, 2])
        sink_r = sb("sink_r", [P, HEADS_A])
        lb_c = sb("lb_c", [P, 2, KT])
        bn = sb("bn", [P, TT, 2, 6])
        mv = sb("mv", [P, TT, 2])
        ve = sb("ve", [P, 16])
        nw = sb("nw", [P, 4, 16])
        rstd = sb("rstd", [P, 16])
        mx, nb, sm, sk, ri = (sb(x_, [P, 4, 2]) for x_ in ("mx", "nb", "sm", "sk", "ri"))
        B = [ctx.enter_context(nc.psum_tensor(f"bank{i}", [P, 512], f32)) for i in range(8)]

        def arena(at, *shape):
            n = 1
            for s in shape:
                n *= s
            v = A[:, at:at + n]
            if len(shape) == 2:
                v = v.rearrange("p (a b) -> p a b", a=shape[0])
            return v

        def two(v):
            return v.rearrange("p (a b) -> p a b", a=2)

        hTf = arena(HTF, KT, SEQ)
        probs, probsT = arena(HTF, 2, 384), arena(HTF + 768, 2, 384)
        cT_f = arena(HTF + 1024, 2, SEQ)
        ada_k, ada_acc, gate_r = arena(ADAW, 3 * D), arena(ADAC, 3 * D), arena(GATE, D)
        N = arena(SCR, TT, D)
        rows = arena(SCR + 2048, 2, D)
        u_f = arena(SCR + 4096, 2, 512)
        R_hi, R_lo = R[:, 0], R[:, 1]
        u_hi = [R[:, 0, 2 * i:2 * i + 2, :] for i in range(2)]
        u_lo = [R[:, 1, 2 * i:2 * i + 2, :] for i in range(2)]

        AB_QK = SCR
        AB_TOK = SCR + 16 * 256
        AB_CQ = AB_TOK + 512
        AB_TMP = AB_CQ + 512
        AB_SCORE = AB_TMP + 1024
        AB_MASK = AB_SCORE + 384
        C_V, C_QK = SCR, SCR + 2048
        C_TMP = C_QK + 4096
        H_Q, H_K, H_F, H_V, H_G, H_ST = 0, 2048, 4096, 6144, 8192, 10240
        H_S01 = H_ST + 2048
        H_TMP = H_S01 + 1024
        H_GN = H_TMP + 2048
        L_QN, L_KN, L_QR, L_KR, L_V = 2048, 6144, 10240, 12288, 12544
        L_TMP = 0
        L_C = {"ckv": L_QR, "dq": L_QR + 512}
        assert max(L_V + 4096, H_GN + P, C_TMP + 1024, AB_MASK + 224) <= ARENA
        score = A[:, AB_SCORE:AB_SCORE + 384]
        chosen_b = A[:, AB_MASK:AB_MASK + 192].bitcast(bf16)
        m8, iw = arena(AB_MASK + 192, 2, 8), arena(AB_MASK + 208, TT, IDX_HEADS)
        gn_r = A[:, H_GN:H_GN + P]

        def tile_at(base, j):
            return A[:, base + 256 * j:base + 256 * (j + 1)]

        raw_full = [sem(f"raw_full{i}") for i in range(SLOTS)]
        ld_start = [sem(f"ld_start{i}") for i in range(3)]
        (hi_done, lo_done, unit_done, fill_done, fill_read, u_ready, v_step, a_step, y0_done, y_read, var_ready, rstd_raw,
         n_ready, pair_turned, pair_f, pair_ready, x_ready) = map(sem, (
            "hi_done", "lo_done", "unit_done", "fill_done", "fill_read", "u_ready", "v_step", "a_step", "y0_done", "y_read",
            "var_ready", "rstd_raw", "n_ready", "pair_turned", "pair_f", "pair_ready", "x_ready"))
        (ld_const, ld_row, ld_ada, ld_bias, ld_sink, ld_vec, ld_pos, ld_x, ld_xt, ld_gn, ld_rope2, ld_fn) = map(sem, (
            "ld_const", "ld_row", "ld_ada", "ld_bias", "ld_sink", "ld_vec", "ld_pos", "ld_x", "ld_xt", "ld_gn", "ld_rope2",
            "ld_fn"))
        (consts_ready, c_exp, ang_ready, trig_done, ada_used, acc_zero, ada_col, col_ready, gate_ps, gate_read, turn_f,
         turn_ps, roped, s_done, max_done, exp_done, t_done, pt_done, pv_done, o_done) = map(sem, (
            "consts_ready", "c_exp", "ang_ready", "trig_done", "ada_used", "acc_zero", "ada_col", "col_ready", "gate_ps",
            "gate_read", "turn_f", "turn_ps", "roped", "s_done", "max_done", "exp_done", "t_done", "pt_done", "pv_done",
            "o_done"))
        (ix_ps, ix_relu, ix_used, chosen, e_done, silu_done, lb_in, lb_exp, lv_ps, lv_used, s01_done, ho_ps, ho_read, o_ready,
         out_ready, stored) = map(sem, (
            "ix_ps", "ix_relu", "ix_used", "chosen", "e_done", "silu_done", "lb_in", "lb_exp", "lv_ps", "lv_used", "s01_done",
            "ho_ps", "ho_read", "o_ready", "out_ready", "stored"))

        C_T = {"cq_ab": (R_hi[:, 4:6, :], R_lo[:, 4:6, :]), "cq": (hT_hi[:, 4:6, :], hT_lo[:, 4:6, :]),
               "ckv": (hT_hi[:, 6:8, :], hT_lo[:, 6:8, :])}

        def head(n):
            if n < 8:
                kv = n // (HEADS_A // KV_A)
                return dict(qk=[(tile_at(AB_QK, n // 2), tile_at(AB_QK, 4 + kv), 64 * (n % 2), HD)],
                            v=[A[:, AB_TOK + 256 * t + 64 * kv:][:, 0:64] for t in range(TT)], dv=HD, mask="band",
                            scale=HD ** -0.5, sink=n, o=tile_at(AB_QK, n // 2), oc=64 * (n % 2))
            if n < 16:
                h = n - 8
                return dict(qk=[(tile_at(AB_QK, 8 + h // 2), tile_at(AB_QK, 6), 64 * (h % 2), HD)],
                            v=[A[:, AB_TOK + 256 * t + 128:][:, 0:64] for t in range(TT)], dv=HD, mask="chosen",
                            scale=HD ** -0.5, sink=None, o=tile_at(AB_QK, 8 + h // 2), oc=64 * (h % 2))
            if n < 32:
                h = n - 16
                q, k = 4 * (h // 4) + (h % 4) // 2, 4 * (h // 4) + 2 + (h % 4) // 2
                return dict(qk=[(tile_at(C_QK, q), tile_at(C_QK, k), 64 * (h % 2), HD)],
                            v=[A[:, C_V + D * t + 64 * h:][:, 0:64] for t in range(TT)], dv=HD, mask="causal",
                            scale=HD ** -0.5, sink=None, o=tile_at(C_QK, q), oc=64 * (h % 2))
            h = n - 32
            return dict(qk=[(tile_at(L_QN, h), tile_at(L_KN, h), 0, NOPE),
                            (tile_at(L_QR, h // 2), tile_at(L_KR, 0), 64 * (h % 2), ROPE)],
                        v=[A[:, L_V + 2 * D * t + 128 * h:][:, 0:128] for t in range(TT)], dv=128, mask="causal",
                        scale=(NOPE + ROPE) ** -0.5, sink=None, o=tile_at(L_QN, h), oc=0)

        O_TILES = {"ab": [tile_at(AB_QK, j) for j in (0, 1, 2, 3, 8, 9, 10, 11)],
                   "c": [tile_at(C_QK, j) for j in (0, 1, 4, 5, 8, 9, 12, 13)],
                   "hg": [tile_at(H_K, j) for j in range(8)],
                   "la": [tile_at(L_QN, j) for j in range(8)], "lb": [tile_at(L_QN, 8 + j) for j in range(8)]}

        def fills(u, form, src, reader, dsts):
            return [("fill", u, i, len(dsts), form, src, reader, d) for i, d in enumerate(dsts)]

        def ab_steps():
            s = fills(AB, "N", "h", "plain", [two(A[:, AB_CQ:AB_CQ + 512])])
            s += fills(AB + 1, "N", "h", "plain", [two(A[:, AB_TOK:AB_TOK + 512])])
            s += [("norm2", A[:, AB_CQ:AB_CQ + 512]), ("ada", 1, 0)]
            for j in range(4):
                s += fills(AB + 2 + j, "T", "h", "rope", [AB_TMP])
                s += [("ada", 1, j + 1)]
                if j == 0:
                    s += [("turn2", A[:, AB_CQ:AB_CQ + 512], COL["ab_q"], "cq_ab", 0)]
                s += [("rope", AB_TMP, AB_QK + 512 * j, 512)]
            for i, f in enumerate(fills(AB + 6, "T", "cq_ab", "rope", [AB_TMP] * 4)):
                s += [f, ("rope", AB_TMP, AB_QK + 2048 + 512 * i, 512)]
            s += [("ada", 1, 5), ("ada", 1, 6), ("ada", 1, 7)]
            s += [("index", h) for h in range(IDX_HEADS)]
            for n in range(10):
                s += [("head", n, 0, 8)]
                if n < TOPK // 8:
                    s += [("topk", n)]
            s += [("chosen",)] + [("head", n, 8, 16) for n in range(8, 18)]
            s += [("turn", "ab", "hT", None, None)]
            s += [("rows", 0, 0)] + [("down", AB + 7 + j, 2 * j, 8, "hT", j == 0, j == 3) for j in range(4)]
            return s

        def c_steps():
            s = []
            for j in range(4):
                s += fills(CU + j, "N", "h", "plain", [arena(C_V, TT, D)[:, :, 256 * j:256 * j + 256]])
                s += [("ada", 3, j)]
            for j in range(8):
                s += fills(CU + 4 + j, "T", "h", "rope", [C_TMP])
                s += [("rope", C_TMP, C_QK + 512 * j, 512)]
                if j < 4:
                    s += [("ada", 3, 4 + j)]
            s += [("head", n, 16, 32) for n in range(16, 34)]
            s += [("turn", "c", "hT", None, None)]
            s += [("rows", 1, 0)] + [("down", CU + 12 + j, 2 * j, 8, "hT", j == 0, j == 3) for j in range(4)]
            return s

        def hg_steps():
            s = [("hg_start",)]
            for j in range(4):
                s += fills(HG + j, "T", "h", "silu", [A[:, H_Q + 512 * j:H_Q + 512 * (j + 1)]])
            for j in range(4):
                s += fills(HG + 4 + j, "T", "h", "forget", [j])
            for j in range(4):
                s += fills(HG + 8 + j, "N", "h", "plain", [arena(H_V, TT, D)[:, :, 256 * j:256 * j + 256]])
            for j in range(4):
                s += fills(HG + 12 + j, "N", "h", "gate", [arena(H_G, TT, D)[:, :, 256 * j:256 * j + 256]])
            s += [("level", l) for l in range(LEVELS + 1)]
            s += [("hg_out",), ("turn", "hg", "hT", None, None)]
            s += [("down", HG + 16 + j, 2 * j, 8, "hT", j == 0, j == 3) for j in range(4)]
            return s

        def mla_steps():
            s = fills(ML, "N", "h", "plain", [two(A[:, L_C["ckv"]:L_C["ckv"] + 512])])
            s += fills(ML + 1, "Th", "h", "rope", [L_TMP])
            s += fills(ML + 2, "N", "R", "plain", [two(A[:, L_C["dq"]:L_C["dq"] + 512])])
            s += [("norm2", A[:, L_C["ckv"]:L_C["ckv"] + 512]), ("rope", L_TMP, L_KR, 256),
                  ("turn2", A[:, L_C["ckv"]:L_C["ckv"] + 512], COL["kv"], "ckv", ML + 2)]
            s += [("norm2", A[:, L_C["dq"]:L_C["dq"] + 512]),
                  ("turn2", A[:, L_C["dq"]:L_C["dq"] + 512], COL["mla_q"], "cq", ML + 3)]
            for j in range(2):
                s += fills(ML + 3 + j, "T", "ckv", "plain", [A[:, L_KN + 2048 * j + 512 * i:][:, 0:512] for i in range(4)])
            v = arena(L_V, TT, 2 * D)
            for j in range(2):
                s += fills(ML + 5 + j, "W", "ckv", "plain",
                           [v[:, t, 1024 * j + 512 * h:1024 * j + 512 * h + 512] for t in range(TT) for h in range(2)])
            for j in range(2):
                s += fills(ML + 7 + j, "T", "cq", "plain", [A[:, L_QN + 2048 * j + 512 * i:][:, 0:512] for i in range(4)])
            for i, f in enumerate(fills(ML + 9, "T", "cq", "rope", [L_TMP] * 4)):
                s += [f, ("rope", L_TMP, L_QR + 512 * i, 512)]
            s += [("head", n, 32, 48) for n in range(32, 50)]
            s += [("turn", "la", "hT", None, None), ("turn", "lb", "R", None, None)]
            s += [("down", ML + 10 + j, 2 * j, 16, "hT" if j < 4 else "R", j == 0, j == 7) for j in range(8)]
            return s

        own = lambda name, at=0: (vec[:, COL[name] + at:COL[name] + at + KT], zero8)
        mod = (sc_c, bi_c)
        STEPS = [("start",), ("finish", 0), ("gate", 0)] + ab_steps()
        STEPS += [("finish", 1), ("bound", 0, "ln", AB + 10, mod, None), ("gate", 1), ("rows", 0, 1), ("mlp", 0, M0, 2)]
        STEPS += [("finish", 2), ("bound", 1, "ln", M0 + 31, mod, None), ("gate", 2)] + c_steps()
        STEPS += [("finish", 3), ("bound", 2, "ln", CU + 15, mod, None), ("gate", 3), ("rows", 1, 1), ("mlp", 1, M1, None)]
        STEPS += [("bound", 3, "lnrms", M1 + 31, own("hgrn"), None)] + hg_steps()
        STEPS += [("bound", 4, "rms", HG + 19, own("mlp"), None), ("mlp", 2, M2, None)]
        STEPS += [("bound", 5, "rms", M2 + 31, own("kv_in"), own("mla"))] + mla_steps()
        STEPS += [("bound", 6, "rms", ML + 17, own("mlp", 8), None), ("final_row",), ("mlp", 3, M3, None)]
        STEPS += [("bound", 7, "final", M3 + 31, None, None)]

        def T_unit(u0, k):
            return u0 + (2 * k - 1 if k else 0)

        def D_unit(u0, k):
            return u0 + (2 * k + 2 if k < PAIRS - 1 else 2 * PAIRS - 1)

        LOOPS = (PAIRS - 4) // 2

        block = ctx.enter_context(nc.Block())

        @block.sync
        def _(sp):
            sp.dma_start(vec[:, :], cols).then_inc(ld_vec, 16)
            sp.dma_start(rc[:, :], rope_cols).then_inc(ld_pos, 16)
            sp.dma_start(A[:, HTF:HTF + 256].bitcast(mybir.dt.int32), pos.partition_broadcast(P)).then_inc(ld_pos, 16)
            for k in range(KT):
                if k >= 3:
                    sp.wait_ge(ada_used, k - 2)
                sp.dma_start(START_BUF(A, k), ada_w[0, k]).then_inc(ld_start[k % 3], 16)
            sp.dma_start(X[:, :, :], x.rearrange("(t p) d -> p t d", p=P)).then_inc(ld_x, 16)
            sp.wait_ge(trig_done, 2)
            sp.dma_start(hTf, x_t.rearrange("(k p) t -> p k t", p=P)).then_inc(ld_xt, 16)
            sp.wait_ge(ada_used, KT)
            sp.dma_start(A[:, SCR:SCR + N_CONST * P], consts).then_inc(ld_const, 16)

            def load(u, s):
                sp.dma_start(raw[:, s, :], stream[u]).then_inc(raw_full[s], 16)

            for u in range(SLOTS):
                load(u, u)
            with sp.Fori(1, UNITS // SLOTS) as i:
                for s in range(SLOTS):
                    sp.wait_ge(lo_done, SLOTS * i + (s + 1 - SLOTS))
                    load(SLOTS * i + s, s)
            for u in range(UNITS // SLOTS * SLOTS, UNITS):
                sp.wait_ge(lo_done, u + 1 - SLOTS)
                load(u, u % SLOTS)
            for t in range(TT):
                sp.wait_ge(out_ready, t + 1)
                sp.dma_start(out[t * P:(t + 1) * P, :], N[:, t, :]).then_inc(stored, 16)
            sp.wait_ge(stored, 16 * TT)

        @block.gpsimd
        def _(pool):
            def split(u, s):
                pool.wait_ge(hi_done, u + 1)
                pool.tensor_tensor(w_lo[:, s, :], raw[:, s, :], w_hi[:, s, :], ALU.subtract).then_inc(lo_done, 1)

            with pool.Fori(0, UNITS // SLOTS) as i:
                for s in range(SLOTS):
                    split(SLOTS * i + s, s)
            for u in range(UNITS // SLOTS * SLOTS, UNITS):
                split(u, u % SLOTS)

        @block.tensor
        def _(pe):
            n = dict(fill=0, rope=0, turn=0, plain=0, pair=0, c=0, gates=0, y=0, bound=0)
            reads = []

            def bank_free(back):
                if len(reads) >= back:
                    pe.wait_ge(*reads[-back])

            def weights(u):
                pe.wait_ge(lo_done, u + 1)

            def mm3(o, lh, ll, rh, rl, start, stop):
                pe.matmul(o, lh, rh, start=start, stop=False, skip_group_check=True)
                pe.matmul(o, lh, rl, start=False, stop=False, skip_group_check=True)
                return pe.matmul(o, ll, rh, start=False, stop=stop, skip_group_check=True)

            def source(src):
                return {"h": (hT_hi, hT_lo), "R": (R_hi, R_lo), **C_T}[src]

            def fill(u, part, parts, form, src, reader):
                s, kts = u % SLOTS, KT if parts == 1 else 2
                hh, hl = source(src)
                wh = w_hi[:, s, :].rearrange("p (k n) -> p k n", k=kts)
                wl = w_lo[:, s, :].rearrange("p (k n) -> p k n", k=kts)
                bank = B[n["fill"] % 2]
                bank_free(2)
                if part == 0:
                    weights(u)
                pe.wait_ge(pair_f, 2 * n["pair"])
                last = None
                if form == "W":
                    t, h = part // 2, part % 2
                    for k in range(kts):
                        last = mm3(bank[:, :], hh[:, k, P * t:P * t + P], hl[:, k, P * t:P * t + P],
                                   wh[:, k, 512 * h:512 * h + 512], wl[:, k, 512 * h:512 * h + 512], k == 0, k == kts - 1)
                else:
                    for a in range(1 if form == "Th" else 2):
                        o = bank[:, 256 * a:256 * a + 256]
                        for k in range(kts):
                            if form == "N":
                                at, args = P * a, None
                                last = mm3(o, hh[:, k, at:at + P], hl[:, k, at:at + P], wh[:, k, 0:256], wl[:, k, 0:256],
                                           k == 0, k == kts - 1)
                            else:
                                at = 256 * part + P * a
                                last = mm3(o, wh[:, k, at:at + P], wl[:, k, at:at + P], hh[:, k, :], hl[:, k, :],
                                           k == 0, k == kts - 1)
                n["fill"] += 1
                n[reader] = n.get(reader, 0) + 1
                reads.append({"plain": (fill_read, n["plain"]), "rope": (turn_f, n.get("rope", 0))}.get(
                    reader, (e_done, sum(n.get(k, 0) for k in ("silu", "forget", "gate")))))
                last.then_inc(unit_done if part == parts - 1 else fill_done, 1)

            def down(u, s, lh, ll, first, last, y0=None):
                wh = w_hi[:, s, :].rearrange("p (k n) -> p k n", k=2)
                wl = w_lo[:, s, :].rearrange("p (k n) -> p k n", k=2)
                for t in range(TT):
                    for k in range(2):
                        for h in range(2):
                            c = slice(512 * h, 512 * h + 512)
                            m = mm3(B[4 + 2 * t + h][:, :], lh[:, k, P * t:P * t + P], ll[:, k, P * t:P * t + P],
                                    wh[:, k, c], wl[:, k, c], first and k == 0, last and k == 1)
                    if last and t == 0:
                        m.then_inc(y0_done, 1)
                m.then_inc(unit_done, 1)

            def turn(tiles, w, pairs):
                bank_free(2)
                bank_free(1)
                pe.wait_ge(pair_f, 2 * n["pair"])
                if n["turn"]:
                    pe.wait_ge(roped, n["turn"])
                for j in range(pairs):
                    for a in range(2):
                        for t in range(TT):
                            m = pe.transpose(B[j][:, 256 * a + P * t:256 * a + P * t + P], tiles(2 * j + a, t), ident[:, :])
                    n["pair"] += 1
                    m.then_inc(pair_turned, 1)

            def qk(k):
                h, bank = head(k), B[4 + k % 2]
                if k >= 2:
                    pe.wait_ge(exp_done, k - 1)
                for t in range(TT):
                    o = bank[:, 0:128] if t == 0 else bank[:, 128:384]
                    for i, (q, kk, off, w) in enumerate(h["qk"]):
                        pe.matmul(o, q[off:off + w, P * t:P * t + P], kk[off:off + w, 0:P * (t + 1)], start=i == 0,
                                  stop=False, skip_group_check=True)
                    if h["mask"] == "chosen":
                        m = pe.matmul(o, ident_b[:, :], chosen_b[:, 0:128] if t == 0 else chosen_b[:, 128:384],
                                      start=False, stop=True, skip_group_check=True)
                    else:
                        if t == 1 and h["mask"] == "band":
                            pe.matmul(bank[:, 128:256], ident_b[:, :], band_b[:, :], start=False, stop=False,
                                      skip_group_check=True)
                        m = pe.matmul(bank[:, 256 * t:256 * t + P], ident_b[:, :], causal_b[:, :], start=False, stop=True,
                                      skip_group_check=True)
                m.then_inc(s_done, 1)

            def turn_probs(k):
                pe.wait_ge(exp_done, k + 1)
                if k >= 1:
                    pe.wait_ge(pt_done, k)
                for i in range(3):
                    m = pe.transpose(B[6][:, P * i:P * i + P], probs[:, k % 2, P * i:P * i + P], ident[:, :])
                m.then_inc(t_done, 1)

            def pv(k):
                h = head(k)
                pe.wait_ge(pt_done, k + 1)
                if k >= 1:
                    pe.wait_ge(o_done, k)
                dv, pt = h["dv"], probsT[:, k % 2, :]
                pe.matmul(B[7][:, 0:dv], pt[:, 0:P], h["v"][0], start=True, stop=True, skip_group_check=True)
                pe.matmul(B[7][:, dv:2 * dv], pt[:, P:2 * P], h["v"][0], start=True, stop=False, skip_group_check=True)
                pe.matmul(B[7][:, dv:2 * dv], pt[:, 2 * P:3 * P], h["v"][1], start=False, stop=True,
                          skip_group_check=True).then_inc(pv_done, 1)

            def mlp(m, u0):
                f0, p0 = n["fill"], n["plain"]

                def up(k, kp, u, s):
                    if not (isinstance(k, int) and k < 2):
                        pe.wait_ge(fill_read, k + (p0 - 1))
                    pe.wait_ge(lo_done, u + 1)
                    wh = w_hi[:, s, :].rearrange("p (k n) -> p k n", k=KT)
                    wl = w_lo[:, s, :].rearrange("p (k n) -> p k n", k=KT)
                    for a in range(2):
                        for kt in range(KT):
                            if isinstance(k, int) and k == 0 and a == 0 and kt % 2 == 0:
                                pe.wait_ge(pair_ready, n["pair"] - 3 + kt // 2)
                            last = mm3(B[(f0 + kp) % 2][:, 256 * a:256 * a + 256],
                                       wh[:, kt, P * a:P * a + P], wl[:, kt, P * a:P * a + P],
                                       hT_hi[:, kt, :], hT_lo[:, kt, :], kt == 0, kt == KT - 1)
                    last.then_inc(unit_done, 1)

                def dn(k, kp, u, s, first=False, last=False):
                    pe.wait_ge(lo_done, u + 1)
                    pe.wait_ge(u_ready, PAIRS * m + k + 1)
                    down(u, s, u_hi[kp], u_lo[kp], first, last)

                bank_free(2)
                bank_free(1)
                pe.wait_ge(pair_f, 2 * n["pair"])
                up(0, 0, T_unit(u0, 0), T_unit(u0, 0) % SLOTS)
                up(1, 1, T_unit(u0, 1), T_unit(u0, 1) % SLOTS)
                pe.wait_ge(y_read, n["y"])
                pe.wait_ge(gate_read, 2 * n["gates"])
                dn(0, 0, D_unit(u0, 0), D_unit(u0, 0) % SLOTS, first=True)
                with pe.Fori(0, LOOPS) as i:
                    for j in range(2):
                        ut, ud = T_unit(u0, 2 + j), D_unit(u0, 1 + j)
                        up(2 * i + (2 + j), j, 4 * i + ut, ut % SLOTS)
                        dn(2 * i + (1 + j), (1 + j) % 2, 4 * i + ud, ud % SLOTS)
                for k in (PAIRS - 2, PAIRS - 1):
                    up(k, k % 2, T_unit(u0, k), T_unit(u0, k) % SLOTS)
                    dn(k - 1, (k - 1) % 2, D_unit(u0, k - 1), D_unit(u0, k - 1) % SLOTS)
                k = PAIRS - 1
                dn(k, k % 2, D_unit(u0, k), D_unit(u0, k) % SLOTS, last=True)
                n["fill"] += PAIRS
                n["plain"] += PAIRS
                reads.extend((fill_read, n["plain"] - 1 + j) for j in range(2))

            pe.wait_ge(consts_ready, 1)
            for step in STEPS:
                kind, a = step[0], step[1:]
                if kind == "start":
                    n["pair"] = 4
                elif kind == "finish":
                    pe.wait_ge(ada_used, KT * (a[0] + 1))
                    if a[0]:
                        pe.wait_ge(pair_f, 2 * n["pair"])
                    for j in range(2 * KT):
                        m = pe.matmul(B[3][:, j:j + 1], ada_acc[:, P * j:P * j + P], ones[:, 0:1], start=True, stop=True)
                    m.then_inc(ada_col, 1)
                elif kind == "gate":
                    if n["y"]:
                        pe.wait_ge(y_read, n["y"])
                    for h in range(2):
                        pe.matmul(B[4 + h][:, :], ones[:, :], ada_acc[:, 2 * D + 512 * h:2 * D + 512 * h + 512],
                                  start=True, stop=True).then_inc(gate_ps, 1)
                    n["gates"] += 1
                elif kind == "fill":
                    pe.wait_ge(pair_ready, n["pair"])
                    fill(*a[0:6])
                elif kind == "rope":
                    pe.wait_ge(turn_f, n["turn"] + 1)
                    if n["turn"]:
                        pe.wait_ge(roped, n["turn"])
                    pe.wait_ge(pair_f, 2 * n["pair"])
                    w = a[2]
                    pe.matmul(B[2][:, 0:w], perm[:, :], A[:, a[0]:a[0] + w], start=True, stop=True).then_inc(turn_ps, 1)
                    n["turn"] += 1
                elif kind == "turn2":
                    pe.wait_ge(o_ready, n["c"] + 1)
                    n["c"] += 1
                    t2 = two(a[0])
                    turn(lambda f, t: t2[:, t, P * f:P * f + P], None, 1)
                elif kind == "index":
                    h = a[0]
                    if h == 0:
                        pe.wait_ge(roped, n["turn"])
                        pe.wait_ge(gate_read, 2 * n["gates"])
                    if h >= 2:
                        pe.wait_ge(ix_relu, h - 1)
                    q, kk, off = tile_at(AB_QK, 12 + h // 2), tile_at(AB_QK, 7), 64 * (h % 2)
                    for t in range(TT):
                        m = pe.matmul(B[4 + h % 2][:, 128 * t:128 + 256 * t], q[off:off + HD, P * t:P * t + P],
                                      kk[off:off + HD, 0:P * (t + 1)], start=True, stop=True)
                    m.then_inc(ix_ps, 1)
                elif kind == "chosen":
                    pass
                elif kind == "head":
                    k, first, last = a
                    if k == first:
                        pe.wait_ge(roped, n["turn"])
                        bank_free(1)
                        pe.wait_ge(gate_read, 2 * n["gates"])
                        if n["y"]:
                            pe.wait_ge(y_read, n["y"])
                        if k == 0:
                            pe.wait_ge(ix_relu, IDX_HEADS)
                        if k == 8:
                            pe.wait_ge(chosen, 1)
                    if k < last:
                        qk(k)
                    if first <= k - 1 < last:
                        turn_probs(k - 1)
                    if first <= k - 2 < last:
                        pv(k - 2)
                elif kind == "turn":
                    tiles = O_TILES[a[0]]
                    if a[0] == "hg":
                        pe.wait_ge(o_ready, n["c"] + 1)
                        n["c"] += 1
                    else:
                        pe.wait_ge(o_done, {"ab": 16, "c": 32}.get(a[0], 48))
                    turn(lambda f, t: tiles[f][:, P * t:P * t + P], None, 4)
                elif kind == "down":
                    u, k0, _, src, first, last = a
                    weights(u)
                    if first:
                        if n["y"]:
                            pe.wait_ge(y_read, n["y"])
                        pe.wait_ge(gate_read, 2 * n["gates"])
                    pe.wait_ge(pair_ready, n["pair"])
                    hh, hl = source("h" if src == "hT" else "R")
                    k1 = k0 % KT
                    down(u, u % SLOTS, hh[:, k1:k1 + 2], hl[:, k1:k1 + 2], first, last)
                elif kind == "bound":
                    n["y"] += TT
                    if a[1] != "final":
                        pe.wait_ge(n_ready, TT * (n["bound"] + 1))
                        if n["bound"] < 3:
                            pe.wait_ge(col_ready, n["bound"] + 2)
                        n["bound"] += 1
                        for _ in range(2 if a[4] is not None else 1):
                            turn(lambda f, t: N[:, t, P * f:P * f + P], None, 4)
                elif kind == "mlp":
                    mlp(a[0], a[1])
                elif kind == "level":
                    l = a[0]
                    for g in range(2):
                        if l == 0:
                            pe.wait_ge(silu_done, 12)
                            if g == 0 and n["y"]:
                                pe.wait_ge(y_read, n["y"])
                        else:
                            pe.wait_ge(lv_used, 2 * (l - 1) + g + 1)
                        for h in range(4 * g, 4 * g + 4):
                            for t in range(TT):
                                if l == LEVELS and t == 1:
                                    continue
                                i = (h - 4 * g) if l == LEVELS else 2 * (h - 4 * g) + t
                                bank = B[4 + 2 * g + i // 4]
                                tq = 1 if l == LEVELS else t
                                m = pe.matmul(bank[:, P * (i % 4):P * (i % 4) + P], tile_at(H_K, h)[:, P * t:P * t + P],
                                              tile_at(H_Q, h)[:, P * tq:P * tq + P], start=True, stop=True)
                        m.then_inc(lv_ps, 1)
                elif kind == "hg_out":
                    pe.wait_ge(lv_used, 2 * LEVELS)
                    pe.wait_ge(s01_done, 2)
                    pe.wait_ge(fill_read, n["plain"])
                    v = arena(H_V, TT, D)
                    for t in range(TT):
                        for h in range(HG_HEADS):
                            o = B[4 + 2 * t + h // 4][:, P * (h % 4):P * (h % 4) + P]
                            if t == 1:
                                pe.matmul(o, A[:, H_S01 + P * h:H_S01 + P * h + P], v[:, 0, P * h:P * h + P], start=True,
                                          stop=False, skip_group_check=True)
                            m = pe.matmul(o, A[:, H_ST + 256 * h + P * t:H_ST + 256 * h + P * t + P],
                                          v[:, t, P * h:P * h + P], start=t == 0, stop=True, skip_group_check=True)
                        m.then_inc(ho_ps, 1)

        @block.scalar
        def _(act):
            n = dict(step=0, fill=0, rope=0, pair=0, var=0, e=0, x=0, part=0)

            def link(ins):
                n["step"] += 1
                ins.then_inc(a_step, 1)
                act.wait_ge(a_step, n["step"])

            def hi(u, s, k):
                act.wait_ge(raw_full[s], 16 * k)
                if not (isinstance(u, int) and u < SLOTS):
                    act.wait_ge(unit_done, u + (1 - SLOTS))
                act.activation(w_hi[:, s, :], raw[:, s, :], ACT.Copy).then_inc(hi_done, 1)

            def ahead(u, i=0):
                if isinstance(i, int) and u + SLOTS >= UNITS:
                    return
                v = u + SLOTS
                hi(4 * i + v if not isinstance(i, int) else v, v % SLOTS, i + (v // SLOTS + 1))

            def inverse_root(c0, w):
                n["var"] += 1
                act.wait_ge(var_ready, n["var"])
                link(act.activation(nw[:, 0, c0:c0 + w], ve[:, c0:c0 + w], ACT.Ln))
                act.activation(nw[:, 1, c0:c0 + w], nw[:, 0, c0:c0 + w], ACT.Exp, scale=-0.5).then_inc(rstd_raw, 1)

            def turned(pairs, scale, bias, dst):
                act.wait_ge(pair_ready, n["pair"])
                for j in range(pairs):
                    n["pair"] += 1
                    act.wait_ge(pair_turned, n["pair"] - 4)
                    for k in (2 * j, 2 * j + 1):
                        o, i = dst[:, k, :], B[j][:, 256 * (k % 2):256 * (k % 2) + 256]
                        if scale is None:
                            act.activation(o, i, ACT.Copy).then_inc(pair_f, 1)
                        else:
                            act.activation(o, i, ACT.Identity, scale=scale[:, k:k + 1],
                                           bias=bias[:, k:k + 1]).then_inc(pair_f, 1)

            def load_ada(s, k):
                act.wait_ge(ada_used, KT * s + k)
                act.dma_start(ada_k, ada_w[s, k]).then_inc(ld_ada, 16)

            def ada_begin(s):
                act.wait_ge(acc_zero, s + 1)
                act.dma_start(ada_acc[0:1, :], ada_b[s:s + 1, :]).then_inc(ld_bias, 16)
                if s:
                    load_ada(s, 0)

            def mlp(m, u0, s_ada):
                f0 = n["fill"]

                def relu(k, kp, u):
                    act.wait_ge(unit_done, u + 1)
                    if not (isinstance(k, int) and PAIRS * m + k < 2):
                        act.wait_ge(u_ready, k + (PAIRS * m - 1))
                    act.activation(u_f[:, kp, :], B[(f0 + kp) % 2][:, :], ACT.Relu).then_inc(fill_read, 1)

                relu(0, 0, T_unit(u0, 0))
                ahead(T_unit(u0, 0))
                relu(1, 1, T_unit(u0, 1))
                ahead(T_unit(u0, 1))
                ahead(D_unit(u0, 0))
                if s_ada:
                    load_ada(s_ada, 1)
                with act.Fori(0, LOOPS) as i:
                    for j in range(2):
                        relu(2 * i + (2 + j), j, 4 * i + T_unit(u0, 2 + j))
                        ahead(T_unit(u0, 2 + j), i)
                        ahead(D_unit(u0, 1 + j), i)
                    if s_ada:
                        act.wait_ge(ada_used, i + (KT * s_ada + 2))
                        act.dma_start(ada_k, ada_w[s_ada, i + 2]).then_inc(ld_ada, 16)
                for k in (PAIRS - 2, PAIRS - 1):
                    relu(k, k % 2, T_unit(u0, k))
                    ahead(T_unit(u0, k))
                    ahead(D_unit(u0, k - 1))
                ahead(D_unit(u0, PAIRS - 1))
                n["fill"] += PAIRS

            act.dma_start(sink_r[:, :], sinks.partition_broadcast(P)).then_inc(ld_sink, 16)
            ada_begin(0)
            act.wait_ge(ld_sink, 16)
            act.wait_ge(ld_vec, 16)
            act.activation(silu_c[:, :], vec[:, 0:KT], ACT.Exp, scale=-1.0).then_inc(c_exp, 1)
            act.wait_ge(ang_ready, 1)
            act.activation(sinT[:, :], A[:, HTF + 512:HTF + 768], ACT.Sin).then_inc(trig_done, 1)
            act.activation(cosT[:, :], A[:, HTF + 768:HTF + 1024], ACT.Sin).then_inc(trig_done, 1)
            for u in range(SLOTS):
                hi(u, u, 1)
            for step in STEPS:
                kind, a = step[0], step[1:]
                if kind == "finish" and a[0] == 0:
                    act.wait_ge(ld_xt, 16)
                    act.wait_ge(col_ready, 1)
                    for k in range(KT):
                        act.activation(hTf[:, k, :], hTf[:, k, :], ACT.Identity, scale=sc_c[:, k:k + 1],
                                       bias=bi_c[:, k:k + 1]).then_inc(pair_f, 1)
                    n["pair"] = 4
                elif kind == "gate":
                    s = a[0]
                    for h in range(2):
                        act.wait_ge(gate_ps, 2 * s + h + 1)
                        act.activation(gate_r[:, 512 * h:512 * h + 512], B[4 + h][:, :], ACT.Identity,
                                       bias=ones[:, 0:1]).then_inc(gate_read, 1)
                    if s < 3:
                        ada_begin(s + 1)
                elif kind == "fill":
                    u, part, parts, form, src, reader, dst = a
                    if part == parts - 1:
                        act.wait_ge(unit_done, u + 1)
                    else:
                        n["part"] += 1
                        act.wait_ge(fill_done, n["part"])
                    bank = B[n["fill"] % 2]
                    act.wait_ge(x_ready, n["x"]) if n["x"] else None
                    if reader == "plain":
                        if len(dst.shape) == 3:
                            act.activation(dst, two(bank[:, :]), ACT.Copy).then_inc(fill_read, 1)
                        else:
                            act.activation(dst, bank[:, :], ACT.Copy).then_inc(fill_read, 1)
                    elif reader == "rope":
                        w = 256 if form == "Th" else 512
                        if n["rope"]:
                            act.wait_ge(roped, n["rope"])
                        if u == ML + 1:
                            act.wait_ge(pair_ready, n["pair"])
                        act.activation(A[:, dst:dst + w], bank[:, 0:w], ACT.Copy).then_inc(turn_f, 1)
                        n["rope"] += 1
                    else:
                        e = A[:, H_TMP + 512 * (n["e"] % 2):][:, 0:512]
                        if n["e"] >= 2:
                            act.wait_ge(silu_done, n["e"] - 1)
                        if reader == "silu":
                            link(act.activation(dst, bank[:, :], ACT.Copy))
                            act.activation(e, bank[:, :], ACT.Exp, scale=-1.0).then_inc(e_done, 1)
                        elif reader == "gate":
                            link(act.activation(dst, two(bank[:, :]), ACT.Copy))
                            act.activation(e, bank[:, :], ACT.Exp, scale=-1.0).then_inc(e_done, 1)
                        else:
                            act.activation(e, bank[:, :], ACT.Exp, scale=-1.0).then_inc(e_done, 1)
                        n["e"] += 1
                    n["fill"] += 1
                    if part == parts - 1:
                        ahead(u)
                elif kind == "norm2":
                    inverse_root(0, 2)
                elif kind == "turn2":
                    turned(1, vec[:, a[1]:a[1] + 2], zero8, cT_f)
                elif kind == "ada" and a[1] < KT - 1:
                    load_ada(a[0], a[1] + 1)
                elif kind == "index":
                    h = a[0]
                    act.wait_ge(ix_ps, h + 1)
                    if h == 0:
                        act.wait_ge(roped, n["rope"])
                    if h >= 2:
                        act.wait_ge(ix_used, h - 1)
                    act.activation(A[:, AB_TMP + 384 * (h % 2):][:, 0:384], B[4 + h % 2][:, 0:384],
                                   ACT.Relu).then_inc(ix_relu, 1)
                elif kind == "head":
                    k, first, last = a
                    if k < last:
                        act.wait_ge(max_done, k + 1)
                        if k == first:
                            act.wait_ge(pair_ready, n["pair"])
                        if k >= 2:
                            act.wait_ge(t_done, k - 1)
                        h, pb, bank = head(k), probs[:, k % 2, :], B[4 + k % 2]
                        act.activation(pb[:, 0:128], bank[:, 0:128], ACT.Exp, bias=nb[:, k % 4, 0:1], scale=h["scale"],
                                       accum_out=sm[:, k % 4, 0:1])
                        if h["sink"] is not None:
                            act.activation(sk[:, k % 4, :], nb[:, k % 4, :], ACT.Exp,
                                           bias=sink_r[:, h["sink"]:h["sink"] + 1])
                        act.activation(pb[:, 128:384], bank[:, 128:384], ACT.Exp, bias=nb[:, k % 4, 1:2],
                                       scale=h["scale"], accum_out=sm[:, k % 4, 1:2]).then_inc(exp_done, 1)
                    if first <= k - 1 < last:
                        act.wait_ge(t_done, k)
                        if k - 1 >= 2:
                            act.wait_ge(pv_done, k - 2)
                        act.activation(probsT[:, (k - 1) % 2, :], B[6][:, 0:384], ACT.Copy).then_inc(pt_done, 1)
                elif kind == "turn":
                    turned(4, None, None, hTf)
                elif kind == "rows":
                    act.wait_ge(pair_turned, n["pair"] - 4)
                    if n["x"]:
                        act.wait_ge(x_ready, n["x"])
                    layer, j = a
                    act.dma_start(rows[:, 0, :], ln_g[layer, j].partition_broadcast(P)).then_inc(ld_row, 16)
                    act.dma_start(rows[:, 1, :], ln_b[layer, j].partition_broadcast(P)).then_inc(ld_row, 16)
                elif kind == "final_row":
                    act.wait_ge(pair_turned, n["pair"] - 4)
                    act.dma_start(rows[:, 0, :], final_norm.partition_broadcast(P)).then_inc(ld_fn, 16)
                elif kind == "down":
                    ahead(a[0])
                elif kind == "bound":
                    for t in range(TT):
                        inverse_root(t, 1)
                    if a[1] == "lnrms":
                        for t in range(TT):
                            inverse_root(t, 1)
                    if a[1] != "final":
                        turned(4, a[3][0], a[3][1], hTf)
                    if a[1] != "final" and a[4] is not None:
                        turned(4, a[4][0], a[4][1], hTf)
                    if a[0] < 4:
                        n["x"] += 1
                elif kind == "mlp":
                    mlp(a[0], a[1], a[2])
                elif kind == "hg_start":
                    act.wait_ge(pair_ready, n["pair"])
                    act.dma_start(gn_r, g_norm.partition_broadcast(P)).then_inc(ld_gn, 16)
                    act.dma_start(cosT[:, :], rope_2[:, 0, :]).then_inc(ld_rope2, 16)
                    act.dma_start(sinT[:, :], rope_2[:, 1, :]).then_inc(ld_rope2, 16)
                    act.wait_ge(lb_in, 1)
                    act.activation(tmp_c[:, 2, :], tmp_c[:, 0, :], ACT.Exp)
                    act.activation(tmp_c[:, 3, :], tmp_c[:, 1, :], ACT.Exp).then_inc(lb_exp, 1)
                elif kind == "level" and a[0] == LEVELS:
                    for g in range(2):
                        act.wait_ge(lv_ps, 2 * LEVELS + g + 1)
                        act.activation(A[:, H_S01 + 512 * g:H_S01 + 512 * g + 512], B[4 + 2 * g][:, :],
                                       ACT.Copy).then_inc(s01_done, 1)
                elif kind == "hg_out":
                    o = A[:, H_K:H_K + 2048].rearrange("p (h t v) -> p h t v", h=HG_HEADS, t=TT)
                    for t in range(TT):
                        act.wait_ge(ho_ps, t + 1)
                        for h in range(2):
                            act.activation(o[:, 4 * h:4 * h + 4, t, :], B[4 + 2 * t + h][:, :].rearrange(
                                "p (h v) -> p h v", h=4), ACT.Copy).then_inc(ho_read, 1)
                    inverse_root(0, 16)

        @block.vector
        def _(v):
            n = dict(step=0, plain=0, rope=0, pair=0, raw=0, e=0, row=0, n=0)

            def link(ins):
                n["step"] += 1
                ins.then_inc(v_step, 1)
                v.wait_ge(v_step, n["step"])

            def newton(c0, w):
                n["raw"] += 1
                v.wait_ge(rstd_raw, n["raw"])
                c = slice(c0, c0 + w)
                link(v.tensor_tensor(nw[:, 2, c], nw[:, 1, c], nw[:, 1, c], ALU.mult))
                link(v.tensor_tensor(nw[:, 3, c], nw[:, 2, c], ve[:, c], ALU.mult))
                link(v.tensor_scalar(nw[:, 3, c], nw[:, 3, c], -0.5, 1.5, ALU.mult, ALU.add))
                link(v.tensor_tensor(rstd[:, c], nw[:, 3, c], nw[:, 1, c], ALU.mult))

            def stats(t, rms, src, width):
                parts = width // 512 if width > 512 else 1
                w = width // parts
                for h in range(parts):
                    link(v.bn_stats(bn[:, t, h, :], src[:, w * h:w * h + w]))
                link(v.bn_aggr(mv[:, t, :], bn[:, t, 0:parts, :]))
                if rms:
                    link(v.scalar_tensor_tensor(out=ve[:, t:t + 1], in0=mv[:, t, 0:1], scalar=mv[:, t, 0:1],
                                                in1=mv[:, t, 1:2], op0=ALU.mult, op1=ALU.add))
                    return v.tensor_scalar(ve[:, t:t + 1], ve[:, t:t + 1], RMS_EPS, None, ALU.add)
                return v.tensor_scalar(ve[:, t:t + 1], mv[:, t, 1:2], LN_EPS, None, ALU.add)

            def split(pairs, f, hi, lo):
                for j in range(pairs):
                    n["pair"] += 1
                    v.wait_ge(pair_f, 2 * n["pair"])
                    c = slice(2 * j, 2 * j + 2)
                    link(v.tensor_copy(hi[:, c, :], f[:, c, :]))
                    v.tensor_tensor(lo[:, c, :], f[:, c, :], hi[:, c, :], ALU.subtract).then_inc(pair_ready, 1)

            def ada(s, k):
                if s:
                    v.wait_ge(ld_ada, 16 * (KT * (s - 1) + k + 1))
                    w = ada_k
                else:
                    v.wait_ge(ld_start[k % 3], 16 * (k // 3 + 1))
                    w = START_BUF(A, k)
                if k == 0:
                    v.wait_ge(ld_bias, 16 * (s + 1))
                v.scalar_tensor_tensor(out=ada_acc, in0=w, scalar=silu_c[:, k:k + 1], in1=ada_acc, op0=ALU.mult,
                                       op1=ALU.add).then_inc(ada_used, 1)
                v.wait_ge(ada_used, KT * s + k + 1)

            def mlp(m, u0, s_ada):
                p0, st = n["plain"], n["step"]

                def square(k, kp, step, u_free):
                    v.wait_ge(fill_read, k + (p0 + 1))
                    v.tensor_tensor(u_f[:, kp, :], u_f[:, kp, :], u_f[:, kp, :], ALU.mult).then_inc(v_step, 1)
                    v.wait_ge(v_step, step + 1)
                    if u_free is not None:
                        v.wait_ge(unit_done, u_free + 1)
                    v.tensor_copy(u_hi[kp], two(u_f[:, kp, :])).then_inc(v_step, 1)
                    v.wait_ge(v_step, step + 2)
                    v.tensor_tensor(u_lo[kp], two(u_f[:, kp, :]), u_hi[kp], ALU.subtract).then_inc(u_ready, 1)

                square(0, 0, st, None)
                square(1, 1, st + 2, None)
                if s_ada:
                    ada(s_ada, 0)
                with v.Fori(0, LOOPS) as i:
                    for j in range(2):
                        square(2 * i + (2 + j), j, 4 * i + (st + 4 + 2 * j), 4 * i + D_unit(u0, j))
                    if s_ada:
                        k = KT * (s_ada - 1) + 2
                        v.wait_ge(ld_ada, 16 * i + 16 * k)
                        v.scalar_tensor_tensor(out=ada_acc, in0=ada_k, scalar=silu_c[:, bass.ds(i + 1, 1)], in1=ada_acc,
                                               op0=ALU.mult, op1=ALU.add).then_inc(ada_used, 1)
                        v.wait_ge(ada_used, i + (KT * s_ada + 2))
                st += 4 + 4 * LOOPS
                for k in (PAIRS - 2, PAIRS - 1):
                    square(k, k % 2, st, D_unit(u0, k - 2))
                    st += 2
                if s_ada:
                    ada(s_ada, KT - 1)
                n["step"], n["plain"] = st, p0 + PAIRS

            def zero_acc():
                v.memset(ada_acc, 0.0).then_inc(acc_zero, 1)

            zero_acc()
            v.memset(zero8[:, :], 0.0)
            link(v.memset(ones[:, :], 1.0))
            v.wait_ge(ld_pos, 32)
            p_f, ang, cs = arena(HTF + 256, SEQ), arena(HTF + 1024, SEQ), arena(HTF + 1280, SEQ)
            link(v.tensor_copy(p_f, A[:, HTF:HTF + 256].bitcast(mybir.dt.int32)))
            link(v.tensor_scalar(ang, p_f, rc[:, 0:1], None, ALU.mult))
            for at, quarter in ((512, 0.0), (768, 0.25)):
                r = A[:, HTF + at:HTF + at + SEQ]
                link(v.tensor_scalar(cs, ang, 1.0 / TWO_PI, quarter, ALU.mult, ALU.add))
                link(v.tensor_scalar(cs, cs, ROUNDER, None, ALU.add))
                link(v.tensor_scalar(cs, cs, ROUNDER, None, ALU.subtract))
                link(v.tensor_copy(r, ang))
                for part in TWO_PI_PARTS:
                    link(v.scalar_tensor_tensor(out=r, in0=cs, scalar=-part, in1=r, op0=ALU.mult, op1=ALU.add))
                if quarter:
                    link(v.tensor_scalar(r, r, TWO_PI / 4, None, ALU.add))
                link(v.tensor_scalar(r, r, PI_BELOW, -PI_BELOW, ALU.min, ALU.max))
            r = A[:, HTF + 512:HTF + 768]
            v.tensor_scalar(r, r, rc[:, 1:2], None, ALU.mult).then_inc(ang_ready, 1)
            v.wait_ge(c_exp, 1)
            link(v.tensor_scalar(tmp_c[:, 0, :], silu_c[:, :], 1.0, None, ALU.add))
            link(v.reciprocal(tmp_c[:, 1, :], tmp_c[:, 0, :]))
            link(v.tensor_tensor(silu_c[:, :], tmp_c[:, 1, :], vec[:, 0:KT], ALU.mult))
            for k in range(KT):
                ada(0, k)
            v.wait_ge(ld_const, 16)
            cst = arena(SCR, N_CONST, P)
            for i, dst in enumerate((ident, perm, ident_b, causal_b, band_b)):
                v.tensor_copy(dst[:, :], cst[:, i, :])
            v.tensor_copy(level_m[:, :, :], cst[:, 5:5 + LEVELS, :]).then_inc(consts_ready, 1)

            for step in STEPS:
                kind, a = step[0], step[1:]
                if kind == "finish":
                    s = a[0]
                    v.wait_ge(ada_col, s + 1)
                    shift, sc1 = B[3][:, 0:KT], B[3][:, KT:2 * KT]
                    if s == 0:
                        link(v.tensor_scalar(sc_c[:, :], sc1, 1.0, None, ALU.add))
                        v.tensor_copy(bi_c[:, :], shift).then_inc(col_ready, 1)
                    else:
                        g = vec[:, COL["ln_g"] + KT * (s - 1):COL["ln_g"] + KT * s]
                        b = vec[:, COL["ln_b"] + KT * (s - 1):COL["ln_b"] + KT * s]
                        link(v.tensor_scalar(tmp_c[:, 0, :], sc1, 1.0, None, ALU.add))
                        link(v.tensor_tensor(sc_c[:, :], tmp_c[:, 0, :], g, ALU.mult))
                        link(v.tensor_tensor(tmp_c[:, 1, :], tmp_c[:, 0, :], b, ALU.mult))
                        v.tensor_tensor(bi_c[:, :], tmp_c[:, 1, :], shift, ALU.add).then_inc(col_ready, 1)
                    if s == 0:
                        v.wait_ge(consts_ready, 1)
                        split(4, hTf, hT_hi, hT_lo)
                elif kind == "gate":
                    v.wait_ge(gate_ps, 2 * a[0] + 2)
                    if a[0] < 3:
                        zero_acc()
                elif kind == "fill":
                    u, part, parts, form, src, reader, dst = a
                    n["plain"] += reader == "plain"
                    if reader in ("silu", "forget", "gate"):
                        i = n["e"]
                        e = A[:, H_TMP + 512 * (i % 2):][:, 0:512]
                        n["e"] += 1
                        v.wait_ge(e_done, n["e"])
                        link(v.tensor_scalar(e, e, 1.0, None, ALU.add))
                        link(v.reciprocal(e, e))
                        if reader == "silu":
                            v.tensor_tensor(dst, dst, e, ALU.mult).then_inc(silu_done, 1)
                        elif reader == "gate":
                            link(v.tensor_tensor(dst, dst, two(e), ALU.mult))
                            if i == 8:
                                v.wait_ge(ld_gn, 16)
                            g4 = dst.rearrange("p t (h v) -> p t h v", v=P)
                            gb = gn_r.unsqueeze(1).unsqueeze(1).to_broadcast([P, TT, 2, P])
                            v.tensor_tensor(g4, g4, gb, ALU.mult).then_inc(silu_done, 1)
                        else:
                            f, k = A[:, H_F + 512 * dst:][:, 0:512], A[:, H_K + 512 * dst:][:, 0:512]
                            for q in range(2):
                                c, m = slice(256 * q, 256 * q + 256), 2 * dst + q
                                link(v.tensor_scalar(f[:, c], e[:, c], lb_c[:, 1, m:m + 1], lb_c[:, 0, m:m + 1],
                                                     ALU.mult, ALU.add))
                            v.tensor_scalar(k, f, -1.0, 1.0, ALU.mult, ALU.add).then_inc(silu_done, 1)
                elif kind == "rope":
                    tmp, dst, w = a
                    r = n["rope"]
                    n["rope"] += 1
                    v.wait_ge(turn_f, r + 1)
                    if w == 256:
                        v.wait_ge(ld_rope2, 32)
                    def shape(x_):
                        return two(x_) if w == 512 else x_
                    cos, sin = ((cosT[:, :].unsqueeze(1).to_broadcast([P, 2, SEQ]),
                                 sinT[:, :].unsqueeze(1).to_broadcast([P, 2, SEQ])) if w == 512 else
                                (cosT[:, :], sinT[:, :]))
                    d, f, tb = A[:, dst:dst + w], A[:, tmp:tmp + w], A[:, tmp + 512:tmp + 512 + w]
                    link(v.tensor_tensor(shape(d), shape(f), cos, ALU.mult))
                    v.wait_ge(turn_ps, r + 1)
                    link(v.tensor_tensor(shape(tb), shape(B[2][:, 0:w]), sin, ALU.mult))
                    v.tensor_tensor(d, d, tb, ALU.add).then_inc(roped, 1)
                elif kind == "ada":
                    ada(a[0], a[1])
                elif kind == "norm2":
                    c = two(a[0])
                    v.wait_ge(fill_read, n["plain"])
                    for t in range(TT):
                        ins = stats(t, True, c[:, t, :], RANK)
                        if t == 0:
                            link(ins)
                    ins.then_inc(var_ready, 1)
                    newton(0, 2)
                    link(v.tensor_scalar(c[:, 0, :], c[:, 0, :], rstd[:, 0:1], None, ALU.mult))
                    v.tensor_scalar(c[:, 1, :], c[:, 1, :], rstd[:, 1:2], None, ALU.mult).then_inc(o_ready, 1)
                elif kind == "turn2":
                    if a[3]:
                        v.wait_ge(unit_done, a[3])
                    split(1, cT_f, *C_T[a[2]])
                elif kind == "index":
                    h = a[0]
                    v.wait_ge(ix_relu, h + 1)
                    if h == 0:
                        for t in range(TT):
                            link(v.tensor_scalar(iw[:, t, :], A[:, AB_TOK + 256 * t + 192:][:, 0:IDX_HEADS],
                                                 IDX_HEADS ** -0.5 * HD ** -0.5, None, ALU.mult))
                    for t in range(TT):
                        c = slice(128 * t, 128 + 256 * t)
                        r = A[:, AB_TMP + 384 * (h % 2):][:, 0:384][:, c]
                        if h == 0:
                            ins = v.tensor_scalar(score[:, c], r, iw[:, t, h:h + 1], None, ALU.mult)
                        else:
                            ins = v.scalar_tensor_tensor(out=score[:, c], in0=r, scalar=iw[:, t, h:h + 1],
                                                         in1=score[:, c], op0=ALU.mult, op1=ALU.add)
                        if t == 0:
                            link(ins)
                    ins.then_inc(ix_used, 1)
                    v.wait_ge(ix_used, h + 1)
                    if h == IDX_HEADS - 1:
                        for t in range(TT):
                            c = slice(256 * t, 256 * t + P)
                            link(v.tensor_tensor(score[:, c], score[:, c], causal_b[:, :], ALU.add))
                elif kind == "topk":
                    for t in range(TT):
                        c = slice(128 * t, 128 + 256 * t)
                        link(v.max(m8[:, t, :], score[:, c]))
                        link(v.match_replace(score[:, c], m8[:, t, :], score[:, c], TAKEN))
                elif kind == "chosen":
                    link(v.tensor_scalar(chosen_b[:, :], score, TAKEN / 2, NEG, ALU.is_gt, ALU.mult))
                    for t in range(TT):
                        c = slice(256 * t, 256 * t + P)
                        ins = v.tensor_tensor(chosen_b[:, c], chosen_b[:, c], causal_b[:, :], ALU.min)
                        if t == 0:
                            link(ins)
                    ins.then_inc(chosen, 1)
                elif kind == "head":
                    k, first, last = a
                    if k < last:
                        v.wait_ge(s_done, k + 1)
                        h, bank = head(k), B[4 + k % 2]
                        v.reduce_max(mx[:, k % 4, 0:1], bank[:, 0:128], AX.X)
                        link(v.reduce_max(mx[:, k % 4, 1:2], bank[:, 128:384], AX.X))
                        if h["sink"] is not None:
                            link(v.tensor_scalar(mx[:, k % 4, :], mx[:, k % 4, :], h["scale"], None, ALU.mult))
                            link(v.tensor_scalar(mx[:, k % 4, :], mx[:, k % 4, :], sink_r[:, k:k + 1], None, ALU.max))
                            v.tensor_scalar(nb[:, k % 4, :], mx[:, k % 4, :], -1.0, None,
                                            ALU.mult).then_inc(max_done, 1)
                        else:
                            v.tensor_scalar(nb[:, k % 4, :], mx[:, k % 4, :], -h["scale"], None,
                                            ALU.mult).then_inc(max_done, 1)
                    if first <= k - 2 < last:
                        j = k - 2
                        h, q = head(j), j % 4
                        v.wait_ge(pv_done, j + 1)
                        if h["sink"] is not None:
                            link(v.tensor_tensor(sm[:, q, :], sm[:, q, :], sk[:, q, :], ALU.add))
                        link(v.reciprocal(ri[:, q, :], sm[:, q, :]))
                        dv, oc = h["dv"], h["oc"]
                        v.tensor_scalar(h["o"][:, oc:oc + dv], B[7][:, 0:dv], ri[:, q, 0:1], None, ALU.mult)
                        v.tensor_scalar(h["o"][:, P + oc:P + oc + dv], B[7][:, dv:2 * dv], ri[:, q, 1:2], None,
                                        ALU.mult).then_inc(o_done, 1)
                elif kind == "turn":
                    hi_, lo_ = (hT_hi, hT_lo) if a[1] == "hT" else (R_hi, R_lo)
                    split(4, hTf, hi_, lo_)
                elif kind == "bound":
                    b, what, last_unit, _, second = a
                    if b == 0:
                        v.wait_ge(ld_x, 16)
                    for t in range(TT):
                        if t == 0:
                            v.wait_ge(y0_done, b + 1)
                        else:
                            v.wait_ge(unit_done, last_unit + 1)
                        y = [B[4 + 2 * t + h] for h in range(2)]
                        if b < 4:
                            v.tensor_tensor(N[:, t, 0:512], y[0][:, :], gate_r[:, 0:512], ALU.mult)
                            ins = v.tensor_tensor(N[:, t, 512:1024], y[1][:, :], gate_r[:, 512:1024], ALU.mult)
                            ins.then_inc(y_read, 1)
                            v.wait_ge(y_read, TT * b + t + 1)
                            link(v.scalar_tensor_tensor(out=X[:, t, :], in0=X[:, t, :], scalar=ALPHA, in1=N[:, t, :],
                                                        op0=ALU.mult, op1=ALU.add))
                        else:
                            v.tensor_tensor(X[:, t, 0:512], y[0][:, :], X[:, t, 0:512], ALU.add)
                            ins = v.tensor_tensor(X[:, t, 512:1024], y[1][:, :], X[:, t, 512:1024], ALU.add)
                            ins.then_inc(y_read, 1)
                            v.wait_ge(y_read, TT * b + t + 1)
                        stats(t, b >= 4, X[:, t, :], D).then_inc(var_ready, 1)
                    if what == "final":
                        v.wait_ge(ld_fn, 16)
                    for t in range(TT):
                        newton(t, 1)
                        if b < 4:
                            ins = v.tensor_scalar(N[:, t, :], X[:, t, :], mv[:, t, 0:1], rstd[:, t:t + 1], ALU.subtract,
                                                  ALU.mult)
                        else:
                            ins = v.tensor_scalar(N[:, t, :], X[:, t, :], rstd[:, t:t + 1], None, ALU.mult)
                        if what in ("ln", "rms"):
                            ins.then_inc(n_ready, 1)
                            n["n"] += 1
                        else:
                            link(ins)
                        if what == "final":
                            v.tensor_tensor(N[:, t, :], N[:, t, :], rows[:, 0, :], ALU.mult).then_inc(out_ready, 1)

                    def affine():
                        n["row"] += 1
                        v.wait_ge(ld_row, 32 * n["row"])
                        v.wait_ge(n_ready, n["n"]) if n["n"] else None
                        for t in range(TT):
                            link(v.tensor_tensor(X[:, t, :], N[:, t, :], rows[:, 0, :], ALU.mult))
                            ins = v.tensor_tensor(X[:, t, :], X[:, t, :], rows[:, 1, :], ALU.add)
                            if t == 0:
                                link(ins)
                        ins.then_inc(x_ready, 1)
                        v.wait_ge(x_ready, n["row"])

                    if what == "lnrms":
                        affine()
                        for t in range(TT):
                            stats(t, True, X[:, t, :], D).then_inc(var_ready, 1)
                        for t in range(TT):
                            newton(t, 1)
                            v.tensor_scalar(N[:, t, :], X[:, t, :], rstd[:, t:t + 1], None, ALU.mult).then_inc(n_ready, 1)
                            n["n"] += 1
                    if what != "final":
                        split(4, hTf, hT_hi, hT_lo)
                        if second is not None:
                            split(4, hTf, R_hi, R_lo)
                    if what == "ln":
                        affine()
                elif kind == "mlp":
                    mlp(a[0], a[1], a[2])
                elif kind == "hg_start":
                    l0, l1 = vec[:, COL["lb"]:COL["lb"] + KT], vec[:, COL["lb"] + KT:COL["lb"] + 2 * KT]
                    link(v.tensor_tensor(tmp_c[:, 2, :], l0, l1, ALU.max))
                    link(v.tensor_tensor(tmp_c[:, 0, :], l0, tmp_c[:, 2, :], ALU.subtract))
                    v.tensor_tensor(tmp_c[:, 1, :], l1, tmp_c[:, 2, :], ALU.subtract).then_inc(lb_in, 1)
                    v.wait_ge(lb_exp, 1)
                    link(v.tensor_tensor(tmp_c[:, 0, :], tmp_c[:, 2, :], tmp_c[:, 3, :], ALU.add))
                    link(v.reciprocal(tmp_c[:, 1, :], tmp_c[:, 0, :]))
                    link(v.tensor_tensor(lb_c[:, 0, :], tmp_c[:, 2, :], tmp_c[:, 1, :], ALU.mult))
                    link(v.tensor_scalar(lb_c[:, 1, :], lb_c[:, 0, :], -1.0, 1.0, ALU.mult, ALU.add))
                elif kind == "level":
                    l = a[0]
                    if l == 0:
                        link(v.memset(A[:, H_ST:H_ST + 2048], 0.0))
                    if l == LEVELS:
                        continue
                    W = 4 * SEQ
                    for g in range(2):
                        v.wait_ge(lv_ps, 2 * l + g + 1)
                        for i in range(2):
                            st = A[:, H_ST + 1024 * g + 512 * i:][:, 0:512].rearrange("p (a b) -> p a b", b=P)
                            ps = B[4 + 2 * g + i][:, :].rearrange("p (a b) -> p a b", b=P)
                            link(v.copy_predicated(st, level_m[:, l, :].unsqueeze(1).to_broadcast([P, 4, P]), ps))
                        q, k = A[:, H_Q + W * g:][:, 0:W], A[:, H_K + W * g:][:, 0:W]
                        if l == 0:
                            v.tensor_tensor(q, q, A[:, H_F + W * g:][:, 0:W], ALU.mult).then_inc(lv_used, 1)
                            v.wait_ge(lv_used, g + 1)
                            continue
                        w = 1 << (l - 1)
                        nbk = W // (2 * w)
                        ends = (A[:, H_F + W * g:][:, 0:W] if l == 1 else
                                A[:, H_TMP + (W if l % 2 else 0) + W // 2 * g:][:, 0:W // w])
                        e2 = ends.rearrange("p (n s) -> p n s", s=2)
                        q2 = q.rearrange("p (n s w) -> p n s w", s=2, w=w)
                        k2 = k.rearrange("p (n s w) -> p n s w", s=2, w=w)
                        eb = [e2[:, :, s:s + 1].to_broadcast([P, nbk, w]) for s in range(2)]
                        link(v.tensor_tensor(q2[:, :, 1, :], q2[:, :, 1, :], eb[0], ALU.mult))
                        nxt = A[:, H_TMP + (0 if l % 2 else W) + W // 2 * g:][:, 0:nbk]
                        link(v.tensor_tensor(nxt, e2[:, :, 0], e2[:, :, 1], ALU.mult))
                        v.tensor_tensor(k2[:, :, 0, :], k2[:, :, 0, :], eb[1], ALU.mult).then_inc(lv_used, 1)
                        v.wait_ge(lv_used, 2 * l + g + 1)
                elif kind == "hg_out":
                    o = A[:, H_K:H_K + 2048].rearrange("p (h t v) -> p h t v", h=HG_HEADS, t=TT)
                    gate = arena(H_G, TT, D)
                    v.wait_ge(ho_read, 4)
                    sq = A[:, H_F:H_F + 1024].rearrange("p (h v) -> p h v", h=HG_HEADS)
                    for t in range(TT):
                        link(v.tensor_tensor(sq, o[:, :, t, :], o[:, :, t, :], ALU.mult))
                        link(v.reduce_sum(ve[:, 8 * t:8 * t + 8], sq, AX.X))
                    v.tensor_scalar(ve[:, :], ve[:, :], 1.0 / P, RMS_EPS, ALU.mult, ALU.add).then_inc(var_ready, 1)
                    newton(0, 16)
                    for t in range(TT):
                        rb = rstd[:, 8 * t:8 * t + 8].unsqueeze(2).to_broadcast([P, HG_HEADS, P])
                        link(v.tensor_tensor(o[:, :, t, :], o[:, :, t, :], rb, ALU.mult))
                        ins = v.tensor_tensor(o[:, :, t, :], o[:, :, t, :],
                                              gate[:, t, :].rearrange("p (h v) -> p h v", h=HG_HEADS), ALU.mult)
                        if t == 0:
                            link(ins)
                    ins.then_inc(o_ready, 1)


def kernel(**inputs):
    import numpy as np
    import concourse.bacc as bacc
    from concourse.bass_utils import run_bass_kernel_spmd as run

    g = {k: np.asarray(a) for k, a in inputs.items()}

    def wide(w):
        return w.reshape(KT, P, -1, 256).transpose(2, 1, 0, 3).reshape(-1, P, UNIT)

    def tall(w):
        return w.reshape(-1, 2, P, D).transpose(0, 2, 1, 3).reshape(-1, P, UNIT)

    def rank(w):
        return w.reshape(2, P, -1, D).transpose(2, 1, 0, 3).reshape(-1, P, UNIT)

    def mlp(w1, w2):
        up, dn = wide(w1), tall(w2)
        order = [up[0]]
        for k in range(1, PAIRS):
            order += [up[k], dn[k - 1]]
        return np.stack(order + [dn[PAIRS - 1]])

    z = lambda k: np.zeros((D, k), np.float32)
    ab = g["ab_w_in"][0]
    aq, ak, av, cq, bk, bv, bik, biw = np.split(ab, np.cumsum([512, 128, 128, RANK, HD, HD, HD]), axis=1)
    qkt = np.concatenate([aq, ak[:, :64], ak[:, :64], ak[:, 64:], ak[:, 64:], bk, bk, bik, bik], axis=1)
    c_in = g["c_w_in"][0]
    cqkv = [wide(c_in[:, D * i:D * (i + 1)]) for i in range(3)]
    dkv = g["kv_w_dkv_2"]
    uq = g["mla_w_uq_2"][0].reshape(RANK, MLA_HEADS, NOPE + ROPE)
    stream = np.concatenate([
        wide(cq), wide(np.concatenate([av, bv, biw, z(56)], axis=1)), wide(qkt),
        rank(np.concatenate([g["ab_w_uq"][0], g["ab_w_uiq"][0]], axis=1)), tall(g["ab_w_out"][0]),
        mlp(g["mlp_w1"][0], g["mlp_w2"][0]),
        cqkv[2], np.stack([cqkv[i][j] for j in range(4) for i in range(2)]), tall(g["c_w_out"][0]),
        mlp(g["mlp_w1"][1], g["mlp_w2"][1]),
        wide(g["hgrn_w_q_2"][0]), wide(g["hgrn_w_f_2"][0]), wide(g["hgrn_w_i_2"][0]), wide(g["hgrn_w_g_2"][0]),
        tall(g["hgrn_w_o_2"][0]),
        mlp(g["mlp_w_up_2"][0], g["mlp_w_down_2"][0]),
        wide(dkv[:, :RANK]), wide(np.concatenate([dkv[:, RANK:], dkv[:, RANK:], z(P)], axis=1)),
        wide(g["mla_w_dq_2"][0]), rank(g["kv_w_uk_2"]), rank(g["kv_w_uv_2"]),
        rank(np.concatenate([uq[:, :, :NOPE].reshape(RANK, -1), uq[:, :, NOPE:].reshape(RANK, -1)], axis=1)),
        tall(g["mla_w_o_2"][0]),
        mlp(g["mlp_w_up_2"][1], g["mlp_w_down_2"][1]),
    ])
    assert stream.shape == (UNITS, P, UNIT)

    def columns(a):
        return np.asarray(a).reshape(-1, P).T

    cols = np.concatenate([columns(g[k]) for k in (
        "c", "ln_g", "ln_b", "ab_q_norm", "hgrn_norm_2", "mla_norm_2", "mla_q_norm_2", "kv_in_norm_2", "kv_norm_2",
        "mlp_norm_2", "hgrn_lb_logits_2")], axis=1)

    i, j = np.arange(P)[:, None], np.arange(P)[None, :]
    consts = [i == j, (i // 64 == j // 64) & ((i % 64 + 32) % 64 == j % 64), i == j]
    consts = [m.astype(np.float32) for m in consts]
    consts += [np.where(j <= i, 0.0, NEG).astype(np.float32), np.where(j > i, 0.0, NEG).astype(np.float32)]
    consts.append((i == j).astype(np.float32))
    for l in range(1, LEVELS):
        w = 1 << (l - 1)
        consts.append(((i // (2 * w) == j // (2 * w)) & (i // w % 2 == 0) & (j // w % 2 == 1)).astype(np.float32))
    consts = np.stack(consts, axis=1).reshape(P, N_CONST * P)
    inv = (np.float32(10000.0) ** (-np.arange(0, HD, 2, dtype=np.float32) / np.float32(HD))).astype(np.float32)
    inv_col, sign = inv[np.arange(P) % 32], np.where(np.arange(P) % 64 < 32, -1.0, 1.0).astype(np.float32)
    angle = np.arange(SEQ, dtype=np.float32)[None, :] * inv_col[:, None]
    arrays = {
        "stream": stream,
        "ada_w": g["ada_w"].reshape(4, KT, P, 3 * D),
        "ada_b": g["ada_b"].reshape(4, 3 * D),
        "x": g["x"][0],
        "x_t": g["x"][0].T,
        "pos": g["positions"].reshape(SEQ),
        "cols": cols,
        "ln_g": g["ln_g"],
        "ln_b": g["ln_b"],
        "sinks": g["ab_sinks"][0],
        "g_norm": g["hgrn_g_norm_2"][0],
        "final_norm": g["final_norm_2"],
        "consts": consts,
        "rope_cols": np.stack([inv_col, sign], axis=1),
        "rope_2": np.stack([np.cos(angle), np.sin(angle) * sign[:, None]], axis=1).astype(np.float32),
    }
    nc = bacc.Bacc("TRN2", target_bir_lowering=False, num_devices=1)
    args = []
    for name in arrays:
        arrays[name] = np.ascontiguousarray(arrays[name])
        args.append(nc.dram_tensor(name, arrays[name].shape, mybir.dt.from_np(arrays[name].dtype),
                                   kind="ExternalInput").ap())
    args.append(nc.dram_tensor("out", (SEQ, D), mybir.dt.float32, kind="ExternalOutput").ap())
    two_block_kernel(nc, *args)
    r = run(nc, [arrays], core_ids=[0])
    return r.results[0]["out"].reshape(1, SEQ, D)
```

```python
import concourse.bass as bass
from concourse import mybir
from contextlib import ExitStack

D = 1024
SEQ = 256
P = 128
TT = SEQ // P
KT = D // P
HD = 64
D_FF = 4 * D
HEADS_A, KV_A, HEADS_B, HEADS_C = 8, 2, 8, 16
TOPK = min(256, SEQ // 4)
IDX_HEADS = 8
HG_HEADS = 8
MLA_HEADS, NOPE, ROPE = 16, 128, 64
RANK = 256
ALPHA = (2 * 2) ** 0.25
LN_EPS, RMS_EPS = 1e-5, 1e-6
NEG = -1.0e30
TAKEN = -3.0e38

UNIT = 2048
SLOTS = 4
AB = 0
M0 = AB + 11
CU = M0 + 32
M1 = CU + 16
HG = M1 + 32
M2 = HG + 20
ML = M2 + 32
M3 = ML + 18
UNITS = M3 + 32
PAIRS = D_FF // 256

COL = {}
_at = 0
for _name, _n in (("c", 8), ("ln_g", 32), ("ln_b", 32), ("ab_q", 2), ("hgrn", 8), ("mla", 8), ("mla_q", 2),
                  ("kv_in", 8), ("kv", 2), ("mlp", 16), ("lb", 16)):
    COL[_name] = _at
    _at += _n
NCOLS = _at

LEVELS = 8
N_CONST = 4 + LEVELS
TWO_PI = 6.283185307179586
PI_BELOW = 3.1415925
GUESS = 1597463007.0
ROUNDER = 1.5 * 2.0 ** 23


def _parts(x, bits, n):
    import math
    out = []
    for _ in range(n - 1):
        step = 2.0 ** (math.floor(math.log2(abs(x))) - bits + 1)
        out.append(math.floor(x / step) * step)
        x -= out[-1]
    return out + [x]


TWO_PI_PARTS = _parts(TWO_PI, 8, 4)

HTF = 0
ADAW = HTF + 2048
ADAC = ADAW + 3 * D
GATE = ADAC + 3 * D
SCR = GATE + D
ARENA = SCR + 7424


START_BUFS = 4


def START_BUF(A, k):
    at = (ADAW, SCR, SCR + 2 * D, SCR + 4 * D)[k % START_BUFS]
    return A[:, at:at + 2 * D]


def two_block_kernel(nc, stream, ada_w, ada_b, x, x_t, pos, cols, ln_g, ln_b, sinks, g_norm, final_norm,
                     consts, rope_cols, rope_2, out):
    f32, f32r, bf16 = mybir.dt.float32, mybir.dt.float32r, mybir.dt.bfloat16
    ALU = mybir.AluOpType
    ACT = mybir.ActivationFunctionType
    AX = mybir.AxisListType
    ctx = ExitStack()
    with ctx:
        def sb(name, shape, dt=f32):
            return ctx.enter_context(nc.sbuf_tensor(name, shape, dt))

        def sem(name):
            return ctx.enter_context(nc.semaphore(name))

        raw = sb("raw", [P, SLOTS, UNIT])
        w_hi = sb("w_hi", [P, SLOTS, UNIT], f32r)
        w_lo = sb("w_lo", [P, SLOTS, UNIT], f32r)
        X = sb("X", [P, TT, D])
        hT_hi = sb("hT_hi", [P, KT, SEQ], f32r)
        hT_lo = sb("hT_lo", [P, KT, SEQ], f32r)
        R = sb("R", [P, 2, KT, SEQ], f32r)
        A = sb("A", [P, ARENA])
        ident = sb("ident", [P, P])
        perm = sb("perm", [P, P])
        ones = sb("ones", [P, P])
        ident_b = sb("ident_b", [P, P], bf16)
        causal_b = sb("causal_b", [P, P], bf16)
        band_b = sb("band_b", [P, P], bf16)
        level_m = sb("level_m", [P, LEVELS, P], mybir.dt.uint8)
        cosT = sb("cosT", [P, SEQ])
        sinT = sb("sinT", [P, SEQ])
        vec = sb("vec", [P, NCOLS])
        silu_c = sb("silu_c", [P, KT])
        zero8 = sb("zero8", [P, KT])
        sc_c = sb("sc_c", [P, KT])
        bi_c = sb("bi_c", [P, KT])
        tmp_c = sb("tmp_c", [P, 4, KT])
        rc = sb("rc", [P, 2])
        sink_r = sb("sink_r", [P, HEADS_A])
        lb_c = sb("lb_c", [P, 2, KT])
        bn = sb("bn", [P, TT, 2, 6])
        mv = sb("mv", [P, TT, 2])
        ve = sb("ve", [P, 16])
        nw = sb("nw", [P, 2, 16])
        nmr = sb("nmr", [P, TT])
        rstd = sb("rstd", [P, 16])
        mx, nb, sm, sk, ri = (sb(x_, [P, 4, 2]) for x_ in ("mx", "nb", "sm", "sk", "ri"))
        B = [ctx.enter_context(nc.psum_tensor(f"bank{i}", [P, 512], f32)) for i in range(8)]

        def arena(at, *shape):
            n = 1
            for s in shape:
                n *= s
            v = A[:, at:at + n]
            if len(shape) == 2:
                v = v.rearrange("p (a b) -> p a b", a=shape[0])
            return v

        def two(v):
            return v.rearrange("p (a b) -> p a b", a=2)

        hTf = arena(HTF, KT, SEQ)
        cT_f = arena(HTF + 1024, 2, SEQ)
        ada_acc, gate_r = arena(ADAC, 3 * D), arena(GATE, D)
        START_CONSTS = HTF + 3 * 512
        gate_bufs = [((0, 2), X[:, :, :].rearrange("p t d -> p (t d)")), ((2, 5), arena(ADAW, 3 * D)),
                     ((5, 7), arena(SCR + 2 * D, 2 * D)), ((7, 8), arena(HTF, D))]
        gate_w = [buf[:, D * i:D * i + D] for (k0, k1), buf in gate_bufs for i in range(k1 - k0)]

        def ada_part(part):
            return arena(ADAW + D * part, D)

        def adas_before(s_, k=0, part=0):
            return (2 * KT + 3 * KT * (s_ - 1) if s_ else 0) + (3 if s_ else 2) * k + part

        N = arena(SCR, TT, D)
        rows = arena(SCR + 2048, 2, D)
        u_f = arena(SCR + 4096, 2, 512)
        R_hi, R_lo = R[:, 0], R[:, 1]
        u_hi = [R[:, 0, 2 * i:2 * i + 2, :] for i in range(2)]
        u_lo = [R[:, 1, 2 * i:2 * i + 2, :] for i in range(2)]

        AB_QK = SCR
        AB_TOK = SCR + 16 * 256
        AB_CQ = AB_TOK + 512
        AB_IX = AB_CQ
        AB_TMP = AB_IX + 768
        TURNED = HTF + 1536
        AB_SCORE = AB_TMP + 1024
        AB_MASK = AB_SCORE + 384
        C_V, C_QK = SCR, SCR + 2048
        C_TMP = C_QK + 4096
        H_Q, H_K, H_F, H_V, H_G, H_ST = 0, 2048, 4096, 6144, 8192, 10240
        H_S01 = H_ST + 2048
        H_TMP = H_S01 + 1024
        H_GN = H_TMP + 2048
        H_E = H_GN + P
        L_QN, L_KN, L_QR, L_KR, L_V = 2048, 6144, 10240, 12288, 12544
        L_C = {"ckv": L_V, "dq": L_V + 512}
        L_TMP = L_V + 1024
        L_TURNED = L_V + 2048
        assert max(L_V + 4096, H_E + 1024, C_TMP + 1024, AB_MASK + 224) <= ARENA
        score = A[:, AB_SCORE:AB_SCORE + 384]
        chosen_b = A[:, AB_MASK:AB_MASK + 192].bitcast(bf16)
        m8, iw = arena(AB_MASK + 192, 2, 8), arena(AB_MASK + 208, TT, IDX_HEADS)
        gn_r = A[:, H_GN:H_GN + P]

        def tile_at(base, j):
            return A[:, base + 256 * j:base + 256 * (j + 1)]

        raw_full = [sem(f"raw_full{i}") for i in range(SLOTS)]
        ld_start = [sem(f"ld_start{i}") for i in range(START_BUFS)]
        (hi_done, lo_done, unit_done, fill_done, fill_read, u_ready, v_step, y_done, y_read, rstd_ready,
         n_ready, pair_turned, pair_f, pair_ready, x_ready) = map(sem, (
            "hi_done", "lo_done", "unit_done", "fill_done", "fill_read", "u_ready", "v_step", "y_done", "y_read",
            "rstd_ready", "n_ready", "pair_turned", "pair_f", "pair_ready", "x_ready"))
        ld_adas = [sem(f"ld_ada{i}") for i in range(3)]
        (ld_const, ld_row, ld_gate, ld_level, ld_bias, ld_sink, ld_vec, ld_pos, ld_x, ld_xt, ld_gn, ld_rope2, ld_fn) = map(sem, (
            "ld_const", "ld_row", "ld_gate", "ld_level", "ld_bias", "ld_sink", "ld_vec", "ld_pos", "ld_x", "ld_xt", "ld_gn", "ld_rope2",
            "ld_fn"))
        (consts_ready, c_exp, ang_ready, trig_done, ada_used, gate_used, acc_zero, ada_col, col_ready, gate_ps, gate_read, turn_f,
         turn_ps, roped, s_done, max_done, exp_done, t_done, pt_done, pv_done, o_done) = map(sem, (
            "consts_ready", "c_exp", "ang_ready", "trig_done", "ada_used", "gate_used", "acc_zero", "ada_col", "col_ready", "gate_ps",
            "gate_read", "turn_f", "turn_ps", "roped", "s_done", "max_done", "exp_done", "t_done", "pt_done", "pv_done",
            "o_done"))
        (ix_ps, ix_relu, ix_used, chosen, e_done, silu_done, lb_in, lb_exp, lv_ps, lv_used, s01_done, ho_ps, ho_read, o_ready,
         out_ready, stored) = map(sem, (
            "ix_ps", "ix_relu", "ix_used", "chosen", "e_done", "silu_done", "lb_in", "lb_exp", "lv_ps", "lv_used", "s01_done",
            "ho_ps", "ho_read", "o_ready", "out_ready", "stored"))

        C_T = {"cq_ab": (R_lo[:, 4:6, :], R_lo[:, 6:8, :]), "cq": (hT_hi[:, 4:6, :], hT_lo[:, 4:6, :]),
               "ckv": (hT_hi[:, 6:8, :], hT_lo[:, 6:8, :])}

        def head(n):
            pp = A[:, HTF + 384 * (n % 2):][:, 0:384], A[:, HTF + 768 + 384 * (n % 2):][:, 0:384]
            if n < 8:
                kv = n // (HEADS_A // KV_A)
                return dict(qk=[(tile_at(AB_QK, n // 2), tile_at(AB_QK, 4 + kv), 64 * (n % 2), HD)],
                            v=[A[:, AB_TOK + 256 * t + 64 * kv:][:, 0:64] for t in range(TT)], dv=HD, mask="band",
                            scale=HD ** -0.5, sink=n, o=tile_at(AB_QK, n // 2), oc=64 * (n % 2), pp=pp,
                            units=(AB + 1, AB + 2, AB + 5 + n // 4))
            if n < 16:
                h = n - 8
                return dict(qk=[(tile_at(AB_QK, 8 + h // 2), tile_at(AB_QK, 6), 64 * (h % 2), HD)],
                            v=[A[:, AB_TOK + 256 * t + 128:][:, 0:64] for t in range(TT)], dv=HD, mask="chosen",
                            scale=HD ** -0.5, sink=None, o=tile_at(AB_QK, 8 + h // 2), oc=64 * (h % 2), pp=pp,
                            units=(AB + 1, AB + 3, AB + 4))
            if n < 32:
                h = n - 16
                q, k = 4 * (h // 4) + (h % 4) // 2, 4 * (h // 4) + 2 + (h % 4) // 2
                return dict(qk=[(tile_at(C_QK, q), tile_at(C_QK, k), 64 * (h % 2), HD)],
                            v=[A[:, C_V + D * t + 64 * h:][:, 0:64] for t in range(TT)], dv=HD, mask="causal",
                            scale=HD ** -0.5, sink=None, o=tile_at(C_QK, q), oc=64 * (h % 2), pp=pp,
                            units=(CU + h // 4, CU + 4 + 2 * (h // 4), CU + 5 + 2 * (h // 4)))
            h = n - 32
            return dict(qk=[(tile_at(L_QN, h), tile_at(L_KN, h), 0, NOPE),
                            (tile_at(L_QR, h // 2), tile_at(L_KR, 0), 64 * (h % 2), ROPE)],
                        v=[A[:, L_V + 2 * D * t + 128 * h:][:, 0:128] for t in range(TT)], dv=128, mask="causal",
                        scale=(NOPE + ROPE) ** -0.5, sink=None, o=tile_at(L_QN, h), oc=0, pp=pp,
                        units=(ML + 1, ML + 4) + ((ML + 3, ML + 5, ML + 6) if h < 8 else (ML + 7, ML + 8, ML + 9)))

        O_TILES = {"ab": [tile_at(AB_QK, j) for j in (0, 1, 2, 3, 8, 9, 10, 11)],
                   "c": [tile_at(C_QK, j) for j in (0, 1, 4, 5, 8, 9, 12, 13)],
                   "hg": [tile_at(H_K, j) for j in range(8)],
                   "la": [tile_at(L_QN, j) for j in range(8)], "lb": [tile_at(L_QN, 8 + j) for j in range(8)]}

        STAGE = {"ab": (TURNED, AB_TMP), "c": (TURNED, C_TMP), "hg": (HTF, HTF + 512), "la": (TURNED, TURNED),
                 "lb": (HTF, HTF + 512)}
        TURN_TO = {"ab": (hT_hi, hT_lo), "c": (hT_hi, hT_lo), "hg": (hT_hi, hT_lo), "la": (R_hi, R_lo),
                   "lb": (hT_hi, hT_lo)}

        def fills(u, form, src, reader, dsts):
            return [("fill", u, i, len(dsts), form, src, reader, d) for i, d in enumerate(dsts)]

        LAG = 3

        def whole(s_, k):
            return [("ada", s_, k, part) for part in range(3)]

        def turn_pair(name, j):
            return [("turn", name, j)]

        def downs(u0, groups, after=None):
            s, n_ = [], len(groups)
            for j, g in enumerate(groups):
                if j < n_ - 2:
                    s += [("down", u0 + j, g, j == 0)] + (after or {}).get(j, [])
            return s + [("last", u0 + n_ - 2, groups[-2:])]

        def ab_steps():
            cq = A[:, AB_CQ:AB_CQ + 512]
            s = fills(AB, "N", "h", "plain", [two(cq)])
            s += fills(AB + 1, "N", "h", "plain", [two(A[:, AB_TOK:AB_TOK + 512])])
            s += [("norm2", cq, AB), ("gate_sum",)]
            s += fills(AB + 2, "T", "h", "rope", [AB_TMP])
            s += [("turn2", cq, COL["ab_q"], "cq_ab", 0)]
            s += fills(AB + 3, "T", "h", "rope", [AB_TMP])
            rope = lambda tile: [("rope", AB_TMP, TURNED, AB_QK + 256 * tile, 512)]
            s += rope(4)
            f = fills(AB + 4, "T", "cq_ab", "rope", [AB_TMP] * 4)
            s += [f[0]] + rope(6) + [f[1]] + rope(12) + [("gate0",), f[2]] + rope(14) + [f[3]] + rope(8)
            s += fills(AB + 5, "T", "h", "rope", [AB_TMP]) + rope(10)
            s += [("index", h) for h in range(3)]
            s += fills(AB + 6, "T", "h", "rope", [AB_TMP]) + rope(0)
            s += [("index", h) for h in range(3, IDX_HEADS)] + rope(2)
            ada_parts = [("ada", 1, k, part) for k in range(6) for part in range(3)]
            for n in range(16 + LAG):
                s += [("head", n, 0, 16)]
                if n < TOPK // 8:
                    s += [("topk", n)]
                if n == TOPK // 8 - 1:
                    s += [("chosen",)]
                if n >= 1:
                    s, ada_parts = s + ada_parts[:1], ada_parts[1:]
                if n in (7, 11, 15):
                    s += turn_pair("ab", (n - 7) // 4)
            s += ada_parts + turn_pair("ab", 3) + [("rows", 0, 0)]
            return s + downs(AB + 7, [0, 1, 2, 3], {0: whole(1, 6), 1: whole(1, 7)})

        def c_steps():
            s = []
            for j in range(4):
                s += fills(CU + j, "N", "h", "plain", [arena(C_V, TT, D)[:, :, 256 * j:256 * j + 256]])
                if j >= 1:
                    s += whole(3, j - 1)
            rope = lambda j: [("rope", C_TMP, TURNED, C_QK + 512 * j, 512)]
            n = 16
            for j in range(8):
                s += fills(CU + 4 + j, "T", "h", "rope", [C_TMP])
                if j:
                    s += rope(j - 1)
                if j in (2, 4, 6):
                    s += whole(3, 2 + j // 2)
                if j >= 3:
                    for _ in range(2 if j > 3 else 1):
                        s += [("head", n, 16, 32)]
                        n += 1
            s += rope(7)
            after = {25: 0, 28: 1, 31: 2}
            while n < 32 + LAG:
                s += [("head", n, 16, 32)]
                if n in after:
                    s += turn_pair("c", after[n])
                if n in (27, 28, 29):
                    s += [("ada", 3, 6, n - 27)]
                n += 1
            s += turn_pair("c", 3) + [("rows", 1, 0)]
            return s + downs(CU + 12, [0, 1, 2, 3], {0: whole(3, 7)})

        def hg_steps():
            value = lambda u, j: fills(u, "N", "h", "plain", [arena(H_V, TT, D)[:, :, 256 * j:256 * j + 256]])
            s = [("hg_start",)] + value(HG, 0) + value(HG + 1, 1)
            for j in range(4):
                s += fills(HG + 2 + j, "T", "h", "silu", [A[:, H_Q + 512 * j:H_Q + 512 * (j + 1)]])
            for j in range(4):
                s += fills(HG + 6 + j, "T", "h", "forget", [j])
            for j in range(8):
                s += [("level", j)]
                if j < 2:
                    s += value(HG + 10 + j, 2 + j)
                elif j < 6:
                    s += fills(HG + 10 + j, "N", "h", "gate", [arena(H_G, TT, D)[:, :, 256 * (j - 2):256 * (j - 2) + 256]])
            s += [("level", LEVELS), ("hg_out",)] + [x_ for j in range(4) for x_ in turn_pair("hg", j)]
            return s + downs(HG + 16, [0, 1, 2, 3])

        def mla_steps():
            ckv, dq = (A[:, L_C[k_]:L_C[k_] + 512] for k_ in ("ckv", "dq"))
            s = fills(ML, "N", "h", "plain", [two(ckv)])
            s += [("second", 0)] + fills(ML + 1, "Th", "h", "rope", [L_TMP])
            s += [("norm2", ckv, ML), ("second", 1)]
            s += fills(ML + 2, "N", "R", "plain", [two(dq)])
            s += [("turn2", ckv, COL["kv"], "ckv", ML + 2), ("rope", L_TMP, L_TURNED, L_KR, 256), ("norm2", dq, ML + 2)]
            f = fills(ML + 3, "T", "ckv", "plain", [A[:, L_KN + 512 * i:][:, 0:512] for i in range(4)])
            s += f[0:3] + [("turn2", dq, COL["mla_q"], "cq", 0)] + f[3:]
            for i, f in enumerate(fills(ML + 4, "T", "cq", "rope", [L_TMP] * 4)):
                s += [f] + ([("rope", L_TMP, L_TURNED, L_QR + 512 * (i - 1), 512)] if i else [])
            s += [("rope", L_TMP, L_TURNED, L_QR + 512 * 3, 512)]
            v = arena(L_V, TT, 2 * D)

            def values(u, j):
                return fills(u, "W", "ckv", "plain",
                             [v[:, t, 1024 * j + 512 * h:1024 * j + 512 * h + 512] for t in range(TT) for h in range(2)])

            s += values(ML + 5, 0)
            s += fills(ML + 6, "T", "cq", "plain", [A[:, L_QN + 512 * i:][:, 0:512] for i in range(4)])
            rest = fills(ML + 7, "T", "ckv", "plain", [A[:, L_KN + 2048 + 512 * i:][:, 0:512] for i in range(4)])
            rest += values(ML + 8, 1)
            rest += fills(ML + 9, "T", "cq", "plain", [A[:, L_QN + 2048 + 512 * i:][:, 0:512] for i in range(4)])
            for n in range(32, 48 + LAG):
                s += [("head", n, 32, 48)]
                take = 2 if n % 2 else 1
                s, rest = s + rest[:take], rest[take:]
                if n in (43, 45, 47, 49):
                    s += turn_pair("la", (n - 43) // 2)
            assert not rest
            return s + downs(ML + 10, list(range(8)), {0: turn_pair("lb", 0) + turn_pair("lb", 1),
                                                       1: turn_pair("lb", 2) + turn_pair("lb", 3)})

        own = lambda name, at=0: (vec[:, COL[name] + at:COL[name] + at + KT], zero8)
        mod = (sc_c, bi_c)

        def bound(b, what, last_unit, sb_, second=None, lead=()):
            return [("bound", b, what, last_unit, sb_, second, lead)]

        STEPS = [("start",), ("finish", 0)] + ab_steps()
        STEPS += [("finish", 1)] + bound(0, "ln", AB + 10, mod) + [
            ("gate", 1), ("rows", 0, 1), ("mlp", 0, M0, 2)]
        STEPS += [("finish", 2)] + bound(1, "ln", M0 + 31, mod, lead=(CU, CU + 1)) + [("gate", 2)] + c_steps()
        STEPS += [("finish", 3)] + bound(2, "ln", CU + 15, mod) + [
            ("gate", 3), ("rows", 1, 1), ("mlp", 1, M1, None)]
        STEPS += bound(3, "lnrms", M1 + 31, own("hgrn"), lead=(HG, HG + 1)) + hg_steps()
        STEPS += bound(4, "rms", HG + 19, own("mlp")) + [("mlp", 2, M2, None)]
        STEPS += bound(5, "rms", M2 + 31, own("kv_in"), own("mla"), lead=(ML,)) + mla_steps()
        STEPS += bound(6, "rms", ML + 17, own("mlp", 8)) + [("final_row",), ("mlp", 3, M3, None)]
        STEPS += bound(7, "final", M3 + 31, None)

        def T_unit(u0, k):
            return u0 + (2 * k - 1 if k else 0)

        def D_unit(u0, k):
            return u0 + (2 * k + 2 if k < PAIRS - 1 else 2 * PAIRS - 1)

        LOOPS = (PAIRS - 4) // 2

        block = ctx.enter_context(nc.Block())

        @block.sync
        def _(sp):
            def load(u, s):
                sp.dma_start(raw[:, s, :], stream[u]).then_inc(raw_full[s], 16)

            def load_start(k):
                if k >= START_BUFS:
                    sp.wait_ge(ada_used, adas_before(0, k - START_BUFS + 1))
                sp.dma_start(START_BUF(A, k), ada_w[0, k, :, 0:2 * D]).then_inc(ld_start[k % START_BUFS], 16)

            sp.dma_start(vec[:, :], cols).then_inc(ld_vec, 16)
            sp.dma_start(rc[:, :], rope_cols).then_inc(ld_pos, 16)
            sp.dma_start(A[:, HTF:HTF + 256].bitcast(mybir.dt.int32), pos.partition_broadcast(P)).then_inc(ld_pos, 16)
            sp.dma_start(A[:, START_CONSTS:START_CONSTS + 4 * P], consts[:, 0:4 * P]).then_inc(ld_const, 16)
            for k in range(START_BUFS):
                load_start(k)
            sp.wait_ge(trig_done, 2)
            sp.wait_ge(consts_ready, 1)
            sp.dma_start(hTf, x_t.rearrange("(k p) t -> p k t", p=P)).then_inc(ld_xt, 16)
            for k in range(START_BUFS, KT):
                load_start(k)
                if k == 5:
                    load(0, 0)
            load(1, 1)
            load(2, 2)
            sp.wait_ge(ada_used, adas_before(0, KT))
            load(3, 3)
            for (k0, k1), buf in gate_bufs:
                if k1 == KT:
                    sp.wait_ge(pair_ready, 4)
                sp.dma_start(buf.rearrange("p (k n) -> p k n", n=D),
                             ada_w[0, k0:k1, :, 2 * D:3 * D].rearrange("k p n -> p k n")).then_inc(ld_gate, 16)
            sp.wait_ge(gate_used, KT)
            sp.dma_start(X[:, :, :], x.rearrange("(t p) d -> p t d", p=P)).then_inc(ld_x, 16)
            with sp.Fori(1, UNITS // SLOTS) as i:
                for s in range(SLOTS):
                    sp.wait_ge(lo_done, SLOTS * i + (s + 1 - SLOTS))
                    load(SLOTS * i + s, s)
            for u in range(UNITS // SLOTS * SLOTS, UNITS):
                sp.wait_ge(lo_done, u + 1 - SLOTS)
                load(u, u % SLOTS)
            for t in range(TT):
                sp.wait_ge(out_ready, t + 1)
                sp.dma_start(out[t * P:(t + 1) * P, :], N[:, t, :]).then_inc(stored, 16)
            sp.wait_ge(stored, 16 * TT)

        @block.gpsimd
        def _(pool):
            def split(u, s):
                pool.wait_ge(hi_done, u + 1)
                pool.tensor_tensor(w_lo[:, s, :], raw[:, s, :], w_hi[:, s, :], ALU.subtract).then_inc(lo_done, 1)

            with pool.Fori(0, UNITS // SLOTS) as i:
                for s in range(SLOTS):
                    split(SLOTS * i + s, s)
            for u in range(UNITS // SLOTS * SLOTS, UNITS):
                split(u, u % SLOTS)

        @block.tensor
        def _(pe):
            n = dict(fill=0, rope=0, turn=0, plain=0, e=0, pair=0, c=0, gates=0, y=0, norm=0, q=0)
            held = {}
            ready = {}
            made = {}
            led = set()

            def claim(b):
                if b in held:
                    pe.wait_ge(*held[b])

            def weights(u):
                pe.wait_ge(lo_done, u + 1)

            def mm3(o, lh, ll, rh, rl, start, stop):
                pe.matmul(o, lh, rh, start=start, stop=False, skip_group_check=True)
                pe.matmul(o, lh, rl, start=False, stop=False, skip_group_check=True)
                return pe.matmul(o, ll, rh, start=False, stop=stop, skip_group_check=True)

            def source(src):
                return {"h": (hT_hi, hT_lo), "R": (R_hi, R_lo), **C_T}[src]

            def parts_of(u, kts):
                return [t_[:, u % SLOTS, :].rearrange("p (k n) -> p k n", k=kts) for t_ in (w_hi, w_lo)]

            def fill(u, part, parts, form, src, reader):
                kts = KT if parts == 1 else 2
                hh, hl = source(src)
                wh, wl = parts_of(u, kts)
                b = n["fill"] % 2
                bank = B[b]
                if u not in led:
                    claim(b)
                    if part == 0:
                        weights(u)
                    if u:
                        pe.wait_ge(pair_ready, made[src])
                    last = None
                    if form == "W":
                        t, h = part // 2, part % 2
                        for k in range(kts):
                            last = mm3(bank[:, :], hh[:, k, P * t:P * t + P], hl[:, k, P * t:P * t + P],
                                       wh[:, k, 512 * h:512 * h + 512], wl[:, k, 512 * h:512 * h + 512], k == 0,
                                       k == kts - 1)
                    else:
                        for a in range(1 if form == "Th" else 2):
                            o = bank[:, 256 * a:256 * a + 256]
                            for k in range(kts):
                                if u == 0 and a == 0 and k % 2 == 0:
                                    pe.wait_ge(pair_ready, k // 2 + 1)
                                if form == "N":
                                    at = P * a
                                    last = mm3(o, hh[:, k, at:at + P], hl[:, k, at:at + P], wh[:, k, 0:256],
                                               wl[:, k, 0:256], k == 0, k == kts - 1)
                                else:
                                    at = 256 * part + P * a
                                    last = mm3(o, wh[:, k, at:at + P], wl[:, k, at:at + P], hh[:, k, :], hl[:, k, :],
                                               k == 0, k == kts - 1)
                    last.then_inc(unit_done if part == parts - 1 else fill_done, 1)
                n["fill"] += 1
                key = {"plain": "plain", "rope": "rope"}.get(reader, "e")
                n[key] += 1
                held[b] = ({"plain": fill_read, "rope": turn_f, "e": e_done}[key], n[key])
                ready[(u, part)] = ({"plain": fill_read, "rope": roped, "e": silu_done}[key], n[key])

            def lead(units):
                for t in range(TT):
                    if t == 1:
                        groups(1)
                    for i, u in enumerate(units):
                        wh, wl = parts_of(u, KT)
                        b = (n["fill"] + i) % 2
                        if t == 0:
                            claim(b)
                            weights(u)
                        for k in range(KT):
                            if i == 0 and k % 4 == 0:
                                pe.wait_ge(pair_ready, n["pair"] - 1 + k // 4)
                            at = P * t
                            last = mm3(B[b][:, 256 * t:256 * t + 256], hT_hi[:, k, at:at + P], hT_lo[:, k, at:at + P],
                                       wh[:, k, 0:256], wl[:, k, 0:256], k == 0, k == KT - 1)
                        if t == 1:
                            last.then_inc(unit_done, 1)
                led.update(units)

            def down(u, s, lh, ll, first):
                wh = w_hi[:, s, :].rearrange("p (k n) -> p k n", k=2)
                wl = w_lo[:, s, :].rearrange("p (k n) -> p k n", k=2)
                for t in range(TT):
                    for k in range(2):
                        for h in range(2):
                            c = slice(512 * h, 512 * h + 512)
                            m = mm3(B[4 + 2 * t + h][:, :], lh[:, k, P * t:P * t + P], ll[:, k, P * t:P * t + P],
                                    wh[:, k, c], wl[:, k, c], first and k == 0, False)
                m.then_inc(unit_done, 1)

            def down_last(u, rows_, wait_second):
                w = [parts_of(u + i, 2) for i in range(2)]
                for i, t, h in [(0, 0, 0), (0, 0, 1), (1, 0, 0), (1, 0, 1), (0, 1, 0), (1, 1, 0), (0, 1, 1), (1, 1, 1)]:
                    if (i, t, h) == (1, 0, 0):
                        wait_second()
                    c = slice(512 * h, 512 * h + 512)
                    for k in range(2):
                        m = mm3(B[4 + 2 * t + h][:, :], rows_[i][0][:, k, P * t:P * t + P], rows_[i][1][:, k, P * t:P * t + P],
                                w[i][0][:, k, c], w[i][1][:, k, c], False, i == 1 and k == 1)
                    if t == 1 and h == 1:
                        m.then_inc(unit_done, 1)
                    elif i == 1:
                        m.then_inc(y_done, 1)

            def group(b, tiles, out=None):
                claim(b)
                for i, tile in enumerate(tiles):
                    m = pe.transpose(B[b][:, P * i:P * i + P], tile, ident[:, :])
                n["pair"] += 1
                m.then_inc(pair_turned, 1)
                held[b] = (pair_f, n["pair"])

            def groups(t, banks=None):
                n["norm"] += banks is None
                if banks is None:
                    pe.wait_ge(n_ready, n["norm"])
                for j in range(2):
                    group((banks or (2 * t, 2 * t + 1))[j], [N[:, t, P * f:P * f + P] for f in range(4 * j, 4 * j + 4)])

            def qk(k):
                h, bank = head(k), B[4 + k % 2]
                for u in h["units"]:
                    pe.wait_ge(*ready[(u, max(part for u_, part in ready if u_ == u))])
                if k >= 2:
                    pe.wait_ge(exp_done, k - 1)
                for t in range(TT):
                    o = bank[:, 0:128] if t == 0 else bank[:, 128:384]
                    for i, (q, kk, off, w) in enumerate(h["qk"]):
                        pe.matmul(o, q[off:off + w, P * t:P * t + P], kk[off:off + w, 0:P * (t + 1)], start=i == 0,
                                  stop=False, skip_group_check=True)
                    if h["mask"] == "chosen":
                        m = pe.matmul(o, ident_b[:, :], chosen_b[:, 0:128] if t == 0 else chosen_b[:, 128:384],
                                      start=False, stop=True, skip_group_check=True)
                    else:
                        if t == 1 and h["mask"] == "band":
                            pe.matmul(bank[:, 128:256], ident_b[:, :], band_b[:, :], start=False, stop=False,
                                      skip_group_check=True)
                        m = pe.matmul(bank[:, 256 * t:256 * t + P], ident_b[:, :], causal_b[:, :], start=False, stop=True,
                                      skip_group_check=True)
                m.then_inc(s_done, 1)

            def turn_probs(k):
                pe.wait_ge(exp_done, k + 1)
                if k >= 1:
                    pe.wait_ge(pt_done, k)
                for i in range(3):
                    m = pe.transpose(B[6][:, P * i:P * i + P], head(k)["pp"][0][:, P * i:P * i + P], ident[:, :])
                m.then_inc(t_done, 1)

            def pv(k):
                h = head(k)
                pe.wait_ge(pt_done, k + 1)
                if k >= 1:
                    pe.wait_ge(o_done, k)
                dv, pt = h["dv"], h["pp"][1]
                pe.matmul(B[7][:, 0:dv], pt[:, 0:P], h["v"][0], start=True, stop=True, skip_group_check=True)
                pe.matmul(B[7][:, dv:2 * dv], pt[:, P:2 * P], h["v"][0], start=True, stop=False, skip_group_check=True)
                pe.matmul(B[7][:, dv:2 * dv], pt[:, 2 * P:3 * P], h["v"][1], start=False, stop=True,
                          skip_group_check=True).then_inc(pv_done, 1)

            def mlp(m, u0):
                f0, p0 = n["fill"], n["plain"]

                def up(k, kp, u, s):
                    if isinstance(k, int) and k < 2:
                        claim((f0 + kp) % 2)
                    else:
                        pe.wait_ge(fill_read, k + (p0 - 1))
                    pe.wait_ge(lo_done, u + 1)
                    wh = w_hi[:, s, :].rearrange("p (k n) -> p k n", k=KT)
                    wl = w_lo[:, s, :].rearrange("p (k n) -> p k n", k=KT)
                    for a in range(2):
                        for kt in range(KT):
                            if isinstance(k, int) and k == 0 and a == 0 and kt % 4 == 0:
                                pe.wait_ge(pair_ready, n["pair"] - 1 + kt // 4)
                            last = mm3(B[(f0 + kp) % 2][:, 256 * a:256 * a + 256],
                                       wh[:, kt, P * a:P * a + P], wl[:, kt, P * a:P * a + P],
                                       hT_hi[:, kt, :], hT_lo[:, kt, :], kt == 0, kt == KT - 1)
                    last.then_inc(unit_done, 1)

                def dn(k, kp, u, s, first=False):
                    pe.wait_ge(lo_done, u + 1)
                    pe.wait_ge(u_ready, PAIRS * m + k + 1)
                    down(u, s, u_hi[kp], u_lo[kp], first)

                for k in range(2):
                    up(k, k, T_unit(u0, k), T_unit(u0, k) % SLOTS)
                pe.wait_ge(y_read, n["y"])
                pe.wait_ge(gate_read, n["gates"])
                dn(0, 0, D_unit(u0, 0), D_unit(u0, 0) % SLOTS, first=True)
                with pe.Fori(0, LOOPS) as i:
                    for j in range(2):
                        ut, ud = T_unit(u0, 2 + j), D_unit(u0, 1 + j)
                        up(2 * i + (2 + j), j, 4 * i + ut, ut % SLOTS)
                        dn(2 * i + (1 + j), (1 + j) % 2, 4 * i + ud, ud % SLOTS)
                k = PAIRS - 2
                up(k, k % 2, T_unit(u0, k), T_unit(u0, k) % SLOTS)
                dn(k - 1, (k - 1) % 2, D_unit(u0, k - 1), D_unit(u0, k - 1) % SLOTS)
                k = PAIRS - 1
                up(k, k % 2, T_unit(u0, k), T_unit(u0, k) % SLOTS)
                weights(D_unit(u0, k))
                pe.wait_ge(u_ready, PAIRS * m + k)
                down_last(D_unit(u0, k - 1), [(u_hi[j], u_lo[j]) for j in ((k - 1) % 2, k % 2)],
                          lambda: pe.wait_ge(u_ready, PAIRS * m + k + 1))
                n["fill"] += PAIRS
                n["plain"] += PAIRS
                for j in range(2):
                    held[(f0 + j) % 2] = (fill_read, n["plain"] - 1 + j)

            def gate(first=False):
                if n["y"]:
                    pe.wait_ge(y_read, n["y"] - 2)
                if first:
                    pe.wait_ge(gate_used, KT)
                acc = gate_r if first else ada_acc[:, 2 * D:3 * D]
                for h in range(2):
                    m = pe.matmul(B[4 + h][:, :], ones[:, :], acc[:, 512 * h:512 * h + 512], start=True, stop=True)
                m.then_inc(gate_ps, 1)
                n["gates"] += 1

            pe.wait_ge(consts_ready, 1)
            for step in STEPS:
                kind, a = step[0], step[1:]
                if kind == "start":
                    n["pair"] = made["h"] = 4
                elif kind == "finish":
                    pe.wait_ge(ada_used, adas_before(a[0], KT))
                    claim(3)
                    for j in range(2 * KT):
                        m = pe.matmul(B[3][:, j:j + 1], ada_acc[:, P * j:P * j + P], ones[:, 0:1], start=True, stop=True)
                    m.then_inc(ada_col, 1)
                    held[3] = (col_ready, a[0] + 1)
                elif kind == "gate0" or kind == "gate" and a[0] == 2:
                    gate(kind == "gate0")
                elif kind == "fill":
                    fill(*a[0:6])
                elif kind == "rope":
                    pe.wait_ge(turn_f, n["turn"] + 1)
                    claim(2)
                    buf, w = a[0] + 512 * (n["turn"] % 2), a[3]
                    pe.matmul(B[2][:, 0:w], perm[:, :], A[:, buf:buf + w], start=True, stop=True).then_inc(turn_ps, 1)
                    n["turn"] += 1
                    held[2] = (roped, n["turn"])
                elif kind == "turn2":
                    n["c"] += 1
                    pe.wait_ge(o_ready, n["c"])
                    t2 = two(a[0])
                    group(3, [t2[:, t, P * f:P * f + P] for f in range(2) for t in range(TT)])
                    made[a[2]] = n["pair"]
                elif kind == "second":
                    groups(a[0], (2, 3))
                    made["R"] = n["pair"]
                elif kind == "index":
                    h = a[0]
                    if h == 0:
                        pe.wait_ge(*ready[(AB + 3, 0)])
                        pe.wait_ge(*ready[(AB + 4, 1)])
                        pe.wait_ge(gate_read, n["gates"])
                    if h >= 2:
                        pe.wait_ge(ix_relu, h - 1)
                    q, kk, off = tile_at(AB_QK, 12 + h // 2), tile_at(AB_QK, 7), 64 * (h % 2)
                    for t in range(TT):
                        m = pe.matmul(B[4 + h % 2][:, 128 * t:128 + 256 * t], q[off:off + HD, P * t:P * t + P],
                                      kk[off:off + HD, 0:P * (t + 1)], start=True, stop=True)
                    m.then_inc(ix_ps, 1)
                elif kind == "chosen":
                    pass
                elif kind == "head":
                    k, first, last = a
                    if k == first:
                        pe.wait_ge(gate_read, n["gates"])
                        if n["y"]:
                            pe.wait_ge(y_read, n["y"])
                        if k == 0:
                            pe.wait_ge(ix_relu, IDX_HEADS)
                    if k == HEADS_A:
                        pe.wait_ge(chosen, 1)
                    if k < last:
                        qk(k)
                    if first <= k - 2 < last:
                        turn_probs(k - 2)
                    if first <= k - 3 < last:
                        pv(k - 3)
                elif kind == "turn":
                    name, j = a
                    tiles = O_TILES[name]
                    if name == "hg":
                        if j == 0:
                            n["c"] += 1
                            pe.wait_ge(o_ready, n["c"])
                    else:
                        pe.wait_ge(o_done, {"ab": 4 * j + 4, "c": 20 + 4 * j, "la": 34 + 2 * j, "lb": 42 + 2 * j}[name])
                    group(j, [tiles[f][:, P * t:P * t + P] for f in (2 * j, 2 * j + 1) for t in range(TT)])
                    made[(name, j)] = n["pair"]
                    n["turned"] = name
                elif kind in ("down", "last"):
                    u, g = a[0], a[1]
                    if kind == "down" and a[2]:
                        if n["y"]:
                            pe.wait_ge(y_read, n["y"])
                        pe.wait_ge(gate_read, n["gates"])
                        if n["turned"] == "la":
                            pe.wait_ge(o_done, 48)
                        names = ["la", "lb"] if n["turned"] in ("la", "lb") else [n["turned"]]

                    def rows_of(g):
                        hh, hl = TURN_TO[names[g // 4]]
                        c = slice(2 * (g % 4), 2 * (g % 4) + 2)
                        return hh[:, c], hl[:, c]

                    if kind == "down":
                        weights(u)
                        pe.wait_ge(pair_ready, made[(names[g // 4], g % 4)])
                        down(u, u % SLOTS, *rows_of(g), a[2])
                    else:
                        weights(u + 1)
                        pe.wait_ge(pair_ready, made[(names[g[1] // 4], g[1] % 4)])
                        down_last(u, [rows_of(g_) for g_ in g], lambda: None)
                elif kind == "bound":
                    b, what, _, _, second, units = a
                    n["y"] += 2 * TT
                    if what != "final":
                        if what == "lnrms":
                            n["norm"] += TT
                        groups(0)
                        if units:
                            lead(units)
                        elif b < 3:
                            gate()
                        if not units:
                            groups(1)
                        made["h"] = n["pair"]
                elif kind == "mlp":
                    mlp(a[0], a[1])
                elif kind == "level":
                    l = a[0]
                    for g in range(2):
                        if l == 0:
                            pe.wait_ge(silu_done, 8)
                            if g == 0 and n["y"]:
                                pe.wait_ge(y_read, n["y"])
                        else:
                            pe.wait_ge(lv_used, 2 * (l - 1) + g + 1)
                        for h in range(4 * g, 4 * g + 4):
                            for t in range(TT):
                                if l == LEVELS and t == 1:
                                    continue
                                i = (h - 4 * g) if l == LEVELS else 2 * (h - 4 * g) + t
                                bank = B[4 + 2 * g + i // 4]
                                tq = 1 if l == LEVELS else t
                                m = pe.matmul(bank[:, P * (i % 4):P * (i % 4) + P], tile_at(H_K, h)[:, P * t:P * t + P],
                                              tile_at(H_Q, h)[:, P * tq:P * tq + P], start=True, stop=True)
                        m.then_inc(lv_ps, 1)
                elif kind == "hg_out":
                    pe.wait_ge(lv_used, 2 * LEVELS)
                    pe.wait_ge(s01_done, 2)
                    pe.wait_ge(*ready[(HG + 11, 0)])
                    v = arena(H_V, TT, D)
                    for t in range(TT):
                        for h in range(HG_HEADS):
                            o = B[4 + 2 * t + h // 4][:, P * (h % 4):P * (h % 4) + P]
                            if t == 1:
                                pe.matmul(o, A[:, H_S01 + P * h:H_S01 + P * h + P], v[:, 0, P * h:P * h + P], start=True,
                                          stop=False, skip_group_check=True)
                            m = pe.matmul(o, A[:, H_ST + 256 * h + P * t:H_ST + 256 * h + P * t + P],
                                          v[:, t, P * h:P * h + P], start=t == 0, stop=True, skip_group_check=True)
                        m.then_inc(ho_ps, 1)

        @block.scalar
        def _(act):
            n = dict(fill=0, rope=0, pair=0, rstd=0, e=0, x=0, part=0, gates=0)

            def hi(u, s, k):
                act.wait_ge(raw_full[s], 16 * k)
                if not (isinstance(u, int) and u < SLOTS):
                    act.wait_ge(unit_done, u + (1 - SLOTS))
                act.activation(w_hi[:, s, :], raw[:, s, :], ACT.Copy).then_inc(hi_done, 1)

            def ahead(u, i=0):
                if isinstance(i, int) and u + SLOTS >= UNITS:
                    return
                v = u + SLOTS
                hi(4 * i + v if not isinstance(i, int) else v, v % SLOTS, i + (v // SLOTS + 1))

            def turned(b, j, scale, bias):
                t = j // 2 % 2
                n["pair"] += 1
                act.wait_ge(pair_turned, n["pair"] - 4)
                for i in range(4):
                    k = 4 * (j % 2) + i
                    ins = act.activation(hTf[:, k, P * t:P * t + P], B[b][:, P * i:P * i + P], ACT.Identity,
                                         scale=scale[:, k:k + 1], bias=bias[:, k:k + 1])
                ins.then_inc(pair_f, 1)

            def normalise(t, rms):
                n["rstd"] += 1
                act.wait_ge(rstd_ready, n["rstd"])
                bias = zero8[:, 0:1] if rms else nmr[:, t:t + 1]
                act.activation(N[:, t, :], X[:, t, :], ACT.Identity, scale=rstd[:, t:t + 1], bias=bias).then_inc(n_ready, 1)

            def load_ada(s, k, part, i=0):
                act.wait_ge(ada_used, adas_before(s, k - 1, part + 1) if isinstance(i, int) else
                            3 * i + adas_before(s, k - 1, part + 1))
                src = ada_w[s, k + i] if isinstance(i, int) else ada_w[s, i + k]
                act.dma_start(ada_part(part), src[:, D * part:D * part + D]).then_inc(ld_adas[part], 16)

            def ada_begin(s):
                act.wait_ge(acc_zero, s + 1)
                act.dma_start(ada_acc[0:1, :], ada_b[s:s + 1, :]).then_inc(ld_bias, 16)
                for part in range(3):
                    act.wait_ge(ada_used, adas_before(s))
                    act.dma_start(ada_part(part), ada_w[s, 0, :, D * part:D * part + D]).then_inc(ld_adas[part], 16)

            def mlp(m, u0, s_ada):
                f0 = n["fill"]

                def relu(k, kp, u):
                    act.wait_ge(unit_done, u + 1)
                    if not (isinstance(k, int) and PAIRS * m + k < 2):
                        act.wait_ge(u_ready, k + (PAIRS * m - 1))
                    act.activation(u_f[:, kp, :], B[(f0 + kp) % 2][:, :], ACT.Relu).then_inc(fill_read, 1)

                relu(0, 0, T_unit(u0, 0))
                ahead(T_unit(u0, 0))
                relu(1, 1, T_unit(u0, 1))
                ahead(T_unit(u0, 1))
                ahead(D_unit(u0, 0))
                if s_ada:
                    ada_begin(s_ada)
                with act.Fori(0, LOOPS) as i:
                    for j in range(2):
                        relu(2 * i + (2 + j), j, 4 * i + T_unit(u0, 2 + j))
                        ahead(T_unit(u0, 2 + j), i)
                        ahead(D_unit(u0, 1 + j), i)
                        if s_ada and j == 0:
                            for part in range(3):
                                load_ada(s_ada, 1, part, i)
                for k in (PAIRS - 2, PAIRS - 1):
                    relu(k, k % 2, T_unit(u0, k))
                    ahead(T_unit(u0, k))
                    if k < PAIRS - 1:
                        ahead(D_unit(u0, k - 1))
                        if s_ada:
                            for part in range(3):
                                load_ada(s_ada, KT - 1, part)
                n["fill"] += PAIRS

            act.dma_start(sink_r[:, :], sinks.partition_broadcast(P)).then_inc(ld_sink, 16)
            act.wait_ge(acc_zero, 1)
            act.dma_start(ada_acc[0:1, 0:2 * D], ada_b[0:1, 0:2 * D]).then_inc(ld_bias, 16)
            act.dma_start(gate_r[0:1, :], ada_b[0:1, 2 * D:3 * D]).then_inc(ld_bias, 16)
            act.wait_ge(ld_sink, 16)
            act.wait_ge(ld_vec, 16)
            act.activation(silu_c[:, :], vec[:, 0:KT], ACT.Exp, scale=-1.0).then_inc(c_exp, 1)
            act.wait_ge(ang_ready, 1)
            act.activation(sinT[:, :], A[:, HTF + 512:HTF + 768], ACT.Sin).then_inc(trig_done, 1)
            act.activation(cosT[:, :], A[:, HTF + 768:HTF + 1024], ACT.Sin).then_inc(trig_done, 1)
            for u in range(SLOTS):
                hi(u, u, 1)
            for step in STEPS:
                kind, a = step[0], step[1:]
                if kind == "finish" and a[0] == 0:
                    act.wait_ge(ld_xt, 16)
                    act.wait_ge(col_ready, 1)
                    for j in range(4):
                        for k in (2 * j, 2 * j + 1):
                            ins = act.activation(hTf[:, k, :], hTf[:, k, :], ACT.Identity, scale=sc_c[:, k:k + 1],
                                                 bias=bi_c[:, k:k + 1])
                        ins.then_inc(pair_f, 1)
                    n["pair"] = 4
                elif kind in ("gate", "gate0"):
                    act.wait_ge(gate_ps, n["gates"] + 1)
                    act.wait_ge(y_read, 4 * n["gates"]) if n["gates"] else None
                    for h in range(2):
                        ins = act.activation(gate_r[:, 512 * h:512 * h + 512], B[4 + h][:, :], ACT.Identity,
                                             bias=ones[:, 0:1])
                    ins.then_inc(gate_read, 1)
                    n["gates"] += 1
                    if n["gates"] in (1, 3):
                        ada_begin(n["gates"])
                elif kind == "fill":
                    u, part, parts, form, src, reader, dst = a
                    if part == parts - 1:
                        act.wait_ge(unit_done, u + 1)
                    else:
                        n["part"] += 1
                        act.wait_ge(fill_done, n["part"])
                    bank = B[n["fill"] % 2]
                    act.wait_ge(x_ready, TT * n["x"]) if n["x"] else None
                    if u == ML + 5 and part == 0:
                        act.wait_ge(roped, n["rope"])
                    if reader == "plain":
                        if len(dst.shape) == 3:
                            act.activation(dst, two(bank[:, :]), ACT.Copy).then_inc(fill_read, 1)
                        else:
                            act.activation(dst, bank[:, :], ACT.Copy).then_inc(fill_read, 1)
                    elif reader == "rope":
                        w = 256 if form == "Th" else 512
                        r = n["rope"]
                        if r >= 2:
                            act.wait_ge(roped, r - 1)
                        act.activation(A[:, dst + 512 * (r % 2):][:, 0:w], bank[:, 0:w], ACT.Copy).then_inc(turn_f, 1)
                        n["rope"] += 1
                    else:
                        e = A[:, H_E + 512 * (n["e"] % 2):][:, 0:512]
                        if n["e"] >= 2:
                            act.wait_ge(silu_done, n["e"] - 1)
                        if reader == "silu":
                            act.activation(dst, bank[:, :], ACT.Copy)
                        elif reader == "gate":
                            act.activation(dst, two(bank[:, :]), ACT.Copy)
                        act.activation(e, bank[:, :], ACT.Exp, scale=-1.0).then_inc(e_done, 1)
                        n["e"] += 1
                    n["fill"] += 1
                    if part == parts - 1:
                        ahead(u)
                elif kind == "turn2":
                    n["pair"] += 1
                    act.wait_ge(pair_ready, n["pair"] - 1)
                    act.wait_ge(pair_turned, n["pair"] - 4)
                    for k in range(2):
                        ins = act.activation(cT_f[:, k, :], B[3][:, 256 * k:256 * k + 256], ACT.Identity,
                                             scale=vec[:, a[1] + k:a[1] + k + 1], bias=zero8[:, 0:1])
                    ins.then_inc(pair_f, 1)
                elif kind == "second":
                    for j in range(2):
                        if j == 0:
                            act.wait_ge(pair_ready, n["pair"])
                        turned(2 + j, 2 * a[0] + j, *SECOND)
                elif kind == "ada" and a[1] + 1 < KT:
                    load_ada(a[0], a[1] + 1, a[2])
                elif kind == "index":
                    h = a[0]
                    act.wait_ge(ix_ps, h + 1)
                    if h >= 2:
                        act.wait_ge(ix_used, h - 1)
                    act.activation(A[:, AB_IX + 384 * (h % 2):][:, 0:384], B[4 + h % 2][:, 0:384],
                                   ACT.Relu).then_inc(ix_relu, 1)
                elif kind == "head":
                    k, first, last = a
                    if k < last:
                        act.wait_ge(max_done, k + 1)
                        if k == first:
                            act.wait_ge(pair_ready, n["pair"])
                        if k >= 2:
                            act.wait_ge(t_done, k - 1)
                        h, bank = head(k), B[4 + k % 2]
                        pb = h["pp"][0]
                        act.activation(pb[:, 0:128], bank[:, 0:128], ACT.Exp, bias=nb[:, k % 4, 0:1], scale=h["scale"],
                                       accum_out=sm[:, k % 4, 0:1])
                        if h["sink"] is not None:
                            act.activation(sk[:, k % 4, :], nb[:, k % 4, :], ACT.Exp,
                                           bias=sink_r[:, h["sink"]:h["sink"] + 1])
                        act.activation(pb[:, 128:384], bank[:, 128:384], ACT.Exp, bias=nb[:, k % 4, 1:2],
                                       scale=h["scale"], accum_out=sm[:, k % 4, 1:2]).then_inc(exp_done, 1)
                    if first <= k - 2 < last:
                        act.wait_ge(t_done, k - 1)
                        if k - 2 >= 2:
                            act.wait_ge(pv_done, k - 3)
                        act.activation(head(k - 2)["pp"][1], B[6][:, 0:384], ACT.Copy).then_inc(pt_done, 1)
                elif kind == "turn":
                    name, j = a
                    n["pair"] += 1
                    if j >= 2:
                        act.wait_ge(pair_ready, n["pair"] - 2)
                    elif j == 0:
                        act.wait_ge(pair_ready, n["pair"] - 1)
                        act.wait_ge(roped, n["rope"])
                    act.wait_ge(pair_turned, n["pair"] - 4)
                    at = STAGE[name][j % 2]
                    act.activation(A[:, at:at + 512], B[j][:, :], ACT.Copy).then_inc(pair_f, 1)
                elif kind == "rows":
                    act.wait_ge(pair_turned, n["pair"] - 4)
                    if n["x"]:
                        act.wait_ge(x_ready, TT * n["x"])
                    layer, j = a
                    act.dma_start(rows[:, 0, :], ln_g[layer, j].partition_broadcast(P)).then_inc(ld_row, 16)
                    act.dma_start(rows[:, 1, :], ln_b[layer, j].partition_broadcast(P)).then_inc(ld_row, 16)
                elif kind == "final_row":
                    act.wait_ge(pair_turned, n["pair"] - 4)
                    act.dma_start(rows[:, 0, :], final_norm.partition_broadcast(P)).then_inc(ld_fn, 16)
                elif kind == "down":
                    ahead(a[0])
                elif kind == "bound":
                    b, what, last_unit, scales, second, _ = a
                    rms = b >= 4
                    if what == "lnrms":
                        for t in range(TT):
                            normalise(t, False)
                        rms = True
                    act.wait_ge(pair_ready, n["pair"])
                    for t in range(TT):
                        normalise(t, rms)
                        if what != "final":
                            if t == 0 and b < 3:
                                act.wait_ge(col_ready, b + 2)
                            for j in range(2):
                                turned(2 * t + j, 2 * t + j, *scales)
                            ahead(last_unit - 1 + t)
                    SECOND = second
                    if a[0] < 4:
                        n["x"] += 1
                elif kind == "mlp":
                    mlp(a[0], a[1], a[2])
                elif kind == "hg_start":
                    act.wait_ge(pair_ready, n["pair"])
                    act.dma_start(A[:, H_E:H_E + LEVELS * P], consts[:, 4 * P:]).then_inc(ld_level, 16)
                    act.dma_start(gn_r, g_norm.partition_broadcast(P)).then_inc(ld_gn, 16)
                    act.dma_start(cosT[:, :], rope_2[:, 0, :]).then_inc(ld_rope2, 16)
                    act.dma_start(sinT[:, :], rope_2[:, 1, :]).then_inc(ld_rope2, 16)
                    act.wait_ge(lb_in, 1)
                    act.activation(tmp_c[:, 2, :], tmp_c[:, 0, :], ACT.Exp)
                    act.activation(tmp_c[:, 3, :], tmp_c[:, 1, :], ACT.Exp).then_inc(lb_exp, 1)
                elif kind == "level" and a[0] == LEVELS:
                    for g in range(2):
                        act.wait_ge(lv_ps, 2 * LEVELS + g + 1)
                        act.activation(A[:, H_S01 + 512 * g:H_S01 + 512 * g + 512], B[4 + 2 * g][:, :],
                                       ACT.Copy).then_inc(s01_done, 1)
                elif kind == "hg_out":
                    o = A[:, H_K:H_K + 2048].rearrange("p (h t v) -> p h t v", h=HG_HEADS, t=TT)
                    for t in range(TT):
                        act.wait_ge(ho_ps, t + 1)
                        for h in range(2):
                            act.activation(o[:, 4 * h:4 * h + 4, t, :], B[4 + 2 * t + h][:, :].rearrange(
                                "p (h v) -> p h v", h=4), ACT.Copy).then_inc(ho_read, 1)

        @block.vector
        def _(v):
            n = dict(step=0, plain=0, rope=0, pair=0, e=0, row=0, n=0, gates=0, x=0, y=0, u={})

            def link(ins):
                n["step"] += 1
                ins.then_inc(v_step, 1)
                v.wait_ge(v_step, n["step"])

            def inverse_root(c0, w):
                c = slice(c0, c0 + w)
                y, t_, v_ = nw[:, 0, c], nw[:, 1, c], ve[:, c]
                i32 = mybir.dt.int32
                link(v.tensor_scalar(y.bitcast(i32), v_.bitcast(i32), -0.5, GUESS, ALU.mult, ALU.add))
                k = 1.0
                for _ in range(3):
                    if w == 1:
                        link(v.scalar_tensor_tensor(out=t_, in0=y, scalar=v_, in1=y, op0=ALU.mult, op1=ALU.mult))
                    else:
                        link(v.tensor_tensor(t_, y, v_, ALU.mult))
                        link(v.tensor_tensor(t_, t_, y, ALU.mult))
                    link(v.scalar_tensor_tensor(out=y, in0=t_, scalar=-3.0 * k * k, in1=y, op0=ALU.add, op1=ALU.mult))
                    k *= -2.0 * k * k
                return v.tensor_scalar(rstd[:, c], y, 1.0 / k, None, ALU.mult)

            def variance(t, rms):
                if rms:
                    link(v.scalar_tensor_tensor(out=ve[:, t:t + 1], in0=mv[:, t, 0:1], scalar=mv[:, t, 0:1],
                                                in1=mv[:, t, 1:2], op0=ALU.mult, op1=ALU.add))
                    link(v.tensor_scalar(ve[:, t:t + 1], ve[:, t:t + 1], RMS_EPS, None, ALU.add))
                else:
                    link(v.tensor_scalar(ve[:, t:t + 1], mv[:, t, 1:2], LN_EPS, None, ALU.add))

            def row_root(t, rms):
                link(v.bn_aggr(mv[:, t, :], bn[:, t, :, :]))
                variance(t, rms)
                ins = inverse_root(t, 1)
                if not rms:
                    link(ins)
                    ins = v.scalar_tensor_tensor(out=nmr[:, t:t + 1], in0=mv[:, t, 0:1], scalar=-1.0,
                                                 in1=rstd[:, t:t + 1], op0=ALU.mult, op1=ALU.mult)
                ins.then_inc(rstd_ready, 1)

            def split(f, hi, lo):
                n["pair"] += 1
                v.wait_ge(pair_f, n["pair"])
                link(v.tensor_copy(hi, f))
                v.tensor_tensor(lo, f, hi, ALU.subtract).then_inc(pair_ready, 1)

            def split_tile(t, hi, lo):
                for j in range(2):
                    c = slice(4 * j, 4 * j + 4)
                    split(hTf[:, c, P * t:P * t + P], hi[:, c, P * t:P * t + P], lo[:, c, P * t:P * t + P])

            def ada(s, k, part):
                c = slice(D * part, D * part + D)
                if s == 0 and part == 0:
                    v.wait_ge(ld_start[k % START_BUFS], 16 * (k // START_BUFS + 1))
                if s:
                    v.wait_ge(ld_adas[part], 16 * (KT * (s - 1) + k + 1))
                if k == 0:
                    v.wait_ge(ld_bias, 16 * (s + 2))
                else:
                    v.wait_ge(ada_used, adas_before(s, k - 1, part + 1))
                w = ada_part(part) if s else START_BUF(A, k)[:, c]
                v.scalar_tensor_tensor(out=ada_acc[:, c], in0=w, scalar=silu_c[:, k:k + 1], in1=ada_acc[:, c],
                                       op0=ALU.mult, op1=ALU.add).then_inc(ada_used, 1)

            def mlp(m, u0, s_ada):
                p0, st = n["plain"], n["step"]

                def square(k, kp, step, u_free):
                    v.wait_ge(fill_read, k + (p0 + 1))
                    v.tensor_tensor(u_f[:, kp, :], u_f[:, kp, :], u_f[:, kp, :], ALU.mult).then_inc(v_step, 1)
                    v.wait_ge(v_step, step + 1)
                    if u_free is not None:
                        v.wait_ge(unit_done, u_free + 1)
                    v.tensor_copy(u_hi[kp], two(u_f[:, kp, :])).then_inc(v_step, 1)
                    v.wait_ge(v_step, step + 2)
                    v.tensor_tensor(u_lo[kp], two(u_f[:, kp, :]), u_hi[kp], ALU.subtract).then_inc(u_ready, 1)

                square(0, 0, st, None)
                square(1, 1, st + 2, None)
                if s_ada:
                    zero_acc()
                    v.wait_ge(ld_bias, 16 * (s_ada + 2))
                with v.Fori(0, LOOPS) as i:
                    for j in range(2):
                        square(2 * i + (2 + j), j, 4 * i + (st + 4 + 2 * j), 4 * i + D_unit(u0, j))
                        if s_ada and j == 0:
                            for part in range(3):
                                c = slice(D * part, D * part + D)
                                v.wait_ge(ld_adas[part], 16 * i + 16 * (KT * (s_ada - 1) + 1))
                                v.wait_ge(ada_used, 3 * i + adas_before(s_ada))
                                v.scalar_tensor_tensor(out=ada_acc[:, c], in0=ada_part(part),
                                                       scalar=silu_c[:, bass.ds(i, 1)], in1=ada_acc[:, c],
                                                       op0=ALU.mult, op1=ALU.add).then_inc(ada_used, 1)
                st += 4 + 4 * LOOPS
                for k in (PAIRS - 2, PAIRS - 1):
                    square(k, k % 2, st, D_unit(u0, k - 2))
                    st += 2
                    if s_ada:
                        for part in range(3):
                            ada(s_ada, KT - PAIRS + k, part)
                n["step"], n["plain"] = st, p0 + PAIRS

            def zero_acc():
                v.memset(ada_acc, 0.0).then_inc(acc_zero, 1)

            v.memset(gate_r, 0.0)
            zero_acc()
            v.memset(zero8[:, :], 0.0)
            link(v.memset(ones[:, :], 1.0))
            v.wait_ge(ld_const, 16)
            cst = arena(START_CONSTS, 4, P)
            for i, dst in ((0, ident), (1, perm), (0, ident_b), (2, causal_b), (3, band_b)):
                ins = v.tensor_copy(dst[:, :], cst[:, i, :])
            ins.then_inc(consts_ready, 1)
            v.wait_ge(ld_pos, 32)
            p_f, ang, cs = arena(HTF + 256, SEQ), arena(HTF + 1024, SEQ), arena(HTF + 1280, SEQ)
            link(v.tensor_copy(p_f, A[:, HTF:HTF + 256].bitcast(mybir.dt.int32)))
            link(v.tensor_scalar(ang, p_f, rc[:, 0:1], None, ALU.mult))
            for at, quarter in ((512, 0.0), (768, 0.25)):
                r = A[:, HTF + at:HTF + at + SEQ]
                link(v.tensor_scalar(cs, ang, 1.0 / TWO_PI, quarter, ALU.mult, ALU.add))
                link(v.tensor_scalar(cs, cs, ROUNDER, None, ALU.add))
                link(v.tensor_scalar(cs, cs, ROUNDER, None, ALU.subtract))
                link(v.tensor_copy(r, ang))
                for part in TWO_PI_PARTS:
                    link(v.scalar_tensor_tensor(out=r, in0=cs, scalar=-part, in1=r, op0=ALU.mult, op1=ALU.add))
                if quarter:
                    link(v.tensor_scalar(r, r, TWO_PI / 4, None, ALU.add))
                link(v.tensor_scalar(r, r, PI_BELOW, -PI_BELOW, ALU.min, ALU.max))
            r = A[:, HTF + 512:HTF + 768]
            v.tensor_scalar(r, r, rc[:, 1:2], None, ALU.mult).then_inc(ang_ready, 1)
            v.wait_ge(c_exp, 1)
            link(v.tensor_scalar(tmp_c[:, 0, :], silu_c[:, :], 1.0, None, ALU.add))
            link(v.reciprocal(tmp_c[:, 1, :], tmp_c[:, 0, :]))
            link(v.tensor_tensor(silu_c[:, :], tmp_c[:, 1, :], vec[:, 0:KT], ALU.mult))
            for k in range(KT):
                for part in range(2):
                    ada(0, k, part)

            def finish(s):
                v.wait_ge(ada_col, s + 1)
                shift, sc1 = B[3][:, 0:KT], B[3][:, KT:2 * KT]
                if s == 0:
                    link(v.tensor_scalar(sc_c[:, :], sc1, 1.0, None, ALU.add))
                    v.tensor_copy(bi_c[:, :], shift).then_inc(col_ready, 1)
                else:
                    g = vec[:, COL["ln_g"] + KT * (s - 1):COL["ln_g"] + KT * s]
                    b = vec[:, COL["ln_b"] + KT * (s - 1):COL["ln_b"] + KT * s]
                    link(v.tensor_scalar(tmp_c[:, 0, :], sc1, 1.0, None, ALU.add))
                    link(v.tensor_tensor(sc_c[:, :], tmp_c[:, 0, :], g, ALU.mult))
                    link(v.tensor_tensor(tmp_c[:, 1, :], tmp_c[:, 0, :], b, ALU.mult))
                    v.tensor_tensor(bi_c[:, :], tmp_c[:, 1, :], shift, ALU.add).then_inc(col_ready, 1)

            for step in STEPS:
                kind, a = step[0], step[1:]
                if kind == "finish":
                    if a[0] == 0:
                        finish(0)
                        for j in range(4):
                            c = slice(2 * j, 2 * j + 2)
                            split(hTf[:, c, :], hT_hi[:, c, :], hT_lo[:, c, :])
                elif kind == "gate_sum":
                    v.wait_ge(ld_gate, 16 * len(gate_bufs))
                    for k in range(KT):
                        v.scalar_tensor_tensor(out=gate_r, in0=gate_w[k], scalar=silu_c[:, k:k + 1], in1=gate_r,
                                               op0=ALU.mult, op1=ALU.add).then_inc(gate_used, 1)
                        v.wait_ge(gate_used, k + 1)
                elif kind in ("gate", "gate0"):
                    n["gates"] += 1
                    v.wait_ge(gate_ps, n["gates"])
                    if n["gates"] in (1, 3):
                        zero_acc()
                elif kind == "fill":
                    u, part, parts, form, src, reader, dst = a
                    n["plain"] += reader == "plain"
                    if reader == "plain":
                        n["u"][u] = n["plain"]
                    if reader in ("silu", "forget", "gate"):
                        i = n["e"]
                        e = A[:, H_E + 512 * (i % 2):][:, 0:512]
                        n["e"] += 1
                        v.wait_ge(e_done, n["e"])
                        link(v.tensor_scalar(e, e, 1.0, None, ALU.add))
                        link(v.reciprocal(e, e))
                        if reader == "silu":
                            v.tensor_tensor(dst, dst, e, ALU.mult).then_inc(silu_done, 1)
                        elif reader == "gate":
                            link(v.tensor_tensor(dst, dst, two(e), ALU.mult))
                            if i == 8:
                                v.wait_ge(ld_gn, 16)
                            g4 = dst.rearrange("p t (h v) -> p t h v", v=P)
                            gb = gn_r.unsqueeze(1).unsqueeze(1).to_broadcast([P, TT, 2, P])
                            v.tensor_tensor(g4, g4, gb, ALU.mult).then_inc(silu_done, 1)
                        else:
                            f, k = A[:, H_F + 512 * dst:][:, 0:512], A[:, H_K + 512 * dst:][:, 0:512]
                            for q in range(2):
                                c, m = slice(256 * q, 256 * q + 256), 2 * dst + q
                                link(v.tensor_scalar(f[:, c], e[:, c], lb_c[:, 1, m:m + 1], lb_c[:, 0, m:m + 1],
                                                     ALU.mult, ALU.add))
                            v.tensor_scalar(k, f, -1.0, 1.0, ALU.mult, ALU.add).then_inc(silu_done, 1)
                elif kind == "rope":
                    tmp, turned_at, dst, w = a
                    r = n["rope"]
                    n["rope"] += 1
                    v.wait_ge(turn_f, r + 1)
                    if w == 256:
                        v.wait_ge(ld_rope2, 32)
                    def shape(x_):
                        return two(x_) if w == 512 else x_
                    cos, sin = ((cosT[:, :].unsqueeze(1).to_broadcast([P, 2, SEQ]),
                                 sinT[:, :].unsqueeze(1).to_broadcast([P, 2, SEQ])) if w == 512 else
                                (cosT[:, :], sinT[:, :]))
                    tmp += 512 * (r % 2)
                    d, f, tb = A[:, dst:dst + w], A[:, tmp:tmp + w], A[:, turned_at:turned_at + w]
                    v.wait_ge(pair_ready, n["pair"])
                    link(v.tensor_tensor(shape(d), shape(f), cos, ALU.mult))
                    v.wait_ge(turn_ps, r + 1)
                    link(v.tensor_tensor(shape(tb), shape(B[2][:, 0:w]), sin, ALU.mult))
                    v.tensor_tensor(d, d, tb, ALU.add).then_inc(roped, 1)
                elif kind == "ada":
                    ada(a[0], a[1], a[2])
                elif kind == "norm2":
                    c = two(a[0])
                    v.wait_ge(fill_read, n["u"][a[1]])
                    for t in range(TT):
                        link(v.bn_stats(bn[:, t, 0, :], c[:, t, :]))
                        link(v.bn_aggr(mv[:, t, :], bn[:, t, 0:1, :]))
                        variance(t, True)
                    link(inverse_root(0, 2))
                    link(v.tensor_scalar(c[:, 0, :], c[:, 0, :], rstd[:, 0:1], None, ALU.mult))
                    v.tensor_scalar(c[:, 1, :], c[:, 1, :], rstd[:, 1:2], None, ALU.mult).then_inc(o_ready, 1)
                elif kind == "turn2":
                    if a[3]:
                        v.wait_ge(unit_done, a[3])
                    split(cT_f, *C_T[a[2]])
                elif kind == "second":
                    split_tile(a[0], R_hi, R_lo)
                elif kind == "index":
                    h = a[0]
                    v.wait_ge(ix_relu, h + 1)
                    if h == 0:
                        for t in range(TT):
                            link(v.tensor_scalar(iw[:, t, :], A[:, AB_TOK + 256 * t + 192:][:, 0:IDX_HEADS],
                                                 IDX_HEADS ** -0.5 * HD ** -0.5, None, ALU.mult))
                    for t in range(TT):
                        c = slice(128 * t, 128 + 256 * t)
                        r = A[:, AB_IX + 384 * (h % 2):][:, 0:384][:, c]
                        if h == 0:
                            ins = v.tensor_scalar(score[:, c], r, iw[:, t, h:h + 1], None, ALU.mult)
                        else:
                            ins = v.scalar_tensor_tensor(out=score[:, c], in0=r, scalar=iw[:, t, h:h + 1],
                                                         in1=score[:, c], op0=ALU.mult, op1=ALU.add)
                        if t == 0:
                            link(ins)
                    ins.then_inc(ix_used, 1)
                    v.wait_ge(ix_used, h + 1)
                    if h == IDX_HEADS - 1:
                        for t in range(TT):
                            c = slice(256 * t, 256 * t + P)
                            link(v.tensor_tensor(score[:, c], score[:, c], causal_b[:, :], ALU.add))
                elif kind == "topk":
                    for t in range(TT):
                        c = slice(128 * t, 128 + 256 * t)
                        link(v.max(m8[:, t, :], score[:, c]))
                        link(v.match_replace(score[:, c], m8[:, t, :], score[:, c], TAKEN))
                elif kind == "chosen":
                    link(v.tensor_scalar(chosen_b[:, :], score, TAKEN / 2, NEG, ALU.is_gt, ALU.mult))
                    for t in range(TT):
                        c = slice(256 * t, 256 * t + P)
                        ins = v.tensor_tensor(chosen_b[:, c], chosen_b[:, c], causal_b[:, :], ALU.min)
                        if t == 0:
                            link(ins)
                    ins.then_inc(chosen, 1)
                elif kind == "head":
                    k, first, last = a
                    if k < last:
                        v.wait_ge(s_done, k + 1)
                        h, bank = head(k), B[4 + k % 2]
                        v.reduce_max(mx[:, k % 4, 0:1], bank[:, 0:128], AX.X)
                        link(v.reduce_max(mx[:, k % 4, 1:2], bank[:, 128:384], AX.X))
                        if h["sink"] is not None:
                            link(v.tensor_scalar(mx[:, k % 4, :], mx[:, k % 4, :], h["scale"], None, ALU.mult))
                            link(v.tensor_scalar(mx[:, k % 4, :], mx[:, k % 4, :], sink_r[:, k:k + 1], None, ALU.max))
                            v.tensor_scalar(nb[:, k % 4, :], mx[:, k % 4, :], -1.0, None,
                                            ALU.mult).then_inc(max_done, 1)
                        else:
                            v.tensor_scalar(nb[:, k % 4, :], mx[:, k % 4, :], -h["scale"], None,
                                            ALU.mult).then_inc(max_done, 1)
                    if first <= k - 3 < last:
                        j = k - 3
                        h, q = head(j), j % 4
                        v.wait_ge(pv_done, j + 1)
                        if h["sink"] is not None:
                            link(v.tensor_tensor(sm[:, q, :], sm[:, q, :], sk[:, q, :], ALU.add))
                        link(v.reciprocal(ri[:, q, :], sm[:, q, :]))
                        dv, oc = h["dv"], h["oc"]
                        v.tensor_scalar(h["o"][:, oc:oc + dv], B[7][:, 0:dv], ri[:, q, 0:1], None, ALU.mult)
                        v.tensor_scalar(h["o"][:, P + oc:P + oc + dv], B[7][:, dv:2 * dv], ri[:, q, 1:2], None,
                                        ALU.mult).then_inc(o_done, 1)
                elif kind == "turn":
                    name, j = a
                    at, c = STAGE[name][j % 2], slice(2 * j, 2 * j + 2)
                    split(two(A[:, at:at + 512]), *(t_[:, c, :] for t_ in TURN_TO[name]))
                elif kind == "bound":
                    b, what, last_unit, _, second, _ = a
                    if b == 0:
                        v.wait_ge(ld_x, 16)

                    def residual(t):
                        for h in range(2):
                            if (t, h) == (1, 1):
                                v.wait_ge(unit_done, last_unit + 1)
                            else:
                                v.wait_ge(y_done, 3 * b + 2 * t + h + 1)
                            y, c = B[4 + 2 * t + h], slice(512 * h, 512 * h + 512)
                            if b < 4:
                                ins = v.tensor_tensor(N[:, t, c], y[:, :], gate_r[:, c], ALU.mult)
                            else:
                                ins = v.tensor_tensor(X[:, t, c], y[:, :], X[:, t, c], ALU.add)
                            ins.then_inc(y_read, 1)
                            n["y"] += 1
                            v.wait_ge(y_read, n["y"])
                            if b < 4:
                                link(v.scalar_tensor_tensor(out=X[:, t, c], in0=X[:, t, c], scalar=ALPHA, in1=N[:, t, c],
                                                            op0=ALU.mult, op1=ALU.add))
                            link(v.bn_stats(bn[:, t, h, :], X[:, t, c]))

                    def affine(t):
                        if t == 0:
                            n["row"] += 1
                            v.wait_ge(ld_row, 32 * n["row"])
                        link(v.tensor_tensor(X[:, t, :], N[:, t, :], rows[:, 0, :], ALU.mult))
                        v.tensor_tensor(X[:, t, :], X[:, t, :], rows[:, 1, :], ALU.add).then_inc(x_ready, 1)
                        n["x"] += 1
                        v.wait_ge(x_ready, n["x"])

                    def normalised():
                        n["n"] += 1
                        v.wait_ge(n_ready, n["n"])

                    for t in range(TT):
                        residual(t)
                        row_root(t, b >= 4)
                        if t == 0 and b < 3:
                            finish(b + 1)
                        if t == 1 and what in ("ln", "rms"):
                            split_tile(0, hT_hi, hT_lo)
                    if what == "lnrms":
                        for t in range(TT):
                            normalised()
                            affine(t)
                            for h in range(2):
                                link(v.bn_stats(bn[:, t, h, :], X[:, t, 512 * h:512 * h + 512]))
                            row_root(t, True)
                        split_tile(0, hT_hi, hT_lo)
                    if what == "final":
                        v.wait_ge(ld_fn, 16)
                        for t in range(TT):
                            normalised()
                            v.tensor_tensor(N[:, t, :], N[:, t, :], rows[:, 0, :], ALU.mult).then_inc(out_ready, 1)
                    else:
                        split_tile(1, hT_hi, hT_lo)
                    if what == "ln":
                        for t in range(TT):
                            normalised()
                            affine(t)
                    elif what != "final":
                        n["n"] += TT
                elif kind == "mlp":
                    mlp(a[0], a[1], a[2])
                elif kind == "hg_start":
                    v.wait_ge(ld_level, 16)
                    link(v.tensor_copy(level_m[:, :, :], arena(H_E, LEVELS, P)))
                    l0, l1 = vec[:, COL["lb"]:COL["lb"] + KT], vec[:, COL["lb"] + KT:COL["lb"] + 2 * KT]
                    link(v.tensor_tensor(tmp_c[:, 2, :], l0, l1, ALU.max))
                    link(v.tensor_tensor(tmp_c[:, 0, :], l0, tmp_c[:, 2, :], ALU.subtract))
                    v.tensor_tensor(tmp_c[:, 1, :], l1, tmp_c[:, 2, :], ALU.subtract).then_inc(lb_in, 1)
                    v.wait_ge(lb_exp, 1)
                    link(v.tensor_tensor(tmp_c[:, 0, :], tmp_c[:, 2, :], tmp_c[:, 3, :], ALU.add))
                    link(v.reciprocal(tmp_c[:, 1, :], tmp_c[:, 0, :]))
                    link(v.tensor_tensor(lb_c[:, 0, :], tmp_c[:, 2, :], tmp_c[:, 1, :], ALU.mult))
                    link(v.tensor_scalar(lb_c[:, 1, :], lb_c[:, 0, :], -1.0, 1.0, ALU.mult, ALU.add))
                elif kind == "level":
                    l = a[0]
                    if l == 0:
                        link(v.memset(A[:, H_ST:H_ST + 2048], 0.0))
                    if l == LEVELS:
                        continue
                    W = 4 * SEQ
                    for g in range(2):
                        v.wait_ge(lv_ps, 2 * l + g + 1)
                        for i in range(2):
                            st = A[:, H_ST + 1024 * g + 512 * i:][:, 0:512].rearrange("p (a b) -> p a b", b=P)
                            ps = B[4 + 2 * g + i][:, :].rearrange("p (a b) -> p a b", b=P)
                            link(v.copy_predicated(st, level_m[:, l, :].unsqueeze(1).to_broadcast([P, 4, P]), ps))
                        q, k = A[:, H_Q + W * g:][:, 0:W], A[:, H_K + W * g:][:, 0:W]
                        if l == 0:
                            v.tensor_tensor(q, q, A[:, H_F + W * g:][:, 0:W], ALU.mult).then_inc(lv_used, 1)
                            v.wait_ge(lv_used, g + 1)
                            continue
                        w = 1 << (l - 1)
                        nbk = W // (2 * w)
                        ends = (A[:, H_F + W * g:][:, 0:W] if l == 1 else
                                A[:, H_TMP + (W if l % 2 else 0) + W // 2 * g:][:, 0:W // w])
                        e2 = ends.rearrange("p (n s) -> p n s", s=2)
                        q2 = q.rearrange("p (n s w) -> p n s w", s=2, w=w)
                        k2 = k.rearrange("p (n s w) -> p n s w", s=2, w=w)
                        eb = [e2[:, :, s:s + 1].to_broadcast([P, nbk, w]) for s in range(2)]
                        link(v.tensor_tensor(q2[:, :, 1, :], q2[:, :, 1, :], eb[0], ALU.mult))
                        nxt = A[:, H_TMP + (0 if l % 2 else W) + W // 2 * g:][:, 0:nbk]
                        link(v.tensor_tensor(nxt, e2[:, :, 0], e2[:, :, 1], ALU.mult))
                        v.tensor_tensor(k2[:, :, 0, :], k2[:, :, 0, :], eb[1], ALU.mult).then_inc(lv_used, 1)
                        v.wait_ge(lv_used, 2 * l + g + 1)
                elif kind == "hg_out":
                    o = A[:, H_K:H_K + 2048].rearrange("p (h t v) -> p h t v", h=HG_HEADS, t=TT)
                    gate = arena(H_G, TT, D)
                    v.wait_ge(ho_read, 4)
                    sq = A[:, H_F:H_F + 1024].rearrange("p (h v) -> p h v", h=HG_HEADS)
                    for t in range(TT):
                        link(v.tensor_tensor(sq, o[:, :, t, :], o[:, :, t, :], ALU.mult))
                        link(v.reduce_sum(ve[:, 8 * t:8 * t + 8], sq, AX.X))
                    link(v.tensor_scalar(ve[:, :], ve[:, :], 1.0 / P, RMS_EPS, ALU.mult, ALU.add))
                    link(inverse_root(0, 16))
                    for t in range(TT):
                        rb = rstd[:, 8 * t:8 * t + 8].unsqueeze(2).to_broadcast([P, HG_HEADS, P])
                        link(v.tensor_tensor(o[:, :, t, :], o[:, :, t, :], rb, ALU.mult))
                        ins = v.tensor_tensor(o[:, :, t, :], o[:, :, t, :],
                                              gate[:, t, :].rearrange("p (h v) -> p h v", h=HG_HEADS), ALU.mult)
                        if t == 0:
                            link(ins)
                    ins.then_inc(o_ready, 1)


def kernel(**inputs):
    import numpy as np
    import concourse.bacc as bacc
    from concourse.bass_utils import run_bass_kernel_spmd as run

    g = {k: np.asarray(a) for k, a in inputs.items()}

    def wide(w):
        return w.reshape(KT, P, -1, 256).transpose(2, 1, 0, 3).reshape(-1, P, UNIT)

    def tall(w):
        return w.reshape(-1, 2, P, D).transpose(0, 2, 1, 3).reshape(-1, P, UNIT)

    def rank(w):
        return w.reshape(2, P, -1, D).transpose(2, 1, 0, 3).reshape(-1, P, UNIT)

    def mlp(w1, w2):
        up, dn = wide(w1), tall(w2)
        order = [up[0]]
        for k in range(1, PAIRS):
            order += [up[k], dn[k - 1]]
        return np.stack(order + [dn[PAIRS - 1]])

    z = lambda k: np.zeros((D, k), np.float32)
    ab = g["ab_w_in"][0]
    aq, ak, av, cq, bk, bv, bik, biw = np.split(ab, np.cumsum([512, 128, 128, RANK, HD, HD, HD]), axis=1)
    kt = np.concatenate([ak[:, :64], ak[:, :64], ak[:, 64:], ak[:, 64:], bk, bk, bik, bik], axis=1)
    c_in = g["c_w_in"][0]
    cqkv = [wide(c_in[:, D * i:D * (i + 1)]) for i in range(3)]
    dkv = g["kv_w_dkv_2"]
    uq = g["mla_w_uq_2"][0].reshape(RANK, MLA_HEADS, NOPE + ROPE)
    hg_i = wide(g["hgrn_w_i_2"][0])
    uk, uv, uqn = rank(g["kv_w_uk_2"]), rank(g["kv_w_uv_2"]), rank(uq[:, :, :NOPE].reshape(RANK, -1))
    stream = np.concatenate([
        wide(cq), wide(np.concatenate([av, bv, biw, z(56)], axis=1)), wide(kt),
        rank(np.concatenate([g["ab_w_uiq"][0], g["ab_w_uq"][0]], axis=1)), wide(aq), tall(g["ab_w_out"][0]),
        mlp(g["mlp_w1"][0], g["mlp_w2"][0]),
        cqkv[2], np.stack([cqkv[i][j] for j in range(4) for i in range(2)]), tall(g["c_w_out"][0]),
        mlp(g["mlp_w1"][1], g["mlp_w2"][1]),
        hg_i[:2], wide(g["hgrn_w_q_2"][0]), wide(g["hgrn_w_f_2"][0]), hg_i[2:], wide(g["hgrn_w_g_2"][0]),
        tall(g["hgrn_w_o_2"][0]),
        mlp(g["mlp_w_up_2"][0], g["mlp_w_down_2"][0]),
        wide(dkv[:, :RANK]), wide(np.concatenate([dkv[:, RANK:], dkv[:, RANK:], z(P)], axis=1)),
        wide(g["mla_w_dq_2"][0]), uk[:1], rank(uq[:, :, NOPE:].reshape(RANK, -1)), uv[:1], uqn[:1], uk[1:], uv[1:], uqn[1:],
        tall(g["mla_w_o_2"][0]),
        mlp(g["mlp_w_up_2"][1], g["mlp_w_down_2"][1]),
    ])
    assert stream.shape == (UNITS, P, UNIT)

    def columns(a):
        return np.asarray(a).reshape(-1, P).T

    cols = np.concatenate([columns(g[k]) for k in (
        "c", "ln_g", "ln_b", "ab_q_norm", "hgrn_norm_2", "mla_norm_2", "mla_q_norm_2", "kv_in_norm_2", "kv_norm_2",
        "mlp_norm_2", "hgrn_lb_logits_2")], axis=1)

    i, j = np.arange(P)[:, None], np.arange(P)[None, :]
    consts = [i == j, (i // 64 == j // 64) & ((i % 64 + 32) % 64 == j % 64)]
    consts = [m.astype(np.float32) for m in consts]
    consts += [np.where(j <= i, 0.0, NEG).astype(np.float32), np.where(j > i, 0.0, NEG).astype(np.float32)]
    consts.append((i == j).astype(np.float32))
    for l in range(1, LEVELS):
        w = 1 << (l - 1)
        consts.append(((i // (2 * w) == j // (2 * w)) & (i // w % 2 == 0) & (j // w % 2 == 1)).astype(np.float32))
    consts = np.stack(consts, axis=1).reshape(P, N_CONST * P)
    inv = (np.float32(10000.0) ** (-np.arange(0, HD, 2, dtype=np.float32) / np.float32(HD))).astype(np.float32)
    inv_col, sign = inv[np.arange(P) % 32], np.where(np.arange(P) % 64 < 32, -1.0, 1.0).astype(np.float32)
    angle = np.arange(SEQ, dtype=np.float32)[None, :] * inv_col[:, None]
    arrays = {
        "stream": stream,
        "ada_w": g["ada_w"].reshape(4, KT, P, 3 * D),
        "ada_b": g["ada_b"].reshape(4, 3 * D),
        "x": g["x"][0],
        "x_t": g["x"][0].T,
        "pos": g["positions"].reshape(SEQ),
        "cols": cols,
        "ln_g": g["ln_g"],
        "ln_b": g["ln_b"],
        "sinks": g["ab_sinks"][0],
        "g_norm": g["hgrn_g_norm_2"][0],
        "final_norm": g["final_norm_2"],
        "consts": consts,
        "rope_cols": np.stack([inv_col, sign], axis=1),
        "rope_2": np.stack([np.cos(angle), np.sin(angle) * sign[:, None]], axis=1).astype(np.float32),
    }
    nc = bacc.Bacc("TRN2", target_bir_lowering=False, num_devices=1)
    args = []
    for name in arrays:
        arrays[name] = np.ascontiguousarray(arrays[name])
        args.append(nc.dram_tensor(name, arrays[name].shape, mybir.dt.from_np(arrays[name].dtype),
                                   kind="ExternalInput").ap())
    args.append(nc.dram_tensor("out", (SEQ, D), mybir.dt.float32, kind="ExternalOutput").ap())
    two_block_kernel(nc, *args)
    r = run(nc, [arrays], core_ids=[0])
    return r.results[0]["out"].reshape(1, SEQ, D)
```

```python
import math

import concourse.bass as bass
from concourse import mybir
from contextlib import ExitStack

D = 1024
SEQ = 256
P = 128
TT = SEQ // P
KT = D // P
HD = 64
D_FF = 4 * D
HEADS_A, KV_A, HEADS_B, HEADS_C = 8, 2, 8, 16
TOPK = min(256, SEQ // 4)
IDX_HEADS = 8
HG_HEADS = 8
MLA_HEADS, NOPE, ROPE = 16, 128, 64
RANK = 256
ALPHA = (2 * 2) ** 0.25
LN_EPS, RMS_EPS = 1e-5, 1e-6
NEG = -1.0e30
TAKEN = -3.0e38

UNIT = 2048
SLOTS = 4
AB = 0
M0 = AB + 11
CU = M0 + 32
M1 = CU + 16
HG = M1 + 32
M2 = HG + 20
ML = M2 + 32
M3 = ML + 18
UNITS = M3 + 32
PAIRS = D_FF // 256

COL = {}
_at = 0
for _name, _n in (("c", 8), ("ln_g", 32), ("ln_b", 32), ("ab_q", 2), ("hgrn", 8), ("mla", 8), ("mla_q", 2),
                  ("kv_in", 8), ("kv", 2), ("mlp", 16), ("lb", 16)):
    COL[_name] = _at
    _at += _n
NCOLS = _at

LEVELS = 8
BARE_LEVELS = (6, 7)
N_CONST = 4 + LEVELS
TWO_PI = 6.283185307179586
PI_BELOW = 3.1415925
GUESS = 1597463007.0
ROUNDER = 1.5 * 2.0 ** 23


def _parts(x, bits, n):
    out = []
    for _ in range(n - 1):
        step = 2.0 ** (math.floor(math.log2(abs(x))) - bits + 1)
        out.append(math.floor(x / step) * step)
        x -= out[-1]
    return out + [x]


TWO_PI_PARTS = _parts(TWO_PI, 8, 4)

HTF = 0
ADAW = HTF + 2048
ADAC = ADAW + 3 * D
GATE = ADAC + 3 * D
SCR = GATE + D
ARENA = SCR + 7424


START_BUFS = 4


def START_BUF(A, k):
    at = (ADAW, SCR, SCR + 2 * D, SCR + 4 * D)[k % START_BUFS]
    return A[:, at:at + 2 * D]


def two_block_kernel(nc, stream, ada_w, ada_b, x, x_t, pos, cols, ln_g, ln_b, sinks, g_norm, final_norm,
                     consts, rope_cols, rope_2, out):
    f32, f32r, bf16 = mybir.dt.float32, mybir.dt.float32r, mybir.dt.bfloat16
    ALU = mybir.AluOpType
    ACT = mybir.ActivationFunctionType
    AX = mybir.AxisListType
    ctx = ExitStack()
    with ctx:
        def sb(name, shape, dt=f32):
            return ctx.enter_context(nc.sbuf_tensor(name, shape, dt))

        def sem(name):
            return ctx.enter_context(nc.semaphore(name))

        raw = sb("raw", [P, SLOTS, UNIT])
        w_hi = sb("w_hi", [P, SLOTS, UNIT], f32r)
        w_lo = sb("w_lo", [P, SLOTS, UNIT], f32r)
        X = sb("X", [P, TT, D])
        hT_hi = sb("hT_hi", [P, KT, SEQ], f32r)
        hT_lo = sb("hT_lo", [P, KT, SEQ], f32r)
        R = sb("R", [P, 2, KT, SEQ], f32r)
        A = sb("A", [P, ARENA])
        ident = sb("ident", [P, P])
        perm = sb("perm", [P, P])
        ones = sb("ones", [P, P])
        ident_b = sb("ident_b", [P, P], bf16)
        causal_b = sb("causal_b", [P, P], bf16)
        band_b = sb("band_b", [P, P], bf16)
        level_m = sb("level_m", [P, LEVELS, P], mybir.dt.uint8)
        cosT = sb("cosT", [P, SEQ])
        sinT = sb("sinT", [P, SEQ])
        vec = sb("vec", [P, NCOLS])
        silu_c = sb("silu_c", [P, KT])
        zero8 = sb("zero8", [P, KT])
        sc_c = sb("sc_c", [P, KT])
        bi_c = sb("bi_c", [P, KT])
        tmp_c = sb("tmp_c", [P, 4, KT])
        rc = sb("rc", [P, 2])
        sink_r = sb("sink_r", [P, HEADS_A])
        lb_c = sb("lb_c", [P, 2, KT])
        bn = sb("bn", [P, TT, 2, 6])
        mv = sb("mv", [P, TT, 2])
        ve = sb("ve", [P, 16])
        nw = sb("nw", [P, 1, 16])
        ss = sb("ss", [P, TT, 2])
        nmr = sb("nmr", [P, TT])
        rstd = sb("rstd", [P, 16])
        mx, nb, sm, sk, ri = (sb(x_, [P, 4, 2]) for x_ in ("mx", "nb", "sm", "sk", "ri"))
        B = [ctx.enter_context(nc.psum_tensor(f"bank{i}", [P, 512], f32)) for i in range(8)]

        def arena(at, *shape):
            n = 1
            for s in shape:
                n *= s
            v = A[:, at:at + n]
            if len(shape) == 2:
                v = v.rearrange("p (a b) -> p a b", a=shape[0])
            return v

        def two(v):
            return v.rearrange("p (a b) -> p a b", a=2)

        hTf = arena(HTF, KT, SEQ)
        cT_f = arena(HTF + 1024, 2, SEQ)
        ada_acc, gate_r = arena(ADAC, 3 * D), arena(GATE, D)
        ANGLES = SCR + 6 * D
        START_CONSTS = HTF + 3 * 512
        gate_bufs = [((0, 2), X[:, :, :].rearrange("p t d -> p (t d)")), ((2, 5), arena(ADAW, 3 * D)),
                     ((5, 7), arena(SCR + 2 * D, 2 * D)), ((7, 8), arena(HTF, D))]
        gate_w = [buf[:, D * i:D * i + D] for (k0, k1), buf in gate_bufs for i in range(k1 - k0)]

        def ada_part(part):
            return arena(ADAW + D * part, D)

        def adas_before(s_, k=0, part=0):
            return (2 * KT + 3 * KT * (s_ - 1) if s_ else 0) + (3 if s_ else 2) * k + part

        N = arena(SCR, TT, D)
        rows = arena(SCR + 2048, 2, D)
        u_f = arena(SCR + 4096, 2, 512)
        R_hi, R_lo = R[:, 0], R[:, 1]
        u_hi = [R[:, 0, 2 * i:2 * i + 2, :] for i in range(2)]
        u_lo = [R[:, 1, 2 * i:2 * i + 2, :] for i in range(2)]

        AB_QK = SCR
        AB_TOK = SCR + 16 * 256
        AB_CQ = AB_TOK + 512
        AB_IX = AB_CQ
        AB_TMP = AB_IX + 768
        TURNED = HTF + 1536
        AB_SCORE = AB_TMP + 1024
        AB_MASK = AB_SCORE + 384
        C_V, C_QK = SCR, SCR + 2048
        C_TMP = C_QK + 4096
        H_Q, H_K, H_F, H_V, H_G, H_ST = 0, 2048, 4096, 6144, 8192, 10240
        H_S01 = H_ST + 2048
        H_TMP = H_S01 + 1024
        H_GN = H_TMP + 2048
        H_E = H_GN + P
        L_QN, L_KN, L_QR, L_KR, L_V = 2048, 6144, 10240, 12288, 12544
        L_C = {"ckv": L_V, "dq": L_V + 512}
        L_TMP = L_V + 1024
        L_TURNED = L_V + 2048
        assert max(L_V + 4096, H_E + 1024, C_TMP + 1024, AB_MASK + 224) <= ARENA
        score = A[:, AB_SCORE:AB_SCORE + 384]
        chosen_b = A[:, AB_MASK:AB_MASK + 192].bitcast(bf16)
        m8, iw = arena(AB_MASK + 192, 2, 8), arena(AB_MASK + 208, TT, IDX_HEADS)
        gn_r = A[:, H_GN:H_GN + P]

        def tile_at(base, j):
            return A[:, base + 256 * j:base + 256 * (j + 1)]

        raw_full = [sem(f"raw_full{i}") for i in range(SLOTS)]
        ld_start = [sem(f"ld_start{i}") for i in range(START_BUFS)]
        (hi_done, lo_done, unit_done, fill_done, fill_read, u_ready, v_step, y_done, y_read, rstd_ready,
         n_ready, pair_turned, pair_f, pair_ready, x_ready) = map(sem, (
            "hi_done", "lo_done", "unit_done", "fill_done", "fill_read", "u_ready", "v_step", "y_done", "y_read",
            "rstd_ready", "n_ready", "pair_turned", "pair_f", "pair_ready", "x_ready"))
        ld_adas = [sem(f"ld_ada{i}") for i in range(3)]
        (ld_const, ld_row, ld_gate, ld_level, ld_bias, ld_sink, ld_vec, ld_pos, ld_x, ld_xt, ld_gn, ld_rope2, ld_fn) = map(sem, (
            "ld_const", "ld_row", "ld_gate", "ld_level", "ld_bias", "ld_sink", "ld_vec", "ld_pos", "ld_x", "ld_xt", "ld_gn", "ld_rope2",
            "ld_fn"))
        (consts_ready, c_exp, ang_ready, trig_done, ada_used, gate_used, acc_zero, pool_zero, ada_col, col_ready, gate_ps, gate_read, turn_f,
         turn_ps, roped, s_done, max_done, exp_done, t_done, pt_done, pv_done, o_done) = map(sem, (
            "consts_ready", "c_exp", "ang_ready", "trig_done", "ada_used", "gate_used", "acc_zero", "pool_zero", "ada_col", "col_ready", "gate_ps",
            "gate_read", "turn_f", "turn_ps", "roped", "s_done", "max_done", "exp_done", "t_done", "pt_done", "pv_done",
            "o_done"))
        (ix_ps, ix_relu, ix_used, chosen, e_done, silu_done, lb_in, lb_exp, lv_ps, lv_used, s01_done, ho_ps, ho_sq, ho_read, sq_done, half_ready, staged, o_ready,
         out_ready, stored) = map(sem, (
            "ix_ps", "ix_relu", "ix_used", "chosen", "e_done", "silu_done", "lb_in", "lb_exp", "lv_ps", "lv_used", "s01_done",
            "ho_ps", "ho_sq", "ho_read", "sq_done", "half_ready", "staged", "o_ready", "out_ready", "stored"))

        C_T = {"cq_ab": (R_lo[:, 4:6, :], R_lo[:, 6:8, :]), "cq": (hT_hi[:, 4:6, :], hT_lo[:, 4:6, :]),
               "ckv": (hT_hi[:, 6:8, :], hT_lo[:, 6:8, :])}

        def head(n):
            pp = A[:, HTF + 384 * (n % 2):][:, 0:384], A[:, HTF + 768 + 384 * (n % 2):][:, 0:384]
            if n < 8:
                kv = n // (HEADS_A // KV_A)
                return dict(qk=[(tile_at(AB_QK, n // 2), tile_at(AB_QK, 4 + kv), 64 * (n % 2), HD)],
                            v=[A[:, AB_TOK + 256 * t + 64 * kv:][:, 0:64] for t in range(TT)], dv=HD, mask="band",
                            scale=HD ** -0.5, sink=n, o=tile_at(AB_QK, n // 2), oc=64 * (n % 2), pp=pp,
                            units=(AB + 1, AB + 2, AB + 5 + n // 4))
            if n < 16:
                h = n - 8
                return dict(qk=[(tile_at(AB_QK, 8 + h // 2), tile_at(AB_QK, 6), 64 * (h % 2), HD)],
                            v=[A[:, AB_TOK + 256 * t + 128:][:, 0:64] for t in range(TT)], dv=HD, mask="chosen",
                            scale=HD ** -0.5, sink=None, o=tile_at(AB_QK, 8 + h // 2), oc=64 * (h % 2), pp=pp,
                            units=(AB + 1, AB + 3, AB + 4))
            if n < 32:
                h = n - 16
                q, k = 4 * (h // 4) + (h % 4) // 2, 4 * (h // 4) + 2 + (h % 4) // 2
                return dict(qk=[(tile_at(C_QK, q), tile_at(C_QK, k), 64 * (h % 2), HD)],
                            v=[A[:, C_V + D * t + 64 * h:][:, 0:64] for t in range(TT)], dv=HD, mask="causal",
                            scale=HD ** -0.5, sink=None, o=tile_at(C_QK, q), oc=64 * (h % 2), pp=pp,
                            units=(CU + h // 4, CU + 4 + 2 * (h // 4), CU + 5 + 2 * (h // 4)))
            h = n - 32
            return dict(qk=[(tile_at(L_QN, h), tile_at(L_KN, h), 0, NOPE),
                            (tile_at(L_QR, h // 2), tile_at(L_KR, 0), 64 * (h % 2), ROPE)],
                        v=[A[:, L_V + 2 * D * t + 128 * h:][:, 0:128] for t in range(TT)], dv=128, mask="causal",
                        scale=(NOPE + ROPE) ** -0.5, sink=None, o=tile_at(L_QN, h), oc=0, pp=pp,
                        units=(ML + 1, ML + 4) + ((ML + 3, ML + 5, ML + 6) if h < 8 else (ML + 7, ML + 8, ML + 9)))

        O_TILES = {"ab": [tile_at(AB_QK, j) for j in (0, 1, 2, 3, 8, 9, 10, 11)],
                   "c": [tile_at(C_QK, j) for j in (0, 1, 4, 5, 8, 9, 12, 13)],
                   "hg": [tile_at(H_F, j) for j in range(8)],
                   "la": [tile_at(L_QN, j) for j in range(8)], "lb": [tile_at(L_QN, 8 + j) for j in range(8)]}

        STAGE = {"ab": (TURNED, AB_TMP), "c": (TURNED, C_TMP), "hg": (HTF, HTF + 512), "la": (TURNED, TURNED),
                 "lb": (HTF, HTF + 512)}
        TURN_TO = {"ab": (hT_hi, hT_lo), "c": (hT_hi, hT_lo), "hg": (hT_hi, hT_lo), "la": (R_hi, R_lo),
                   "lb": (hT_hi, hT_lo)}

        def fills(u, form, src, reader, dsts):
            return [("fill", u, i, len(dsts), form, src, reader, d) for i, d in enumerate(dsts)]

        LAG = 3

        def whole(s_, k):
            return [("ada", s_, k, part) for part in range(3)]

        def turn_pair(name, j):
            return [("turn", name, j)]

        def downs(u0, groups, after=None):
            s, n_ = [], len(groups)
            for j, g in enumerate(groups):
                if j < n_ - 2:
                    s += [("down", u0 + j, g, j == 0)] + (after or {}).get(j, [])
            return s + [("last", u0 + n_ - 2, groups[-2:])]

        def ab_steps():
            cq = A[:, AB_CQ:AB_CQ + 512]
            s = [("angles",)] + fills(AB, "N", "h", "plain", [two(cq)])
            s += fills(AB + 1, "N", "h", "plain", [two(A[:, AB_TOK:AB_TOK + 512])])
            s += [("norm2", cq, AB), ("gate_sum", 0, 0, 1, 5, 6)]
            s += fills(AB + 2, "T", "h", "rope", [AB_TMP])
            s += [("turn2", cq, COL["ab_q"], "cq_ab", 0)]
            s += fills(AB + 3, "T", "h", "rope", [AB_TMP])
            rope = lambda tile: [("rope", AB_TMP, TURNED, AB_QK + 256 * tile, 512)]
            s += rope(4) + [("gate_sum", 4, 2)]
            f = fills(AB + 4, "T", "cq_ab", "rope", [AB_TMP] * 4)
            s += [f[0]] + rope(6) + [("gate_sum", 5, 3), f[1]] + rope(12) + [("gate_sum", 6, 4), f[2]] + rope(14)
            s += [("gate_sum", 7, 7), f[3]] + rope(8) + [("gate0",)]
            s += fills(AB + 5, "T", "h", "rope", [AB_TMP]) + rope(10)
            s += [("index", h) for h in range(3)]
            s += fills(AB + 6, "T", "h", "rope", [AB_TMP]) + rope(0)
            s += [("index", h) for h in range(3, IDX_HEADS)] + rope(2)
            ada_parts = [("ada", 1, k, part) for k in range(6) for part in range(3)]
            for n in range(16 + LAG):
                s += [("head", n, 0, 16)]
                if n < TOPK // 8:
                    s += [("topk", n)]
                if n == TOPK // 8 - 1:
                    s += [("chosen",)]
                if n >= 1:
                    take = 2 if n >= TOPK // 8 + 1 and n % 2 else 1
                    s, ada_parts = s + ada_parts[:take], ada_parts[take:]
                if n in (7, 11, 15):
                    s += turn_pair("ab", (n - 7) // 4)
            s += ada_parts + turn_pair("ab", 3) + [("rows", 0, 0)]
            return s + downs(AB + 7, [0, 1, 2, 3], {0: whole(1, 6), 1: whole(1, 7)})

        def c_steps():
            s = []
            for j in range(4):
                s += fills(CU + j, "N", "h", "plain", [arena(C_V, TT, D)[:, :, 256 * j:256 * j + 256]])
                if j == 1:
                    s += [("begin", 3)]
                if j >= 2:
                    s += whole(3, j - 2)
            rope = lambda j: [("rope", C_TMP, TURNED, C_QK + 512 * j, 512)]
            n = 16
            for j in range(8):
                s += fills(CU + 4 + j, "T", "h", "rope", [C_TMP])
                if j:
                    s += rope(j - 1)
                if j in (0, 2, 4, 6):
                    s += whole(3, 2 + j // 2)
                if j >= 3:
                    for _ in range(2 if j > 3 else 1):
                        s += [("head", n, 16, 32)]
                        n += 1
            s += rope(7)
            after = {25: 0, 28: 1, 31: 2}
            while n < 32 + LAG:
                s += [("head", n, 16, 32)]
                if n in after:
                    s += turn_pair("c", after[n])
                n += 1
            s += turn_pair("c", 3) + [("rows", 1, 0)]
            return s + downs(CU + 12, [0, 1, 2, 3], {0: whole(3, 6), 1: whole(3, 7)})

        def hg_steps():
            value = lambda u, j: fills(u, "N", "h", "plain", [arena(H_V, TT, D)[:, :, 256 * j:256 * j + 256]])
            s = [("hg_start",)] + value(HG, 0) + value(HG + 1, 1)
            for j in range(4):
                s += fills(HG + 2 + j, "T", "h", "silu", [A[:, H_Q + 512 * j:H_Q + 512 * (j + 1)]])
            for j in range(4):
                s += fills(HG + 6 + j, "T", "h", "forget", [j])
            between = [value(HG + 10 + j, 2 + j) for j in range(2)]
            between += [fills(HG + 12 + j, "N", "h", "gate", [arena(H_G, TT, D)[:, :, 256 * j:256 * j + 256]])
                        for j in range(4)]
            for l in range(LEVELS):
                if l not in BARE_LEVELS:
                    s += between.pop(0)
                s += [("level", l)]
            s += [("hg_out", 0), ("level", LEVELS), ("hg_out", 1), ("turn_tile", 0), ("turn_tile", 1)]
            return s + downs(HG + 16, [0, 1, 2, 3])

        def mla_steps():
            ckv, dq = (A[:, L_C[k_]:L_C[k_] + 512] for k_ in ("ckv", "dq"))
            s = fills(ML, "N", "h", "plain", [two(ckv)])
            s += [("second", 0)] + fills(ML + 1, "Th", "h", "rope", [L_TMP])
            s += [("norm2", ckv, ML), ("second", 1)]
            s += [("turn2", ckv, COL["kv"], "ckv", ML + 2)]
            s += fills(ML + 2, "N", "R", "plain", [two(dq)])
            s += [("rope", L_TMP, L_TURNED, L_KR, 256), ("norm2", dq, ML + 2)]
            f = fills(ML + 3, "T", "ckv", "plain", [A[:, L_KN + 512 * i:][:, 0:512] for i in range(4)])
            s += f[0:3] + [("turn2", dq, COL["mla_q"], "cq", 0)] + f[3:]
            for i, f in enumerate(fills(ML + 4, "T", "cq", "rope", [L_TMP] * 4)):
                s += [f] + ([("rope", L_TMP, L_TURNED, L_QR + 512 * (i - 1), 512)] if i else [])
            s += [("rope", L_TMP, L_TURNED, L_QR + 512 * 3, 512)]
            v = arena(L_V, TT, 2 * D)

            def values(u, j):
                return fills(u, "W", "ckv", "plain",
                             [v[:, t, 1024 * j + 512 * h:1024 * j + 512 * h + 512] for t in range(TT) for h in range(2)])

            s += values(ML + 5, 0)
            s += fills(ML + 6, "T", "cq", "plain", [A[:, L_QN + 512 * i:][:, 0:512] for i in range(4)])
            rest = fills(ML + 7, "T", "ckv", "plain", [A[:, L_KN + 2048 + 512 * i:][:, 0:512] for i in range(4)])
            rest += values(ML + 8, 1)
            rest += fills(ML + 9, "T", "cq", "plain", [A[:, L_QN + 2048 + 512 * i:][:, 0:512] for i in range(4)])
            for n in range(32, 48 + LAG):
                s += [("head", n, 32, 48)]
                take = 2 if n % 2 else 1
                s, rest = s + rest[:take], rest[take:]
                if n in (43, 45, 47, 49):
                    s += turn_pair("la", (n - 43) // 2)
            assert not rest
            return s + downs(ML + 10, list(range(8)), {0: turn_pair("lb", 0) + turn_pair("lb", 1),
                                                       1: turn_pair("lb", 2) + turn_pair("lb", 3)})

        own = lambda name, at=0: (vec[:, COL[name] + at:COL[name] + at + KT], zero8)
        mod = (sc_c, bi_c)

        def bound(b, what, last_unit, sb_, second=None, lead=()):
            return [("bound", b, what, last_unit, sb_, second, lead)]

        STEPS = [("start",), ("finish", 0)] + ab_steps()
        STEPS += [("finish", 1)] + bound(0, "ln", AB + 10, mod) + [
            ("gate", 1), ("rows", 0, 1), ("mlp", 0, M0, 2)]
        STEPS += [("finish", 2)] + bound(1, "ln", M0 + 31, mod, lead=(CU, CU + 1)) + [("gate", 2)] + c_steps()
        STEPS += [("finish", 3)] + bound(2, "ln", CU + 15, mod) + [
            ("gate", 3), ("rows", 1, 1), ("mlp", 1, M1, None)]
        STEPS += bound(3, "lnrms", M1 + 31, own("hgrn"), lead=(HG, HG + 1)) + hg_steps()
        STEPS += bound(4, "rms", HG + 19, own("mlp")) + [("mlp", 2, M2, None)]
        STEPS += bound(5, "rms", M2 + 31, own("kv_in"), own("mla"), lead=(ML,)) + mla_steps()
        STEPS += bound(6, "rms", ML + 17, own("mlp", 8)) + [("final_row",), ("mlp", 3, M3, None)]
        STEPS += bound(7, "final", M3 + 31, None)

        def T_unit(u0, k):
            return u0 + (2 * k - 1 if k else 0)

        def D_unit(u0, k):
            return u0 + (2 * k + 2 if k < PAIRS - 1 else 2 * PAIRS - 1)

        LOOPS = (PAIRS - 4) // 2

        block = ctx.enter_context(nc.Block())

        @block.sync
        def _(sp):
            def load(u, s):
                sp.dma_start(raw[:, s, :], stream[u]).then_inc(raw_full[s], 16)

            def load_start(k):
                if k >= START_BUFS:
                    sp.wait_ge(ada_used, adas_before(0, k - START_BUFS + 1))
                sp.dma_start(START_BUF(A, k), ada_w[0, k, :, 0:2 * D]).then_inc(ld_start[k % START_BUFS], 16)

            sp.dma_start(vec[:, :], cols).then_inc(ld_vec, 16)
            sp.dma_start(rc[:, :], rope_cols).then_inc(ld_pos, 16)
            sp.dma_start(A[:, ANGLES:ANGLES + SEQ].bitcast(mybir.dt.int32), pos.partition_broadcast(P)).then_inc(ld_pos, 16)
            sp.dma_start(A[:, START_CONSTS:START_CONSTS + 4 * P], consts[:, 0:4 * P]).then_inc(ld_const, 16)
            for k in range(START_BUFS):
                load_start(k)
            for k in range(START_BUFS, KT):
                if k == KT - 1:
                    load(0, 0)
                load_start(k)
            sp.wait_ge(consts_ready, 1)
            sp.dma_start(hTf, x_t.rearrange("(k p) t -> p k t", p=P)).then_inc(ld_xt, 16)
            load(1, 1)
            load(2, 2)
            sp.wait_ge(ada_used, adas_before(0, KT))
            load(3, 3)
            for (k0, k1), buf in gate_bufs[:-1]:
                sp.dma_start(buf.rearrange("p (k n) -> p k n", n=D),
                             ada_w[0, k0:k1, :, 2 * D:3 * D].rearrange("k p n -> p k n")).then_inc(ld_gate, 16)
            with sp.Fori(1, UNITS // SLOTS) as i:
                for s in range(SLOTS):
                    sp.wait_ge(lo_done, SLOTS * i + (s + 1 - SLOTS))
                    load(SLOTS * i + s, s)
            for u in range(UNITS // SLOTS * SLOTS, UNITS):
                sp.wait_ge(lo_done, u + 1 - SLOTS)
                load(u, u % SLOTS)
            for t in range(TT):
                sp.wait_ge(out_ready, t + 1)
                sp.dma_start(out[t * P:(t + 1) * P, :], N[:, t, :]).then_inc(stored, 16)
            sp.wait_ge(stored, 16 * TT)

        @block.gpsimd
        def _(pool):
            def split(u, s):
                pool.wait_ge(hi_done, u + 1)
                pool.tensor_tensor(w_lo[:, s, :], raw[:, s, :], w_hi[:, s, :], ALU.subtract).then_inc(lo_done, 1)

            split(0, 0)
            pool.wait_ge(ada_col, 1)
            pool.memset(ada_acc, 0.0).then_inc(pool_zero, 1)
            for u in range(1, SLOTS):
                split(u, u)
            with pool.Fori(1, UNITS // SLOTS) as i:
                for s in range(SLOTS):
                    split(SLOTS * i + s, s)
            for u in range(UNITS // SLOTS * SLOTS, UNITS):
                split(u, u % SLOTS)

        @block.tensor
        def _(pe):
            n = dict(fill=0, rope=0, turn=0, plain=0, e=0, pair=0, c=0, gates=0, y=0, norm=0, half=0, f=4, staged=0)
            held = {}
            ready = {}
            made = {}
            led = set()

            def claim(b):
                if b in held:
                    pe.wait_ge(*held[b])

            def weights(u):
                pe.wait_ge(lo_done, u + 1)

            def mm3(o, lh, ll, rh, rl, start, stop):
                pe.matmul(o, lh, rh, start=start, stop=False, skip_group_check=True)
                pe.matmul(o, lh, rl, start=False, stop=False, skip_group_check=True)
                return pe.matmul(o, ll, rh, start=False, stop=stop, skip_group_check=True)

            def source(src):
                return {"h": (hT_hi, hT_lo), "R": (R_hi, R_lo), **C_T}[src]

            def parts_of(u, kts):
                return [t_[:, u % SLOTS, :].rearrange("p (k n) -> p k n", k=kts) for t_ in (w_hi, w_lo)]

            def fill(u, part, parts, form, src, reader):
                kts = KT if parts == 1 else 2
                hh, hl = source(src)
                wh, wl = parts_of(u, kts)
                b = n["fill"] % 2
                bank = B[b]
                if u not in led:
                    claim(b)
                    if part == 0:
                        weights(u)
                    if u and src != "R":
                        pe.wait_ge(pair_ready, made[src])
                    last = None
                    if form == "W":
                        t, h = part // 2, part % 2
                        for k in range(kts):
                            last = mm3(bank[:, :], hh[:, k, P * t:P * t + P], hl[:, k, P * t:P * t + P],
                                       wh[:, k, 512 * h:512 * h + 512], wl[:, k, 512 * h:512 * h + 512], k == 0,
                                       k == kts - 1)
                    else:
                        for a in range(1 if form == "Th" else 2):
                            o = bank[:, 256 * a:256 * a + 256]
                            for k in range(kts):
                                if u == 0 and a == 0 and k % 2 == 0:
                                    pe.wait_ge(pair_ready, k // 2 + 1)
                                if src == "R" and k == 0:
                                    pe.wait_ge(pair_ready, made["R"] - 2 * (1 - a))
                                if form == "N":
                                    at = P * a
                                    last = mm3(o, hh[:, k, at:at + P], hl[:, k, at:at + P], wh[:, k, 0:256],
                                               wl[:, k, 0:256], k == 0, k == kts - 1)
                                else:
                                    at = 256 * part + P * a
                                    last = mm3(o, wh[:, k, at:at + P], wl[:, k, at:at + P], hh[:, k, :], hl[:, k, :],
                                               k == 0, k == kts - 1)
                    last.then_inc(unit_done if part == parts - 1 else fill_done, 1)
                n["fill"] += 1
                key = {"plain": "plain", "rope": "rope"}.get(reader, "e")
                n[key] += 1
                held[b] = ({"plain": fill_read, "rope": turn_f, "e": e_done}[key], n[key])
                ready[(u, part)] = ({"plain": fill_read, "rope": roped, "e": silu_done}[key], n[key])

            def lead(units):
                for t in range(TT):
                    if t == 1:
                        groups(1)
                    for i, u in enumerate(units):
                        wh, wl = parts_of(u, KT)
                        b = (n["fill"] + i) % 2
                        if t == 0:
                            claim(b)
                            weights(u)
                        for k in range(KT):
                            if i == 0 and k % 4 == 0:
                                pe.wait_ge(pair_ready, n["pair"] - 1 + k // 4)
                            at = P * t
                            last = mm3(B[b][:, 256 * t:256 * t + 256], hT_hi[:, k, at:at + P], hT_lo[:, k, at:at + P],
                                       wh[:, k, 0:256], wl[:, k, 0:256], k == 0, k == KT - 1)
                        if t == 1:
                            last.then_inc(unit_done, 1)
                led.update(units)

            def down(u, s, lh, ll, first):
                wh = w_hi[:, s, :].rearrange("p (k n) -> p k n", k=2)
                wl = w_lo[:, s, :].rearrange("p (k n) -> p k n", k=2)
                for t in range(TT):
                    for k in range(2):
                        for h in range(2):
                            c = slice(512 * h, 512 * h + 512)
                            m = mm3(B[4 + 2 * t + h][:, :], lh[:, k, P * t:P * t + P], ll[:, k, P * t:P * t + P],
                                    wh[:, k, c], wl[:, k, c], first and k == 0, False)
                m.then_inc(unit_done, 1)

            def down_last(u, rows_, wait_second):
                w = [parts_of(u + i, 2) for i in range(2)]
                for i, t, h in [(0, 0, 0), (0, 0, 1), (1, 0, 0), (1, 0, 1), (0, 1, 0), (1, 1, 0), (0, 1, 1), (1, 1, 1)]:
                    if (i, t, h) == (1, 0, 0):
                        wait_second()
                    c = slice(512 * h, 512 * h + 512)
                    for k in range(2):
                        m = mm3(B[4 + 2 * t + h][:, :], rows_[i][0][:, k, P * t:P * t + P], rows_[i][1][:, k, P * t:P * t + P],
                                w[i][0][:, k, c], w[i][1][:, k, c], False, i == 1 and k == 1)
                    if t == 1 and h == 1:
                        m.then_inc(unit_done, 1)
                    elif i == 1:
                        m.then_inc(y_done, 1)

            def group(b, tiles, by_vector=False):
                claim(b)
                for i, tile in enumerate(tiles):
                    m = pe.transpose(B[b][:, P * i:P * i + P], tile, ident[:, :])
                n["pair"] += 1
                m.then_inc(pair_turned, 1)
                n["staged" if by_vector else "f"] += 1
                held[b] = (staged, n["staged"]) if by_vector else (pair_f, n["f"])

            def groups(t, banks=None):
                n["norm"] += banks is None
                for j in range(2):
                    if banks is None and t == 1 and j == 0:
                        n["half"] += 1
                        pe.wait_ge(half_ready, n["half"])
                    elif banks is None:
                        pe.wait_ge(n_ready, n["norm"])
                    group((banks or (2 * t, 2 * t + 1))[j], [N[:, t, P * f:P * f + P] for f in range(4 * j, 4 * j + 4)],
                          banks is None and t == 1 and j == 0)

            def qk(k):
                h, bank = head(k), B[4 + k % 2]
                for u in h["units"]:
                    pe.wait_ge(*ready[(u, max(part for u_, part in ready if u_ == u))])
                if k >= 2:
                    pe.wait_ge(exp_done, k - 1)
                for t in range(TT):
                    o = bank[:, 0:128] if t == 0 else bank[:, 128:384]
                    for i, (q, kk, off, w) in enumerate(h["qk"]):
                        pe.matmul(o, q[off:off + w, P * t:P * t + P], kk[off:off + w, 0:P * (t + 1)], start=i == 0,
                                  stop=False, skip_group_check=True)
                    if h["mask"] == "chosen":
                        m = pe.matmul(o, ident_b[:, :], chosen_b[:, 0:128] if t == 0 else chosen_b[:, 128:384],
                                      start=False, stop=True, skip_group_check=True)
                    else:
                        if t == 1 and h["mask"] == "band":
                            pe.matmul(bank[:, 128:256], ident_b[:, :], band_b[:, :], start=False, stop=False,
                                      skip_group_check=True)
                        m = pe.matmul(bank[:, 256 * t:256 * t + P], ident_b[:, :], causal_b[:, :], start=False, stop=True,
                                      skip_group_check=True)
                m.then_inc(s_done, 1)

            def turn_probs(k):
                pe.wait_ge(exp_done, k + 1)
                if k >= 1:
                    pe.wait_ge(pt_done, k)
                for i in range(3):
                    m = pe.transpose(B[6][:, P * i:P * i + P], head(k)["pp"][0][:, P * i:P * i + P], ident[:, :])
                m.then_inc(t_done, 1)

            def pv(k):
                h = head(k)
                pe.wait_ge(pt_done, k + 1)
                if k >= 1:
                    pe.wait_ge(o_done, k)
                dv, pt = h["dv"], h["pp"][1]
                pe.matmul(B[7][:, 0:dv], pt[:, 0:P], h["v"][0], start=True, stop=True, skip_group_check=True)
                pe.matmul(B[7][:, dv:2 * dv], pt[:, P:2 * P], h["v"][0], start=True, stop=False, skip_group_check=True)
                pe.matmul(B[7][:, dv:2 * dv], pt[:, 2 * P:3 * P], h["v"][1], start=False, stop=True,
                          skip_group_check=True).then_inc(pv_done, 1)

            def mlp(m, u0):
                f0, p0 = n["fill"], n["plain"]

                def up(k, kp, u, s):
                    if isinstance(k, int) and k < 2:
                        claim((f0 + kp) % 2)
                    else:
                        pe.wait_ge(fill_read, k + (p0 - 1))
                    pe.wait_ge(lo_done, u + 1)
                    wh = w_hi[:, s, :].rearrange("p (k n) -> p k n", k=KT)
                    wl = w_lo[:, s, :].rearrange("p (k n) -> p k n", k=KT)
                    for a in range(2):
                        for kt in range(KT):
                            if isinstance(k, int) and k == 0 and a == 0 and kt % 4 == 0:
                                pe.wait_ge(pair_ready, n["pair"] - 1 + kt // 4)
                            last = mm3(B[(f0 + kp) % 2][:, 256 * a:256 * a + 256],
                                       wh[:, kt, P * a:P * a + P], wl[:, kt, P * a:P * a + P],
                                       hT_hi[:, kt, :], hT_lo[:, kt, :], kt == 0, kt == KT - 1)
                    last.then_inc(unit_done, 1)

                def dn(k, kp, u, s, first=False):
                    pe.wait_ge(lo_done, u + 1)
                    pe.wait_ge(u_ready, PAIRS * m + k + 1)
                    down(u, s, u_hi[kp], u_lo[kp], first)

                for k in range(2):
                    up(k, k, T_unit(u0, k), T_unit(u0, k) % SLOTS)
                pe.wait_ge(y_read, n["y"])
                pe.wait_ge(gate_read, n["gates"])
                dn(0, 0, D_unit(u0, 0), D_unit(u0, 0) % SLOTS, first=True)
                with pe.Fori(0, LOOPS) as i:
                    for j in range(2):
                        ut, ud = T_unit(u0, 2 + j), D_unit(u0, 1 + j)
                        up(2 * i + (2 + j), j, 4 * i + ut, ut % SLOTS)
                        dn(2 * i + (1 + j), (1 + j) % 2, 4 * i + ud, ud % SLOTS)
                k = PAIRS - 2
                up(k, k % 2, T_unit(u0, k), T_unit(u0, k) % SLOTS)
                dn(k - 1, (k - 1) % 2, D_unit(u0, k - 1), D_unit(u0, k - 1) % SLOTS)
                k = PAIRS - 1
                up(k, k % 2, T_unit(u0, k), T_unit(u0, k) % SLOTS)
                weights(D_unit(u0, k))
                pe.wait_ge(u_ready, PAIRS * m + k)
                down_last(D_unit(u0, k - 1), [(u_hi[j], u_lo[j]) for j in ((k - 1) % 2, k % 2)],
                          lambda: pe.wait_ge(u_ready, PAIRS * m + k + 1))
                n["fill"] += PAIRS
                n["plain"] += PAIRS
                for j in range(2):
                    held[(f0 + j) % 2] = (fill_read, n["plain"] - 1 + j)

            def gate(first=False):
                if n["y"]:
                    pe.wait_ge(y_read, n["y"] - 2)
                if first:
                    pe.wait_ge(gate_used, KT)
                acc = gate_r if first else ada_acc[:, 2 * D:3 * D]
                for h in range(2):
                    m = pe.matmul(B[4 + h][:, :], ones[:, :], acc[:, 512 * h:512 * h + 512], start=True, stop=True)
                m.then_inc(gate_ps, 1)
                n["gates"] += 1

            pe.wait_ge(consts_ready, 1)
            for step in STEPS:
                kind, a = step[0], step[1:]
                if kind == "start":
                    n["pair"] = made["h"] = 4
                elif kind == "finish":
                    pe.wait_ge(ada_used, adas_before(a[0], KT))
                    claim(3)
                    for j in range(2 * KT):
                        m = pe.matmul(B[3][:, j:j + 1], ada_acc[:, P * j:P * j + P], ones[:, 0:1], start=True, stop=True)
                    m.then_inc(ada_col, 1)
                    held[3] = (col_ready, a[0] + 1)
                elif kind == "gate0" or kind == "gate" and a[0] == 2:
                    gate(kind == "gate0")
                elif kind == "fill":
                    fill(*a[0:6])
                elif kind == "rope":
                    pe.wait_ge(turn_f, n["turn"] + 1)
                    claim(2)
                    buf, w = a[0] + 512 * (n["turn"] % 2), a[3]
                    pe.matmul(B[2][:, 0:w], perm[:, :], A[:, buf:buf + w], start=True, stop=True).then_inc(turn_ps, 1)
                    n["turn"] += 1
                    held[2] = (roped, n["turn"])
                elif kind == "turn2":
                    n["c"] += 1
                    pe.wait_ge(o_ready, n["c"])
                    t2 = two(a[0])
                    group((n["fill"] + 1) % 2, [t2[:, t, P * f:P * f + P] for f in range(2) for t in range(TT)])
                    made[a[2]] = n["pair"]
                elif kind == "second":
                    groups(a[0], (2, 3))
                    made["R"] = n["pair"]
                elif kind == "index":
                    h = a[0]
                    if h == 0:
                        pe.wait_ge(*ready[(AB + 3, 0)])
                        pe.wait_ge(*ready[(AB + 4, 1)])
                        pe.wait_ge(gate_read, n["gates"])
                    if h >= 2:
                        pe.wait_ge(ix_relu, h - 1)
                    q, kk, off = tile_at(AB_QK, 12 + h // 2), tile_at(AB_QK, 7), 64 * (h % 2)
                    for t in range(TT):
                        m = pe.matmul(B[4 + h % 2][:, 128 * t:128 + 256 * t], q[off:off + HD, P * t:P * t + P],
                                      kk[off:off + HD, 0:P * (t + 1)], start=True, stop=True)
                    m.then_inc(ix_ps, 1)
                elif kind == "chosen":
                    pass
                elif kind == "head":
                    k, first, last = a
                    if k == first:
                        pe.wait_ge(gate_read, n["gates"])
                        if n["y"]:
                            pe.wait_ge(y_read, n["y"])
                        if k == 0:
                            pe.wait_ge(ix_relu, IDX_HEADS)
                    if k == HEADS_A:
                        pe.wait_ge(chosen, 1)
                    if k < last:
                        qk(k)
                    if first <= k - 2 < last:
                        turn_probs(k - 2)
                    if first <= k - 3 < last:
                        pv(k - 3)
                elif kind == "turn":
                    name, j = a
                    tiles = O_TILES[name]
                    pe.wait_ge(o_done, {"ab": 4 * j + 4, "c": 20 + 4 * j, "la": 34 + 2 * j, "lb": 42 + 2 * j}[name])
                    group(j, [tiles[f][:, P * t:P * t + P] for f in (2 * j, 2 * j + 1) for t in range(TT)])
                    made[(name, j)] = n["pair"]
                    n["turned"] = name
                elif kind in ("down", "last"):
                    u, g = a[0], a[1]
                    if kind == "down" and a[2]:
                        if n["y"]:
                            pe.wait_ge(y_read, n["y"])
                        pe.wait_ge(gate_read, n["gates"])
                        if n["turned"] == "hg":
                            pe.wait_ge(ho_read, TT)
                        if n["turned"] == "la":
                            pe.wait_ge(o_done, 48)
                        names = ["la", "lb"] if n["turned"] in ("la", "lb") else [n["turned"]]

                    def rows_of(g):
                        hh, hl = TURN_TO[names[g // 4]]
                        c = slice(2 * (g % 4), 2 * (g % 4) + 2)
                        return hh[:, c], hl[:, c]

                    if kind == "down":
                        weights(u)
                        pe.wait_ge(pair_ready, made[(names[g // 4], g % 4)])
                        down(u, u % SLOTS, *rows_of(g), a[2])
                    else:
                        weights(u + 1)
                        pe.wait_ge(pair_ready, made[(names[g[1] // 4], g[1] % 4)])
                        down_last(u, [rows_of(g_) for g_ in g], lambda: None)
                elif kind == "bound":
                    b, what, _, _, second, units = a
                    n["y"] += 2 * TT
                    if what != "final":
                        if what == "lnrms":
                            n["norm"] += TT
                            n["half"] += 1
                        groups(0)
                        if units:
                            lead(units)
                        elif b < 3:
                            gate()
                        if not units:
                            groups(1)
                        made["h"] = n["pair"]
                elif kind == "mlp":
                    mlp(a[0], a[1])
                elif kind == "level":
                    l = a[0]
                    for g in range(2):
                        if l == 0:
                            pe.wait_ge(silu_done, 8)
                            if g == 0 and n["y"]:
                                pe.wait_ge(y_read, n["y"])
                        elif l < LEVELS:
                            pe.wait_ge(lv_used, 2 * (l - 1) + g + 1)
                        for h in range(4 * g, 4 * g + 4):
                            for t in range(TT):
                                if l == LEVELS and t == 1:
                                    continue
                                i = (h - 4 * g) if l == LEVELS else 2 * (h - 4 * g) + t
                                bank = B[6 + g] if l == LEVELS else B[4 + 2 * g + i // 4]
                                tq = 1 if l == LEVELS else t
                                m = pe.matmul(bank[:, P * (i % 4):P * (i % 4) + P], tile_at(H_K, h)[:, P * t:P * t + P],
                                              tile_at(H_Q, h)[:, P * tq:P * tq + P], start=True, stop=True)
                        m.then_inc(lv_ps, 1)
                elif kind == "hg_out":
                    t = a[0]
                    if t == 0:
                        pe.wait_ge(lv_used, 2 * LEVELS)
                        pe.wait_ge(*ready[(HG + 11, 0)])
                    else:
                        pe.wait_ge(s01_done, 2)
                    v = arena(H_V, TT, D)
                    for h in range(HG_HEADS):
                        o = B[4 + 2 * t + h // 4][:, P * (h % 4):P * (h % 4) + P]
                        if t == 1:
                            pe.matmul(o, A[:, H_S01 + P * h:H_S01 + P * h + P], v[:, 0, P * h:P * h + P], start=True,
                                      stop=False, skip_group_check=True)
                        m = pe.matmul(o, A[:, H_ST + 256 * h + P * t:H_ST + 256 * h + P * t + P],
                                      v[:, t, P * h:P * h + P], start=t == 0, stop=True, skip_group_check=True)
                    m.then_inc(ho_ps, 1)
                elif kind == "turn_tile":
                    t = a[0]
                    pe.wait_ge(o_ready, n["c"] + 1)
                    n["c"] += 1
                    for j in range(2):
                        group(2 * t + j, [O_TILES["hg"][f][:, P * t:P * t + P] for f in range(4 * j, 4 * j + 4)])
                    n["turned"] = "hg"
                    for g in range(4):
                        made[("hg", g)] = n["pair"]

        @block.scalar
        def _(act):
            n = dict(fill=0, rope=0, pair=0, rstd=0, e=0, x=0, part=0, gates=0)

            def hi(u, s, k):
                act.wait_ge(raw_full[s], 16 * k)
                if not (isinstance(u, int) and u < SLOTS):
                    act.wait_ge(unit_done, u + (1 - SLOTS))
                act.activation(w_hi[:, s, :], raw[:, s, :], ACT.Copy).then_inc(hi_done, 1)

            def ahead(u, i=0):
                if isinstance(i, int) and u + SLOTS >= UNITS:
                    return
                v = u + SLOTS
                hi(4 * i + v if not isinstance(i, int) else v, v % SLOTS, i + (v // SLOTS + 1))

            def turned(b, j, scale, bias):
                t = j // 2 % 2
                n["pair"] += 1
                act.wait_ge(pair_turned, n["pair"] - 4)
                for i in range(4):
                    k = 4 * (j % 2) + i
                    ins = act.activation(hTf[:, k, P * t:P * t + P], B[b][:, P * i:P * i + P], ACT.Identity,
                                         scale=scale[:, k:k + 1], bias=bias[:, k:k + 1])
                ins.then_inc(pair_f, 1)

            def normalise(t, rms):
                n["rstd"] += 1
                act.wait_ge(rstd_ready, n["rstd"])
                bias = zero8[:, 0:1] if rms else nmr[:, t:t + 1]
                c = slice(512 * t, D)
                act.activation(N[:, t, c], X[:, t, c], ACT.Identity, scale=rstd[:, t:t + 1], bias=bias).then_inc(n_ready, 1)

            def load_ada(s, k, part, i=0):
                act.wait_ge(ada_used, adas_before(s, k - 1, part + 1) if isinstance(i, int) else
                            3 * i + adas_before(s, k - 1, part + 1))
                src = ada_w[s, k + i] if isinstance(i, int) else ada_w[s, i + k]
                act.dma_start(ada_part(part), src[:, D * part:D * part + D]).then_inc(ld_adas[part], 16)

            def ada_begin(s):
                if s == 1:
                    act.wait_ge(pool_zero, 1)
                else:
                    act.wait_ge(acc_zero, s + 1)
                act.dma_start(ada_acc[0:1, :], ada_b[s:s + 1, :]).then_inc(ld_bias, 16)
                for part in range(3):
                    act.wait_ge(ada_used, adas_before(s))
                    act.dma_start(ada_part(part), ada_w[s, 0, :, D * part:D * part + D]).then_inc(ld_adas[part], 16)

            def mlp(m, u0, s_ada):
                f0 = n["fill"]

                def relu(k, kp, u):
                    act.wait_ge(unit_done, u + 1)
                    if not (isinstance(k, int) and PAIRS * m + k < 2):
                        act.wait_ge(u_ready, k + (PAIRS * m - 1))
                    act.activation(u_f[:, kp, :], B[(f0 + kp) % 2][:, :], ACT.Relu).then_inc(fill_read, 1)

                relu(0, 0, T_unit(u0, 0))
                ahead(T_unit(u0, 0))
                relu(1, 1, T_unit(u0, 1))
                ahead(T_unit(u0, 1))
                ahead(D_unit(u0, 0))
                if s_ada:
                    ada_begin(s_ada)
                with act.Fori(0, LOOPS) as i:
                    for j in range(2):
                        relu(2 * i + (2 + j), j, 4 * i + T_unit(u0, 2 + j))
                        ahead(T_unit(u0, 2 + j), i)
                        ahead(D_unit(u0, 1 + j), i)
                        if s_ada and j == 0:
                            for part in range(3):
                                load_ada(s_ada, 1, part, i)
                for k in (PAIRS - 2, PAIRS - 1):
                    relu(k, k % 2, T_unit(u0, k))
                    ahead(T_unit(u0, k))
                    if k < PAIRS - 1:
                        ahead(D_unit(u0, k - 1))
                        if s_ada:
                            for part in range(3):
                                load_ada(s_ada, KT - 1, part)
                n["fill"] += PAIRS

            act.dma_start(sink_r[:, :], sinks.partition_broadcast(P)).then_inc(ld_sink, 16)
            act.wait_ge(ld_vec, 16)
            act.activation(silu_c[:, :], vec[:, 0:KT], ACT.Exp, scale=-1.0).then_inc(c_exp, 1)
            act.wait_ge(acc_zero, 1)
            act.dma_start(ada_acc[0:1, 0:2 * D], ada_b[0:1, 0:2 * D]).then_inc(ld_bias, 16)
            act.wait_ge(acc_zero, 2)
            act.dma_start(gate_r[0:1, :], ada_b[0:1, 2 * D:3 * D]).then_inc(ld_gate, 16)
            act.wait_ge(ld_sink, 16)
            for u in range(SLOTS):
                hi(u, u, 1)
            for step in STEPS:
                kind, a = step[0], step[1:]
                if kind == "finish" and a[0] == 0:
                    act.wait_ge(ld_xt, 16)
                    act.wait_ge(col_ready, 1)
                    for j in range(4):
                        for k in (2 * j, 2 * j + 1):
                            ins = act.activation(hTf[:, k, :], hTf[:, k, :], ACT.Identity, scale=sc_c[:, k:k + 1],
                                                 bias=bi_c[:, k:k + 1])
                        ins.then_inc(pair_f, 1)
                    n["pair"] = 4
                    act.wait_ge(pair_ready, 4)
                    (k0, _), buf = gate_bufs[-1]
                    act.dma_start(buf, ada_w[0, k0, :, 2 * D:3 * D]).then_inc(ld_gate, 16)
                elif kind == "angles":
                    act.wait_ge(ang_ready, 1)
                    for i, dst in enumerate((sinT, cosT)):
                        ins = act.activation(dst[:, :], arena(ANGLES + SEQ * (2 + i), SEQ), ACT.Sin)
                    ins.then_inc(trig_done, 1)
                elif kind in ("gate", "gate0"):
                    act.wait_ge(gate_ps, n["gates"] + 1)
                    act.wait_ge(y_read, 4 * n["gates"]) if n["gates"] else None
                    for h in range(2):
                        ins = act.activation(gate_r[:, 512 * h:512 * h + 512], B[4 + h][:, :], ACT.Identity,
                                             bias=ones[:, 0:1])
                    ins.then_inc(gate_read, 1)
                    n["gates"] += 1
                    if n["gates"] == 1:
                        act.dma_start(X[:, :, :], x.rearrange("(t p) d -> p t d", p=P)).then_inc(ld_x, 16)
                    if n["gates"] == 1:
                        ada_begin(1)
                elif kind == "begin":
                    ada_begin(a[0])
                elif kind == "fill":
                    u, part, parts, form, src, reader, dst = a
                    if part == parts - 1:
                        act.wait_ge(unit_done, u + 1)
                    else:
                        n["part"] += 1
                        act.wait_ge(fill_done, n["part"])
                    bank = B[n["fill"] % 2]
                    act.wait_ge(x_ready, TT * n["x"]) if n["x"] else None
                    if u == ML + 5 and part == 0:
                        act.wait_ge(roped, n["rope"])
                    if reader == "plain":
                        if len(dst.shape) == 3:
                            act.activation(dst, two(bank[:, :]), ACT.Copy).then_inc(fill_read, 1)
                        else:
                            act.activation(dst, bank[:, :], ACT.Copy).then_inc(fill_read, 1)
                    elif reader == "rope":
                        w = 256 if form == "Th" else 512
                        r = n["rope"]
                        if r >= 2:
                            act.wait_ge(roped, r - 1)
                        act.activation(A[:, dst + 512 * (r % 2):][:, 0:w], bank[:, 0:w], ACT.Copy).then_inc(turn_f, 1)
                        n["rope"] += 1
                    else:
                        e = A[:, H_E + 512 * (n["e"] % 2):][:, 0:512]
                        if n["e"] >= 2:
                            act.wait_ge(silu_done, n["e"] - 1)
                        if reader == "silu":
                            act.activation(dst, bank[:, :], ACT.Copy)
                        elif reader == "gate":
                            act.activation(dst, two(bank[:, :]), ACT.Copy)
                        act.activation(e, bank[:, :], ACT.Exp, scale=-1.0).then_inc(e_done, 1)
                        n["e"] += 1
                    n["fill"] += 1
                    if part == parts - 1:
                        ahead(u)
                elif kind == "turn2":
                    n["pair"] += 1
                    act.wait_ge(pair_ready, n["pair"] - 1)
                    act.wait_ge(pair_turned, n["pair"] - 4)
                    for k in range(2):
                        ins = act.activation(cT_f[:, k, :], B[(n["fill"] + 1) % 2][:, 256 * k:256 * k + 256], ACT.Identity,
                                             scale=vec[:, a[1] + k:a[1] + k + 1], bias=zero8[:, 0:1])
                    ins.then_inc(pair_f, 1)
                elif kind == "second":
                    for j in range(2):
                        if j == 0:
                            act.wait_ge(pair_ready, n["pair"])
                        turned(2 + j, 2 * a[0] + j, *SECOND)
                elif kind == "ada" and a[1] + 1 < KT:
                    load_ada(a[0], a[1] + 1, a[2])
                elif kind == "index":
                    h = a[0]
                    act.wait_ge(ix_ps, h + 1)
                    if h >= 2:
                        act.wait_ge(ix_used, h - 1)
                    act.activation(A[:, AB_IX + 384 * (h % 2):][:, 0:384], B[4 + h % 2][:, 0:384],
                                   ACT.Relu).then_inc(ix_relu, 1)
                elif kind == "head":
                    k, first, last = a
                    if k < last:
                        act.wait_ge(max_done, k + 1)
                        if k == first:
                            act.wait_ge(pair_ready, n["pair"])
                        if k >= 2:
                            act.wait_ge(t_done, k - 1)
                        h, bank = head(k), B[4 + k % 2]
                        pb = h["pp"][0]
                        act.activation(pb[:, 0:128], bank[:, 0:128], ACT.Exp, bias=nb[:, k % 4, 0:1], scale=h["scale"],
                                       accum_out=sm[:, k % 4, 0:1])
                        if h["sink"] is not None:
                            act.activation(sk[:, k % 4, :], nb[:, k % 4, :], ACT.Exp,
                                           bias=sink_r[:, h["sink"]:h["sink"] + 1])
                        act.activation(pb[:, 128:384], bank[:, 128:384], ACT.Exp, bias=nb[:, k % 4, 1:2],
                                       scale=h["scale"], accum_out=sm[:, k % 4, 1:2]).then_inc(exp_done, 1)
                    if first <= k - 2 < last:
                        act.wait_ge(t_done, k - 1)
                        if k - 2 >= 2:
                            act.wait_ge(pv_done, k - 3)
                        act.activation(head(k - 2)["pp"][1], B[6][:, 0:384], ACT.Copy).then_inc(pt_done, 1)
                elif kind == "turn":
                    name, j = a
                    n["pair"] += 1
                    if j >= 2:
                        act.wait_ge(pair_ready, n["pair"] - 2)
                    elif j == 0:
                        act.wait_ge(pair_ready, n["pair"] - 1)
                        act.wait_ge(roped, n["rope"])
                    act.wait_ge(pair_turned, n["pair"] - 4)
                    at = STAGE[name][j % 2]
                    act.activation(A[:, at:at + 512], B[j][:, :], ACT.Copy).then_inc(pair_f, 1)
                elif kind == "rows":
                    act.wait_ge(pair_turned, n["pair"] - 4)
                    if n["x"]:
                        act.wait_ge(x_ready, TT * n["x"])
                    layer, j = a
                    act.dma_start(rows[:, 0, :], ln_g[layer, j].partition_broadcast(P)).then_inc(ld_row, 16)
                    act.dma_start(rows[:, 1, :], ln_b[layer, j].partition_broadcast(P)).then_inc(ld_row, 16)
                elif kind == "final_row":
                    act.wait_ge(pair_turned, n["pair"] - 4)
                    act.dma_start(rows[:, 0, :], final_norm.partition_broadcast(P)).then_inc(ld_fn, 16)
                elif kind == "down":
                    ahead(a[0])
                elif kind == "bound":
                    b, what, last_unit, scales, second, _ = a
                    rms = b >= 4
                    act.wait_ge(pair_ready, n["pair"])

                    def square(t):
                        if what == "lnrms":
                            act.wait_ge(x_ready, TT * n["x"] + t + 1)
                        for h in range(2):
                            if what != "lnrms":
                                act.wait_ge(y_read, 4 * b + 2 * t + h + 1)
                            c = slice(512 * h, 512 * h + 512)
                            ins = act.activation(N[:, t, c], X[:, t, c], ACT.Square, accum_out=ss[:, t, h:h + 1])
                        ins.then_inc(sq_done, 1)

                    if what == "lnrms":
                        normalise(0, False)
                        square(0)
                        normalise(1, False)
                        rms = True
                    for t in range(TT):
                        if b >= 4 and t == 0:
                            square(t)
                        normalise(t, rms)
                        if what == "lnrms" and t == 0:
                            square(1)
                        if what != "final":
                            if t == 0 and b < 3:
                                act.wait_ge(col_ready, b + 2)
                            if t:
                                n["pair"] += 1
                            else:
                                turned(0, 0, *scales)
                            turned(2 * t + 1, 2 * t + 1, *scales)
                            ahead(last_unit - 1 + t)
                    SECOND = second
                    if a[0] < 4:
                        n["x"] += 1
                elif kind == "mlp":
                    mlp(a[0], a[1], a[2])
                elif kind == "hg_start":
                    act.wait_ge(pair_ready, n["pair"])
                    act.dma_start(A[:, H_E:H_E + LEVELS * P], consts[:, 4 * P:]).then_inc(ld_level, 16)
                    act.dma_start(gn_r, g_norm.partition_broadcast(P)).then_inc(ld_gn, 16)
                    act.dma_start(cosT[:, :], rope_2[:, 0, :]).then_inc(ld_rope2, 16)
                    act.dma_start(sinT[:, :], rope_2[:, 1, :]).then_inc(ld_rope2, 16)
                    act.wait_ge(lb_in, 1)
                    act.activation(tmp_c[:, 2, :], tmp_c[:, 0, :], ACT.Exp)
                    act.activation(tmp_c[:, 3, :], tmp_c[:, 1, :], ACT.Exp).then_inc(lb_exp, 1)
                elif kind == "level" and a[0] == LEVELS:
                    for g in range(2):
                        act.wait_ge(lv_ps, 2 * LEVELS + g + 1)
                        act.activation(A[:, H_S01 + 512 * g:H_S01 + 512 * g + 512], B[6 + g][:, :],
                                       ACT.Copy).then_inc(s01_done, 1)
                elif kind == "hg_out":
                    t = a[0]
                    act.wait_ge(ho_ps, t + 1)
                    if t == 0:
                        act.wait_ge(lv_used, 2 * LEVELS)
                    else:
                        act.wait_ge(ho_read, t)
                    for i in range(2):
                        ins = act.activation(A[:, H_TMP + 512 * i:][:, 0:512], B[4 + 2 * t + i][:, :], ACT.Square)
                    ins.then_inc(ho_sq, 1)
                elif kind == "turn_tile":
                    t = a[0]
                    for j in range(2):
                        n["pair"] += 1
                        act.wait_ge(pair_turned, n["pair"] - 4)
                        act.activation(hTf[:, 4 * j:4 * j + 4, P * t:P * t + P],
                                       B[2 * t + j][:, :].rearrange("p (k s) -> p k s", k=4), ACT.Copy).then_inc(pair_f, 1)

        @block.vector
        def _(v):
            n = dict(step=0, plain=0, rope=0, pair=0, e=0, row=0, n=0, gates=0, x=0, y=0, sq=0, root=0, half=0, f=0, staged=0, u={})

            def link(ins):
                n["step"] += 1
                ins.then_inc(v_step, 1)
                v.wait_ge(v_step, n["step"])

            def mark(ins):
                n["step"] += 1
                ins.then_inc(v_step, 1)

            def inverse_root(c0, w):
                c = slice(c0, c0 + w)
                t_, v_ = nw[:, 0, c], ve[:, c]
                i32 = mybir.dt.int32
                ks = [1.0]
                for _ in range(3):
                    ks.insert(0, -abs(ks[0] / 2) ** (1 / 3) if ks[0] > 0 else abs(ks[0] / 2) ** (1 / 3))
                y = rstd[:, c]
                guess = GUESS + math.log2(abs(ks[0])) * 2.0 ** 23 - 2.0 ** 31 * (ks[0] < 0)
                link(v.tensor_scalar(y.bitcast(i32), v_.bitcast(i32), -0.5, guess, ALU.mult, ALU.add))
                for i, k in enumerate(ks[:3]):
                    if w == 1:
                        link(v.scalar_tensor_tensor(out=t_, in0=y, scalar=v_, in1=y, op0=ALU.mult, op1=ALU.mult))
                    else:
                        link(v.tensor_tensor(t_, y, v_, ALU.mult))
                        link(v.tensor_tensor(t_, t_, y, ALU.mult))
                    ins = v.scalar_tensor_tensor(out=y, in0=t_, scalar=-3.0 * k * k, in1=y, op0=ALU.add, op1=ALU.mult)
                    if i < 2:
                        link(ins)
                return ins

            def variance(t, rms):
                if rms:
                    link(v.scalar_tensor_tensor(out=ve[:, t:t + 1], in0=mv[:, t, 0:1], scalar=mv[:, t, 0:1],
                                                in1=mv[:, t, 1:2], op0=ALU.mult, op1=ALU.add))
                    link(v.tensor_scalar(ve[:, t:t + 1], ve[:, t:t + 1], RMS_EPS, None, ALU.add))
                else:
                    link(v.tensor_scalar(ve[:, t:t + 1], mv[:, t, 1:2], LN_EPS, None, ALU.add))

            def row_root(t, rms):
                link(v.bn_aggr(mv[:, t, :], bn[:, t, :, :]))
                variance(t, rms)
                ins = inverse_root(t, 1)
                if not rms:
                    link(ins)
                    ins = v.scalar_tensor_tensor(out=nmr[:, t:t + 1], in0=mv[:, t, 0:1], scalar=-1.0,
                                                 in1=rstd[:, t:t + 1], op0=ALU.mult, op1=ALU.mult)
                ins.then_inc(rstd_ready, 1)
                n["root"] += 1

            def split(f, hi, lo):
                n["pair"] += 1
                n["f"] += 1
                v.wait_ge(pair_f, n["f"])
                link(v.tensor_copy(hi, f))
                v.tensor_tensor(lo, f, hi, ALU.subtract).then_inc(pair_ready, 1)

            def split_tile(t, hi, lo):
                for j in range(2):
                    c = slice(4 * j, 4 * j + 4)
                    split(hTf[:, c, P * t:P * t + P], hi[:, c, P * t:P * t + P], lo[:, c, P * t:P * t + P])

            def ada(s, k, part):
                c = slice(D * part, D * part + D)
                if s == 0 and part == 0:
                    v.wait_ge(ld_start[k % START_BUFS], 16 * (k // START_BUFS + 1))
                if s:
                    v.wait_ge(ld_adas[part], 16 * (KT * (s - 1) + k + 1))
                if k == 0:
                    v.wait_ge(ld_bias, 16 * (s + 1))
                else:
                    v.wait_ge(ada_used, adas_before(s, k - 1, part + 1))
                w = ada_part(part) if s else START_BUF(A, k)[:, c]
                v.scalar_tensor_tensor(out=ada_acc[:, c], in0=w, scalar=silu_c[:, k:k + 1], in1=ada_acc[:, c],
                                       op0=ALU.mult, op1=ALU.add).then_inc(ada_used, 1)

            def mlp(m, u0, s_ada):
                p0, st = n["plain"], n["step"]

                def square(k, kp, step, u_free):
                    v.wait_ge(fill_read, k + (p0 + 1))
                    v.tensor_tensor(u_f[:, kp, :], u_f[:, kp, :], u_f[:, kp, :], ALU.mult).then_inc(v_step, 1)
                    v.wait_ge(v_step, step + 1)
                    if u_free is not None:
                        v.wait_ge(unit_done, u_free + 1)
                    v.tensor_copy(u_hi[kp], two(u_f[:, kp, :])).then_inc(v_step, 1)
                    v.wait_ge(v_step, step + 2)
                    v.tensor_tensor(u_lo[kp], two(u_f[:, kp, :]), u_hi[kp], ALU.subtract).then_inc(u_ready, 1)

                square(0, 0, st, None)
                square(1, 1, st + 2, None)
                if s_ada:
                    zero_acc()
                    v.wait_ge(ld_bias, 16 * (s_ada + 1))
                with v.Fori(0, LOOPS) as i:
                    for j in range(2):
                        square(2 * i + (2 + j), j, 4 * i + (st + 4 + 2 * j), 4 * i + D_unit(u0, j))
                        if s_ada and j == 0:
                            for part in range(3):
                                c = slice(D * part, D * part + D)
                                v.wait_ge(ld_adas[part], 16 * i + 16 * (KT * (s_ada - 1) + 1))
                                v.wait_ge(ada_used, 3 * i + adas_before(s_ada))
                                v.scalar_tensor_tensor(out=ada_acc[:, c], in0=ada_part(part),
                                                       scalar=silu_c[:, bass.ds(i, 1)], in1=ada_acc[:, c],
                                                       op0=ALU.mult, op1=ALU.add).then_inc(ada_used, 1)
                st += 4 + 4 * LOOPS
                for k in (PAIRS - 2, PAIRS - 1):
                    square(k, k % 2, st, D_unit(u0, k - 2))
                    st += 2
                    if s_ada:
                        for part in range(3):
                            ada(s_ada, KT - PAIRS + k, part)
                n["step"], n["plain"] = st, p0 + PAIRS

            def zero_acc():
                v.memset(ada_acc, 0.0).then_inc(acc_zero, 1)

            v.memset(ada_acc[:, 0:2 * D], 0.0).then_inc(acc_zero, 1)
            v.memset(zero8[:, :], 0.0)
            link(v.memset(ones[:, :], 1.0))
            v.wait_ge(c_exp, 1)
            link(v.tensor_scalar(tmp_c[:, 0, :], silu_c[:, :], 1.0, None, ALU.add))
            link(v.reciprocal(tmp_c[:, 1, :], tmp_c[:, 0, :]))
            link(v.tensor_tensor(silu_c[:, :], tmp_c[:, 1, :], vec[:, 0:KT], ALU.mult))
            v.wait_ge(ld_const, 16)
            cst = arena(START_CONSTS, 4, P)
            for i, dst in ((0, ident), (1, perm), (0, ident_b), (2, causal_b), (3, band_b)):
                ins = v.tensor_copy(dst[:, :], cst[:, i, :])
            ins.then_inc(consts_ready, 1)
            v.memset(gate_r, 0.0).then_inc(acc_zero, 1)
            for k in range(KT):
                for part in range(2):
                    ada(0, k, part)

            def angles():
                ang, cs = arena(ANGLES, SEQ), arena(ANGLES + SEQ, SEQ)
                v.wait_ge(ld_pos, 32)
                link(v.tensor_copy(cs, ang.bitcast(mybir.dt.int32)))
                link(v.tensor_scalar(ang, cs, rc[:, 0:1], None, ALU.mult))
                for i, quarter in enumerate((0.0, 0.25)):
                    r = arena(ANGLES + SEQ * (2 + i), SEQ)
                    link(v.tensor_scalar(cs, ang, 1.0 / TWO_PI, quarter, ALU.mult, ALU.add))
                    link(v.tensor_scalar(cs, cs, ROUNDER, None, ALU.add))
                    link(v.tensor_scalar(cs, cs, ROUNDER, None, ALU.subtract))
                    link(v.tensor_copy(r, ang))
                    for part in TWO_PI_PARTS:
                        link(v.scalar_tensor_tensor(out=r, in0=cs, scalar=-part, in1=r, op0=ALU.mult, op1=ALU.add))
                    if quarter:
                        link(v.tensor_scalar(r, r, TWO_PI / 4, None, ALU.add))
                    link(v.tensor_scalar(r, r, PI_BELOW, -PI_BELOW, ALU.min, ALU.max))
                r = arena(ANGLES + 2 * SEQ, SEQ)
                v.tensor_scalar(r, r, rc[:, 1:2], None, ALU.mult).then_inc(ang_ready, 1)

            def finish(s):
                v.wait_ge(ada_col, s + 1)
                shift, sc1 = B[3][:, 0:KT], B[3][:, KT:2 * KT]
                if s == 0:
                    link(v.tensor_scalar(sc_c[:, :], sc1, 1.0, None, ALU.add))
                    v.tensor_copy(bi_c[:, :], shift).then_inc(col_ready, 1)
                else:
                    g = vec[:, COL["ln_g"] + KT * (s - 1):COL["ln_g"] + KT * s]
                    b = vec[:, COL["ln_b"] + KT * (s - 1):COL["ln_b"] + KT * s]
                    link(v.tensor_scalar(tmp_c[:, 0, :], sc1, 1.0, None, ALU.add))
                    link(v.tensor_tensor(sc_c[:, :], tmp_c[:, 0, :], g, ALU.mult))
                    link(v.tensor_tensor(tmp_c[:, 1, :], tmp_c[:, 0, :], b, ALU.mult))
                    v.tensor_tensor(bi_c[:, :], tmp_c[:, 1, :], shift, ALU.add).then_inc(col_ready, 1)

            for step in STEPS:
                kind, a = step[0], step[1:]
                if kind == "finish":
                    if a[0] == 0:
                        finish(0)
                        for j in range(4):
                            c = slice(2 * j, 2 * j + 2)
                            split(hTf[:, c, :], hT_hi[:, c, :], hT_lo[:, c, :])
                elif kind == "angles":
                    angles()
                elif kind == "gate_sum":
                    v.wait_ge(ld_gate, 16 * (len(gate_bufs) + 1))
                    for i, k in enumerate(a[1:]):
                        v.scalar_tensor_tensor(out=gate_r, in0=gate_w[k], scalar=silu_c[:, k:k + 1], in1=gate_r,
                                               op0=ALU.mult, op1=ALU.add).then_inc(gate_used, 1)
                        v.wait_ge(gate_used, a[0] + i + 1)
                elif kind in ("gate", "gate0"):
                    n["gates"] += 1
                    v.wait_ge(gate_ps, n["gates"])
                    if n["gates"] == 3:
                        zero_acc()
                elif kind == "fill":
                    u, part, parts, form, src, reader, dst = a
                    n["plain"] += reader == "plain"
                    if reader == "plain":
                        n["u"][u] = n["plain"]
                    if reader in ("silu", "forget", "gate"):
                        i = n["e"]
                        e = A[:, H_E + 512 * (i % 2):][:, 0:512]
                        n["e"] += 1
                        v.wait_ge(e_done, n["e"])
                        link(v.tensor_scalar(e, e, 1.0, None, ALU.add))
                        link(v.reciprocal(e, e))
                        if reader == "silu":
                            v.tensor_tensor(dst, dst, e, ALU.mult).then_inc(silu_done, 1)
                        elif reader == "gate":
                            link(v.tensor_tensor(dst, dst, two(e), ALU.mult))
                            if i == 8:
                                v.wait_ge(ld_gn, 16)
                            g4 = dst.rearrange("p t (h v) -> p t h v", v=P)
                            gb = gn_r.unsqueeze(1).unsqueeze(1).to_broadcast([P, TT, 2, P])
                            v.tensor_tensor(g4, g4, gb, ALU.mult).then_inc(silu_done, 1)
                        else:
                            f, k = A[:, H_F + 512 * dst:][:, 0:512], A[:, H_K + 512 * dst:][:, 0:512]
                            for q in range(2):
                                c, m = slice(256 * q, 256 * q + 256), 2 * dst + q
                                (link if q else mark)(v.tensor_scalar(
                                    f[:, c], e[:, c], lb_c[:, 1, m:m + 1], lb_c[:, 0, m:m + 1], ALU.mult, ALU.add))
                            v.tensor_scalar(k, f, -1.0, 1.0, ALU.mult, ALU.add).then_inc(silu_done, 1)
                elif kind == "rope":
                    tmp, turned_at, dst, w = a
                    r = n["rope"]
                    n["rope"] += 1
                    v.wait_ge(turn_f, r + 1)
                    v.wait_ge(trig_done, 1)
                    if w == 256:
                        v.wait_ge(ld_rope2, 32)
                    def shape(x_):
                        return two(x_) if w == 512 else x_
                    cos, sin = ((cosT[:, :].unsqueeze(1).to_broadcast([P, 2, SEQ]),
                                 sinT[:, :].unsqueeze(1).to_broadcast([P, 2, SEQ])) if w == 512 else
                                (cosT[:, :], sinT[:, :]))
                    tmp += 512 * (r % 2)
                    d, f, tb = A[:, dst:dst + w], A[:, tmp:tmp + w], A[:, turned_at:turned_at + w]
                    v.wait_ge(pair_ready, n["pair"])
                    mark(v.tensor_tensor(shape(d), shape(f), cos, ALU.mult))
                    v.wait_ge(turn_ps, r + 1)
                    link(v.tensor_tensor(shape(tb), shape(B[2][:, 0:w]), sin, ALU.mult))
                    v.tensor_tensor(d, d, tb, ALU.add).then_inc(roped, 1)
                elif kind == "ada":
                    ada(a[0], a[1], a[2])
                elif kind == "norm2":
                    c = two(a[0])
                    v.wait_ge(fill_read, n["u"][a[1]])
                    for t in range(TT):
                        link(v.bn_stats(bn[:, t, 0, :], c[:, t, :]))
                        link(v.bn_aggr(mv[:, t, :], bn[:, t, 0:1, :]))
                        variance(t, True)
                    link(inverse_root(0, 2))
                    link(v.tensor_scalar(c[:, 0, :], c[:, 0, :], rstd[:, 0:1], None, ALU.mult))
                    v.tensor_scalar(c[:, 1, :], c[:, 1, :], rstd[:, 1:2], None, ALU.mult).then_inc(o_ready, 1)
                elif kind == "turn2":
                    if a[3]:
                        v.wait_ge(unit_done, a[3])
                    split(cT_f, *C_T[a[2]])
                elif kind == "second":
                    split_tile(a[0], R_hi, R_lo)
                elif kind == "index":
                    h = a[0]
                    v.wait_ge(ix_relu, h + 1)
                    if h == 0:
                        for t in range(TT):
                            link(v.tensor_scalar(iw[:, t, :], A[:, AB_TOK + 256 * t + 192:][:, 0:IDX_HEADS],
                                                 IDX_HEADS ** -0.5 * HD ** -0.5, None, ALU.mult))
                    for t in range(TT):
                        c = slice(128 * t, 128 + 256 * t)
                        r = A[:, AB_IX + 384 * (h % 2):][:, 0:384][:, c]
                        if h == 0:
                            ins = v.tensor_scalar(score[:, c], r, iw[:, t, h:h + 1], None, ALU.mult)
                        else:
                            ins = v.scalar_tensor_tensor(out=score[:, c], in0=r, scalar=iw[:, t, h:h + 1],
                                                         in1=score[:, c], op0=ALU.mult, op1=ALU.add)
                        if t == 0:
                            mark(ins)
                    ins.then_inc(ix_used, 1)
                    v.wait_ge(ix_used, h + 1)
                    if h == IDX_HEADS - 1:
                        for t in range(TT):
                            c = slice(256 * t, 256 * t + P)
                            link(v.tensor_tensor(score[:, c], score[:, c], causal_b[:, :], ALU.add))
                elif kind == "topk":
                    c = [slice(128 * t, 128 + 256 * t) for t in range(TT)]
                    for t in range(TT):
                        (link if t else mark)(v.max(m8[:, t, :], score[:, c[t]]))
                    for t in range(TT):
                        (link if t else mark)(v.match_replace(score[:, c[t]], m8[:, t, :], score[:, c[t]], TAKEN))
                elif kind == "chosen":
                    link(v.tensor_scalar(chosen_b[:, :], score, TAKEN / 2, NEG, ALU.is_gt, ALU.mult))
                    for t in range(TT):
                        c = slice(256 * t, 256 * t + P)
                        ins = v.tensor_tensor(chosen_b[:, c], chosen_b[:, c], causal_b[:, :], ALU.min)
                        if t == 0:
                            link(ins)
                    ins.then_inc(chosen, 1)
                elif kind == "head":
                    k, first, last = a
                    if k < last:
                        v.wait_ge(s_done, k + 1)
                        h, bank = head(k), B[4 + k % 2]
                        v.reduce_max(mx[:, k % 4, 0:1], bank[:, 0:128], AX.X)
                        link(v.reduce_max(mx[:, k % 4, 1:2], bank[:, 128:384], AX.X))
                        if h["sink"] is not None:
                            link(v.tensor_scalar(mx[:, k % 4, :], mx[:, k % 4, :], h["scale"], None, ALU.mult))
                            link(v.tensor_scalar(mx[:, k % 4, :], mx[:, k % 4, :], sink_r[:, k:k + 1], None, ALU.max))
                            v.tensor_scalar(nb[:, k % 4, :], mx[:, k % 4, :], -1.0, None,
                                            ALU.mult).then_inc(max_done, 1)
                        else:
                            v.tensor_scalar(nb[:, k % 4, :], mx[:, k % 4, :], -h["scale"], None,
                                            ALU.mult).then_inc(max_done, 1)
                    if first <= k - 3 < last:
                        j = k - 3
                        h, q = head(j), j % 4
                        v.wait_ge(pv_done, j + 1)
                        if h["sink"] is not None:
                            link(v.tensor_tensor(sm[:, q, :], sm[:, q, :], sk[:, q, :], ALU.add))
                        link(v.reciprocal(ri[:, q, :], sm[:, q, :]))
                        dv, oc = h["dv"], h["oc"]
                        v.tensor_scalar(h["o"][:, oc:oc + dv], B[7][:, 0:dv], ri[:, q, 0:1], None, ALU.mult)
                        v.tensor_scalar(h["o"][:, P + oc:P + oc + dv], B[7][:, dv:2 * dv], ri[:, q, 1:2], None,
                                        ALU.mult).then_inc(o_done, 1)
                elif kind == "turn":
                    name, j = a
                    at, c = STAGE[name][j % 2], slice(2 * j, 2 * j + 2)
                    split(two(A[:, at:at + 512]), *(t_[:, c, :] for t_ in TURN_TO[name]))
                elif kind == "bound":
                    b, what, last_unit, _, second, lead = a
                    if b == 0:
                        v.wait_ge(ld_x, 16)

                    def residual(t, halves=(0, 1)):
                        for h in halves:
                            if (t, h) == (1, 1):
                                v.wait_ge(unit_done, last_unit + 1)
                            else:
                                v.wait_ge(y_done, 3 * b + 2 * t + h + 1)
                            y, c = B[4 + 2 * t + h], slice(512 * h, 512 * h + 512)
                            if b < 4:
                                ins = v.tensor_tensor(N[:, t, c], y[:, :], gate_r[:, c], ALU.mult)
                            else:
                                ins = v.tensor_tensor(X[:, t, c], y[:, :], X[:, t, c], ALU.add)
                            ins.then_inc(y_read, 1)
                            n["y"] += 1
                            v.wait_ge(y_read, n["y"])
                            if b < 4:
                                link(v.scalar_tensor_tensor(out=X[:, t, c], in0=X[:, t, c], scalar=ALPHA, in1=N[:, t, c],
                                                            op0=ALU.mult, op1=ALU.add))
                            if b < 4 or t == 1:
                                (link if h else mark)(v.bn_stats(bn[:, t, h, :], X[:, t, c]))

                    def half(rms):
                        v.wait_ge(rstd_ready, n["root"])
                        ins = (v.tensor_scalar(N[:, 1, 0:512], X[:, 1, 0:512], rstd[:, 1:2], None, ALU.mult) if rms else
                               v.tensor_scalar(N[:, 1, 0:512], X[:, 1, 0:512], mv[:, 1, 0:1], rstd[:, 1:2],
                                               ALU.subtract, ALU.mult))
                        n["half"] += 1
                        ins.then_inc(half_ready, 1)

                    def stage():
                        n["pair"] += 1
                        v.wait_ge(pair_turned, n["pair"] - 4)
                        for k in range(4):
                            ins = v.tensor_scalar(hTf[:, k, P:2 * P], B[2][:, P * k:P * k + P], a[3][0][:, k:k + 1],
                                                  a[3][1][:, k:k + 1], ALU.mult, ALU.add)
                        ins.then_inc(staged, 1)
                        n["staged"] += 1
                        v.wait_ge(staged, n["staged"])
                        c, q = slice(0, 4), slice(P, 2 * P)
                        link(v.tensor_copy(hT_hi[:, c, q], hTf[:, c, q]))
                        v.tensor_tensor(hT_lo[:, c, q], hTf[:, c, q], hT_hi[:, c, q], ALU.subtract).then_inc(pair_ready, 1)
                        c = slice(4, 8)
                        split(hTf[:, c, q], hT_hi[:, c, q], hT_lo[:, c, q])

                    def affine(t):
                        if t == 0:
                            n["row"] += 1
                            v.wait_ge(ld_row, 32 * n["row"])
                        link(v.tensor_tensor(X[:, t, :], N[:, t, :], rows[:, 0, :], ALU.mult))
                        v.tensor_tensor(X[:, t, :], X[:, t, :], rows[:, 1, :], ALU.add).then_inc(x_ready, 1)
                        n["x"] += 1
                        v.wait_ge(x_ready, n["x"])

                    def normalised():
                        n["n"] += 1
                        v.wait_ge(n_ready, n["n"])

                    def square_root(t):
                        n["sq"] += 1
                        v.wait_ge(sq_done, n["sq"])
                        link(v.tensor_tensor(ve[:, t:t + 1], ss[:, t, 0:1], ss[:, t, 1:2], ALU.add))
                        link(v.tensor_scalar(ve[:, t:t + 1], ve[:, t:t + 1], 1.0 / D, RMS_EPS, ALU.mult, ALU.add))
                        inverse_root(t, 1).then_inc(rstd_ready, 1)
                        n["root"] += 1

                    if what == "lnrms":
                        residual(0)
                        row_root(0, False)
                        residual(1, (0,))
                        normalised()
                        affine(0)
                        residual(1, (1,))
                        row_root(1, False)
                        half(False)
                        square_root(0)
                        v.wait_ge(half_ready, n["half"])
                        normalised()
                        affine(1)
                        split_tile(0, hT_hi, hT_lo)
                        square_root(1)
                        half(True)
                        stage()
                    for t in range(TT if what != "lnrms" else 0):
                        residual(t)
                        if t == 1 and lead:
                            split_tile(0, hT_hi, hT_lo)
                        if b < 4 or t == 1:
                            row_root(t, b >= 4)
                        else:
                            square_root(t)
                        if t == 1:
                            half(b >= 4)
                        if t == 0 and b < 3:
                            finish(b + 1)
                        if t == 1 and what in ("ln", "rms") and not lead:
                            split_tile(0, hT_hi, hT_lo)
                    if what == "final":
                        v.wait_ge(half_ready, n["half"])
                        v.wait_ge(ld_fn, 16)
                        for t in range(TT):
                            normalised()
                            v.tensor_tensor(N[:, t, :], N[:, t, :], rows[:, 0, :], ALU.mult).then_inc(out_ready, 1)
                    elif what != "lnrms":
                        stage()
                    if what == "ln":
                        v.wait_ge(half_ready, n["half"])
                        for t in range(TT):
                            normalised()
                            affine(t)
                    elif what != "final":
                        n["n"] += TT
                elif kind == "mlp":
                    mlp(a[0], a[1], a[2])
                elif kind == "hg_start":
                    v.wait_ge(ld_level, 16)
                    link(v.tensor_copy(level_m[:, :, :], arena(H_E, LEVELS, P)))
                    l0, l1 = vec[:, COL["lb"]:COL["lb"] + KT], vec[:, COL["lb"] + KT:COL["lb"] + 2 * KT]
                    link(v.tensor_tensor(tmp_c[:, 2, :], l0, l1, ALU.max))
                    link(v.tensor_tensor(tmp_c[:, 0, :], l0, tmp_c[:, 2, :], ALU.subtract))
                    v.tensor_tensor(tmp_c[:, 1, :], l1, tmp_c[:, 2, :], ALU.subtract).then_inc(lb_in, 1)
                    v.wait_ge(lb_exp, 1)
                    link(v.tensor_tensor(tmp_c[:, 0, :], tmp_c[:, 2, :], tmp_c[:, 3, :], ALU.add))
                    link(v.reciprocal(tmp_c[:, 1, :], tmp_c[:, 0, :]))
                    link(v.tensor_tensor(lb_c[:, 0, :], tmp_c[:, 2, :], tmp_c[:, 1, :], ALU.mult))
                    link(v.tensor_scalar(lb_c[:, 1, :], lb_c[:, 0, :], -1.0, 1.0, ALU.mult, ALU.add))
                elif kind == "level":
                    l = a[0]
                    if l == 0:
                        link(v.memset(A[:, H_ST:H_ST + 2048], 0.0))
                    if l == LEVELS:
                        continue
                    W = 4 * SEQ
                    for g in range(2):
                        v.wait_ge(lv_ps, 2 * l + g + 1)
                        if l:
                            v.wait_ge(lv_used, 2 * (l - 1) + g + 1)
                        for i in range(2):
                            st = A[:, H_ST + 1024 * g + 512 * i:][:, 0:512].rearrange("p (a b) -> p a b", b=P)
                            ps = B[4 + 2 * g + i][:, :].rearrange("p (a b) -> p a b", b=P)
                            mark(v.copy_predicated(st, level_m[:, l, :].unsqueeze(1).to_broadcast([P, 4, P]), ps))
                        q, k = A[:, H_Q + W * g:][:, 0:W], A[:, H_K + W * g:][:, 0:W]
                        if l == 0:
                            v.tensor_tensor(q, q, A[:, H_F + W * g:][:, 0:W], ALU.mult).then_inc(lv_used, 1)
                            continue
                        w = 1 << (l - 1)
                        nbk = W // (2 * w)
                        ends = (A[:, H_F + W * g:][:, 0:W] if l == 1 else
                                A[:, H_TMP + (W if l % 2 else 0) + W // 2 * g:][:, 0:W // w])
                        e2 = ends.rearrange("p (n s) -> p n s", s=2)
                        q2 = q.rearrange("p (n s w) -> p n s w", s=2, w=w)
                        k2 = k.rearrange("p (n s w) -> p n s w", s=2, w=w)
                        eb = [e2[:, :, s:s + 1].to_broadcast([P, nbk, w]) for s in range(2)]
                        mark(v.tensor_tensor(q2[:, :, 1, :], q2[:, :, 1, :], eb[0], ALU.mult))
                        nxt = A[:, H_TMP + (0 if l % 2 else W) + W // 2 * g:][:, 0:nbk]
                        mark(v.tensor_tensor(nxt, e2[:, :, 0], e2[:, :, 1], ALU.mult))
                        v.tensor_tensor(k2[:, :, 0, :], k2[:, :, 0, :], eb[1], ALU.mult).then_inc(lv_used, 1)
                elif kind == "turn_tile":
                    split_tile(a[0], hT_hi, hT_lo)
                elif kind == "hg_out":
                    t = a[0]
                    o = A[:, H_F:H_F + 2048].rearrange("p (h t v) -> p h t v", h=HG_HEADS, t=TT)[:, :, t, :]
                    gate = arena(H_G, TT, D)[:, t, :].rearrange("p (h v) -> p h v", h=HG_HEADS)
                    sq = A[:, H_TMP:H_TMP + 1024].rearrange("p (h v) -> p h v", h=HG_HEADS)
                    ps = [B[4 + 2 * t + i][:, :].rearrange("p (h v) -> p h v", h=4) for i in range(2)]
                    v.wait_ge(ho_sq, t + 1)
                    c = slice(8 * t, 8 * t + 8)
                    link(v.reduce_sum(ve[:, c], sq, AX.X))
                    link(v.tensor_scalar(ve[:, c], ve[:, c], 1.0 / P, RMS_EPS, ALU.mult, ALU.add))
                    link(inverse_root(8 * t, 8))
                    for i in range(2):
                        rb = rstd[:, 8 * t + 4 * i:8 * t + 4 * i + 4].unsqueeze(2).to_broadcast([P, 4, P])
                        ins = v.tensor_tensor(o[:, 4 * i:4 * i + 4, :], ps[i], rb, ALU.mult)
                    ins.then_inc(ho_read, 1)
                    v.wait_ge(ho_read, t + 1)
                    v.tensor_tensor(o, o, gate, ALU.mult).then_inc(o_ready, 1)


def kernel(**inputs):
    import numpy as np
    import concourse.bacc as bacc
    from concourse.bass_utils import run_bass_kernel_spmd as run

    g = {k: np.asarray(a) for k, a in inputs.items()}

    def wide(w):
        return w.reshape(KT, P, -1, 256).transpose(2, 1, 0, 3).reshape(-1, P, UNIT)

    def tall(w):
        return w.reshape(-1, 2, P, D).transpose(0, 2, 1, 3).reshape(-1, P, UNIT)

    def rank(w):
        return w.reshape(2, P, -1, D).transpose(2, 1, 0, 3).reshape(-1, P, UNIT)

    def mlp(w1, w2):
        up, dn = wide(w1), tall(w2)
        order = [up[0]]
        for k in range(1, PAIRS):
            order += [up[k], dn[k - 1]]
        return np.stack(order + [dn[PAIRS - 1]])

    z = lambda k: np.zeros((D, k), np.float32)
    ab = g["ab_w_in"][0]
    aq, ak, av, cq, bk, bv, bik, biw = np.split(ab, np.cumsum([512, 128, 128, RANK, HD, HD, HD]), axis=1)
    kt = np.concatenate([ak[:, :64], ak[:, :64], ak[:, 64:], ak[:, 64:], bk, bk, bik, bik], axis=1)
    c_in = g["c_w_in"][0]
    cqkv = [wide(c_in[:, D * i:D * (i + 1)]) for i in range(3)]
    dkv = g["kv_w_dkv_2"]
    uq = g["mla_w_uq_2"][0].reshape(RANK, MLA_HEADS, NOPE + ROPE)
    hg_i = wide(g["hgrn_w_i_2"][0])
    uk, uv, uqn = rank(g["kv_w_uk_2"]), rank(g["kv_w_uv_2"]), rank(uq[:, :, :NOPE].reshape(RANK, -1))
    stream = np.concatenate([
        wide(cq), wide(np.concatenate([av, bv, biw, z(56)], axis=1)), wide(kt),
        rank(np.concatenate([g["ab_w_uiq"][0], g["ab_w_uq"][0]], axis=1)), wide(aq), tall(g["ab_w_out"][0]),
        mlp(g["mlp_w1"][0], g["mlp_w2"][0]),
        cqkv[2], np.stack([cqkv[i][j] for j in range(4) for i in range(2)]), tall(g["c_w_out"][0]),
        mlp(g["mlp_w1"][1], g["mlp_w2"][1]),
        hg_i[:2], wide(g["hgrn_w_q_2"][0]), wide(g["hgrn_w_f_2"][0]), hg_i[2:], wide(g["hgrn_w_g_2"][0]),
        tall(g["hgrn_w_o_2"][0]),
        mlp(g["mlp_w_up_2"][0], g["mlp_w_down_2"][0]),
        wide(dkv[:, :RANK]), wide(np.concatenate([dkv[:, RANK:], dkv[:, RANK:], z(P)], axis=1)),
        wide(g["mla_w_dq_2"][0]), uk[:1], rank(uq[:, :, NOPE:].reshape(RANK, -1)), uv[:1], uqn[:1], uk[1:], uv[1:], uqn[1:],
        tall(g["mla_w_o_2"][0]),
        mlp(g["mlp_w_up_2"][1], g["mlp_w_down_2"][1]),
    ])
    assert stream.shape == (UNITS, P, UNIT)

    def columns(a):
        return np.asarray(a).reshape(-1, P).T

    cols = np.concatenate([columns(g[k]) for k in (
        "c", "ln_g", "ln_b", "ab_q_norm", "hgrn_norm_2", "mla_norm_2", "mla_q_norm_2", "kv_in_norm_2", "kv_norm_2",
        "mlp_norm_2", "hgrn_lb_logits_2")], axis=1)

    i, j = np.arange(P)[:, None], np.arange(P)[None, :]
    consts = [i == j, (i // 64 == j // 64) & ((i % 64 + 32) % 64 == j % 64)]
    consts = [m.astype(np.float32) for m in consts]
    consts += [np.where(j <= i, 0.0, NEG).astype(np.float32), np.where(j > i, 0.0, NEG).astype(np.float32)]
    consts.append((i == j).astype(np.float32))
    for l in range(1, LEVELS):
        w = 1 << (l - 1)
        consts.append(((i // (2 * w) == j // (2 * w)) & (i // w % 2 == 0) & (j // w % 2 == 1)).astype(np.float32))
    consts = np.stack(consts, axis=1).reshape(P, N_CONST * P)
    inv = (np.float32(10000.0) ** (-np.arange(0, HD, 2, dtype=np.float32) / np.float32(HD))).astype(np.float32)
    inv_col, sign = inv[np.arange(P) % 32], np.where(np.arange(P) % 64 < 32, -1.0, 1.0).astype(np.float32)
    angle = np.arange(SEQ, dtype=np.float32)[None, :] * inv_col[:, None]
    arrays = {
        "stream": stream,
        "ada_w": g["ada_w"].reshape(4, KT, P, 3 * D),
        "ada_b": g["ada_b"].reshape(4, 3 * D),
        "x": g["x"][0],
        "x_t": g["x"][0].T,
        "pos": g["positions"].reshape(SEQ),
        "cols": cols,
        "ln_g": g["ln_g"],
        "ln_b": g["ln_b"],
        "sinks": g["ab_sinks"][0],
        "g_norm": g["hgrn_g_norm_2"][0],
        "final_norm": g["final_norm_2"],
        "consts": consts,
        "rope_cols": np.stack([inv_col, sign], axis=1),
        "rope_2": np.stack([np.cos(angle), np.sin(angle) * sign[:, None]], axis=1).astype(np.float32),
    }
    nc = bacc.Bacc("TRN2", target_bir_lowering=False, num_devices=1)
    args = []
    for name in arrays:
        arrays[name] = np.ascontiguousarray(arrays[name])
        args.append(nc.dram_tensor(name, arrays[name].shape, mybir.dt.from_np(arrays[name].dtype),
                                   kind="ExternalInput").ap())
    args.append(nc.dram_tensor("out", (SEQ, D), mybir.dt.float32, kind="ExternalOutput").ap())
    two_block_kernel(nc, *args)
    r = run(nc, [arrays], core_ids=[0])
    return r.results[0]["out"].reshape(1, SEQ, D)
```
